# Optimizing a Trainium2 kernel written in Bass

```python
import jax, jax.numpy as jnp
from jax import lax
import numpy as np

D_MODEL = 2048
BATCH = 1
SEQ = 256
DEPTH = 1
DEC_BATCH = 8
DEC_SEQ = 4
PAST_LEN = 2048
PAGE_SIZE = 128

LRU_WIDTH = D_MODEL // 2
POOL_WIDTH = D_MODEL - LRU_WIDTH
MIX_WIDTH = LRU_WIDTH + POOL_WIDTH
LRU_HEADS = 8
LRU_HEAD_DIM = LRU_WIDTH // LRU_HEADS
CONV_WIDTH = 4
LRU_C = 8.0
POOL_WINDOWS = (2, 4, 8, 16)
POOL_GROUPS = len(POOL_WINDOWS)
POOL_GROUP_DIM = POOL_WIDTH // POOL_GROUPS
POOL_HIST = max(POOL_WINDOWS) - 1
PEER_HEADS = 8
PEER_NKEYS = 128
PEER_EXPERTS = PEER_NKEYS * PEER_NKEYS
PEER_TOPK = 16
PEER_DKEY = 256
PEER_DHALF = PEER_DKEY // 2
PEER_BLOCK = 128
N_MOD = 6
EPS = 1e-6

kernel_name = 'hymba_rglru_pool_peer_adaln_step'

def rmsnorm(x, g):
    xf = x.astype(jnp.float32)
    y = xf * lax.rsqrt(jnp.mean(xf * xf, axis=-1, keepdims=True) + EPS)
    return (y * g.astype(jnp.float32)).astype(x.dtype)

def modulate(h, shift, scale):
    return h * (1 + scale[:, None]) + shift[:, None]

def causal_conv(xcat, w, b, T):
    out = xcat[:, CONV_WIDTH - 1:CONV_WIDTH - 1 + T] * w[CONV_WIDTH - 1] + b
    for k in range(CONV_WIDTH - 1):
        out = out + xcat[:, k:k + T] * w[k]
    return out

def rg_lru(xc, h_prev, wa, ba, wx, bx, lam, pos):
    B, T, C = xc.shape
    xf = xc.astype(jnp.float32)
    xh = xf.reshape(B, T, LRU_HEADS, LRU_HEAD_DIM)
    r = jax.nn.sigmoid(jnp.einsum('bthi,hij->bthj', xh, wa.astype(jnp.float32)) + ba.astype(jnp.float32)).reshape(B, T, C)
    i = jax.nn.sigmoid(jnp.einsum('bthi,hij->bthj', xh, wx.astype(jnp.float32)) + bx.astype(jnp.float32)).reshape(B, T, C)
    log_a = -LRU_C * r * jax.nn.softplus(-lam.astype(jnp.float32))
    a = jnp.exp(log_a)
    mult = jnp.sqrt(-jnp.expm1(2.0 * log_a))
    mult = jnp.where((pos == 0)[None, :, None], 1.0, mult)
    nx = xf * i * mult

    def step(h, inp):
        a_t, x_t = inp
        h = a_t * h + x_t
        return h, h

    h_last, hs = lax.scan(step, h_prev.astype(jnp.float32), (a.transpose(1, 0, 2), nx.transpose(1, 0, 2)))
    return hs.transpose(1, 0, 2), h_last

def pool_mix(pcat, pos, w, b, scale):
    B, L, C = pcat.shape
    T = L - POOL_HIST
    cs = jnp.cumsum(pcat.astype(jnp.float32), axis=1)
    cs = jnp.concatenate([jnp.zeros_like(cs[:, :1]), cs], axis=1)
    hi = np.arange(T) + POOL_HIST + 1
    outs = []
    for g, win in enumerate(POOL_WINDOWS):
        sl = slice(g * POOL_GROUP_DIM, (g + 1) * POOL_GROUP_DIM)
        s = cs[:, hi, sl] - cs[:, hi - win, sl]
        cnt = jnp.minimum(pos + 1, win).astype(jnp.float32)
        outs.append(s / cnt[None, :, None])
    pooled = jnp.concatenate(outs, axis=-1)
    d = (pooled - pcat[:, POOL_HIST:].astype(jnp.float32)).reshape(B, T, POOL_GROUPS, POOL_GROUP_DIM)
    y = jnp.einsum('btgi,gij->btgj', d, w.astype(jnp.float32)) + b.astype(jnp.float32)
    return (y.reshape(B, T, C) * scale.astype(jnp.float32)).astype(pcat.dtype)

def peer(h, wq, keys, eu, ev):
    T, D = h.shape
    Tp = -(-T // PEER_BLOCK) * PEER_BLOCK
    hp = jnp.pad(h, ((0, Tp - T), (0, 0)))
    q = (hp @ wq).astype(jnp.float32).reshape(Tp, PEER_HEADS, 2, PEER_DHALF)
    s = jnp.einsum('thpd,hpnd->thpn', q, keys.astype(jnp.float32))
    s1, i1 = lax.top_k(s[:, :, 0], PEER_TOPK)
    s2, i2 = lax.top_k(s[:, :, 1], PEER_TOPK)
    cand = (s1[..., :, None] + s2[..., None, :]).reshape(Tp, PEER_HEADS, PEER_TOPK * PEER_TOPK)
    cidx = (i1[..., :, None] * PEER_NKEYS + i2[..., None, :]).reshape(Tp, PEER_HEADS, PEER_TOPK * PEER_TOPK)
    top, sel = lax.top_k(cand, PEER_TOPK)
    eidx = jnp.take_along_axis(cidx, sel, axis=-1)
    gates = jax.nn.softmax(top, axis=-1)
    nb = Tp // PEER_BLOCK
    hb = hp.reshape(nb, PEER_BLOCK, D)
    eb = eidx.reshape(nb, PEER_BLOCK, PEER_HEADS * PEER_TOPK)
    gb = gates.reshape(nb, PEER_BLOCK, PEER_HEADS * PEER_TOPK).astype(h.dtype)

    def block(args):
        xb, ib, wb = args
        act = jax.nn.gelu(jnp.einsum('td,ted->te', xb, eu[ib]))
        return jnp.einsum('te,ted->td', wb * act, ev[ib])

    out = lax.map(block, (hb, eb, gb)).reshape(Tp, D)
    return out[:T]

def decoder_layer(x, c, conv_hist, h_prev, pool_hist, start_pos,
                  w_ada, b_ada, norm1_g, w_in, conv_w, conv_b, lru_wa, lru_ba, lru_wx, lru_bx,
                  lru_lambda, pool_w, pool_b, pool_scale, gnorm_lru_g, gnorm_pool_g, w_out,
                  norm2_g, peer_wq, peer_keys, peer_u, peer_v):
    B, T, D = x.shape
    pos = start_pos + jnp.arange(T, dtype=jnp.int32)
    mod = jax.nn.silu(c) @ w_ada + b_ada
    sh1, sc1, g1, sh2, sc2, g2 = jnp.split(mod, N_MOD, axis=-1)
    h = modulate(rmsnorm(x, norm1_g), sh1, sc1)
    z = h @ w_in
    u_lru = z[..., :LRU_WIDTH]
    u_gate = z[..., LRU_WIDTH:2 * LRU_WIDTH]
    u_pool = z[..., 2 * LRU_WIDTH:]
    conv_cat = jnp.concatenate([conv_hist.astype(x.dtype), u_lru], axis=1)
    xc = causal_conv(conv_cat, conv_w, conv_b, T)
    hs, h_last = rg_lru(xc, h_prev, lru_wa, lru_ba, lru_wx, lru_bx, lru_lambda, pos)
    y_lru = (hs * jax.nn.gelu(u_gate.astype(jnp.float32))).astype(x.dtype)
    pool_cat = jnp.concatenate([pool_hist.astype(x.dtype), u_pool], axis=1)
    y_pool = pool_mix(pool_cat, pos, pool_w, pool_b, pool_scale)
    mixed = jnp.concatenate([rmsnorm(y_lru, gnorm_lru_g), rmsnorm(y_pool, gnorm_pool_g)], axis=-1)
    x = x + g1[:, None] * (mixed @ w_out)
    h2 = modulate(rmsnorm(x, norm2_g), sh2, sc2)
    x = x + g2[:, None] * peer(h2.reshape(B * T, D), peer_wq, peer_keys, peer_u, peer_v).reshape(B, T, D)
    return (x, conv_cat[:, -(CONV_WIDTH - 1):], h_last.astype(h_prev.dtype), pool_cat[:, -POOL_HIST:])

def setup_inputs(seed: int = 0) -> dict:
    key = jax.random.key(seed)
    ks = jax.random.split(key, 32)

    def nrm(k, shape, scale):
        return jax.random.normal(k, shape, jnp.float32) * scale

    u = jax.random.uniform(ks[14], (DEPTH, LRU_WIDTH), jnp.float32, minval=0.9, maxval=0.999)
    a0 = u ** (1.0 / LRU_C)
    lru_lambda = jnp.log(a0) - jnp.log1p(-a0)
    return {
        'x_prompt': nrm(ks[0], (BATCH, SEQ, D_MODEL), 1.0),
        'x_sample': nrm(ks[1], (DEC_BATCH, DEC_SEQ, D_MODEL), 1.0),
        'c_prompt': nrm(ks[2], (BATCH, D_MODEL), 1.0),
        'c_sample': nrm(ks[3], (DEC_BATCH, D_MODEL), 1.0),
        'state_conv': nrm(ks[4], (DEPTH, DEC_BATCH, CONV_WIDTH - 1, LRU_WIDTH), 1.0),
        'state_lru': nrm(ks[5], (DEPTH, DEC_BATCH, LRU_WIDTH), 0.5),
        'state_pool': nrm(ks[6], (DEPTH, DEC_BATCH, POOL_HIST, POOL_WIDTH), 1.0),
        'w_ada': nrm(ks[7], (DEPTH, D_MODEL, N_MOD * D_MODEL), 0.5 * D_MODEL ** -0.5),
        'b_ada': nrm(ks[8], (DEPTH, N_MOD * D_MODEL), 0.02),
        'norm1_g': 1.0 + nrm(ks[9], (DEPTH, D_MODEL), 0.02),
        'w_in': nrm(ks[10], (DEPTH, D_MODEL, 2 * LRU_WIDTH + POOL_WIDTH), D_MODEL ** -0.5),
        'conv_w': nrm(ks[11], (DEPTH, CONV_WIDTH, LRU_WIDTH), CONV_WIDTH ** -0.5),
        'conv_b': nrm(ks[12], (DEPTH, LRU_WIDTH), 0.02),
        'lru_wa': nrm(ks[13], (DEPTH, LRU_HEADS, LRU_HEAD_DIM, LRU_HEAD_DIM), LRU_HEAD_DIM ** -0.5),
        'lru_ba': nrm(ks[15], (DEPTH, LRU_HEADS, LRU_HEAD_DIM), 0.02),
        'lru_wx': nrm(ks[16], (DEPTH, LRU_HEADS, LRU_HEAD_DIM, LRU_HEAD_DIM), LRU_HEAD_DIM ** -0.5),
        'lru_bx': nrm(ks[17], (DEPTH, LRU_HEADS, LRU_HEAD_DIM), 0.02),
        'lru_lambda': lru_lambda,
        'pool_w': nrm(ks[18], (DEPTH, POOL_GROUPS, POOL_GROUP_DIM, POOL_GROUP_DIM), POOL_GROUP_DIM ** -0.5),
        'pool_b': nrm(ks[19], (DEPTH, POOL_GROUPS, POOL_GROUP_DIM), 0.02),
        'pool_scale': 1.0 + nrm(ks[20], (DEPTH, POOL_WIDTH), 0.1),
        'gnorm_lru_g': 1.0 + nrm(ks[21], (DEPTH, LRU_WIDTH), 0.02),
        'gnorm_pool_g': 1.0 + nrm(ks[22], (DEPTH, POOL_WIDTH), 0.02),
        'w_out': nrm(ks[23], (DEPTH, MIX_WIDTH, D_MODEL), MIX_WIDTH ** -0.5),
        'norm2_g': 1.0 + nrm(ks[24], (DEPTH, D_MODEL), 0.02),
        'peer_wq': nrm(ks[25], (DEPTH, D_MODEL, PEER_HEADS * PEER_DKEY), D_MODEL ** -0.5),
        'peer_keys': nrm(ks[26], (DEPTH, PEER_HEADS, 2, PEER_NKEYS, PEER_DHALF), PEER_DHALF ** -0.5),
        'peer_u': nrm(ks[27], (DEPTH, PEER_EXPERTS, D_MODEL), D_MODEL ** -0.5),
        'peer_v': nrm(ks[28], (DEPTH, PEER_EXPERTS, D_MODEL), PEER_HEADS ** -0.5),
        'final_g': 1.0 + nrm(ks[29], (D_MODEL,), 0.02),
    }

def reference(x_prompt, x_sample, c_prompt, c_sample, state_conv, state_lru, state_pool,
              w_ada, b_ada, norm1_g, w_in, conv_w, conv_b, lru_wa, lru_ba, lru_wx, lru_bx,
              lru_lambda, pool_w, pool_b, pool_scale, gnorm_lru_g, gnorm_pool_g, w_out,
              norm2_g, peer_wq, peer_keys, peer_u, peer_v, final_g):
    dt = x_prompt.dtype
    bp = x_prompt.shape[0]
    xp, xs = x_prompt, x_sample
    conv_p, lru_p, pool_p, conv_s, lru_s, pool_s = [], [], [], [], [], []
    for l in range(DEPTH):
        params = (w_ada[l], b_ada[l], norm1_g[l], w_in[l], conv_w[l], conv_b[l], lru_wa[l], lru_ba[l],
                  lru_wx[l], lru_bx[l], lru_lambda[l], pool_w[l], pool_b[l], pool_scale[l],
                  gnorm_lru_g[l], gnorm_pool_g[l], w_out[l], norm2_g[l], peer_wq[l], peer_keys[l],
                  peer_u[l], peer_v[l])
        xp, cp, hp, pp = decoder_layer(
            xp, c_prompt,
            jnp.zeros((bp, CONV_WIDTH - 1, LRU_WIDTH), dt),
            jnp.zeros((bp, LRU_WIDTH), dt),
            jnp.zeros((bp, POOL_HIST, POOL_WIDTH), dt),
            0, *params)
        xs, cs, hs, ps = decoder_layer(xs, c_sample, state_conv[l], state_lru[l], state_pool[l], PAST_LEN, *params)
        conv_p.append(cp); lru_p.append(hp); pool_p.append(pp)
        conv_s.append(cs); lru_s.append(hs); pool_s.append(ps)
    y_prompt = rmsnorm(xp, final_g)
    y_sample = rmsnorm(xs, final_g)
    return (y_prompt, y_sample, jnp.stack(conv_p), jnp.stack(lru_p), jnp.stack(pool_p),
            jnp.stack(conv_s), jnp.stack(lru_s), jnp.stack(pool_s))


_drawn_inputs = setup_inputs


def setup_inputs(seed=0):
    import zlib

    import numpy as np

    out = dict(_drawn_inputs(seed))
    spreads = {}
    factors = {'norm1_g': 2.855,
     'lru_ba': 8.0,
     'lru_bx': 7.494,
     'pool_b': 3.699,
     'gnorm_lru_g': 8.0,
     'gnorm_pool_g': 8.0,
     'norm2_g': 6.761,
     'final_g': 2.839}
    for name, (base, spread) in spreads.items():
        noise = np.random.default_rng([zlib.crc32(name.encode()), seed]).standard_normal(out[name].shape)
        drawn = base * np.exp(spread * noise) if base else spread * noise
        out[name] = __import__('jax').numpy.asarray(drawn.astype(out[name].dtype))
    for name, factor in factors.items():
        out[name] = (out[name] * factor).astype(out[name].dtype)
    return out
```

```python
import numpy as np
import concourse.bass as bass
from concourse import mybir
from contextlib import ExitStack, contextmanager

F = mybir.dt.float32
FR = mybir.dt.float32r
I32 = mybir.dt.int32
U32 = mybir.dt.uint32
ALU = mybir.AluOpType
ACT = mybir.ActivationFunctionType
AX = mybir.AxisListType

P = 128
D = 2048
DC = D // P
SEQ = 256
NB, NS = 8, 4
T = SEQ + NB * NS
NC = 1 + NB
LC = 8
CW = 4
HIST = 15
WINDOWS = (2, 4, 8, 16)
HEADS, TOPK = 8, 16
EPS = 1e-6
CS = CW - 1 + NS
CAT = CW - 1 + SEQ
CL = CAT + NB * CS
XL = CL - (CW - 1)
PS = HIST + NS
PAT = HIST + SEQ
PL = PAT + NB * PS
PAIRS = [(a, TOPK // (a + 1)) for a in range(8)]
NCAND = sum(n for _, n in PAIRS) + 8
TT = 3
TP = TT * P

RAW, SPL = 4, 2
ADA0, NADA = 0, 6 * DC
Z0, NZ = ADA0 + NADA, 24
O0, NO = Z0 + NZ, DC
Q0, NQ = O0 + NO, DC
M0 = Q0 + NQ
EG = 8
NG = P // EG
NU = M0 + 2 * P
TCH = 16
NCH = T // TCH


def u_unit(g):
    return M0 if g == 0 else M0 + EG + 2 * EG * (g - 1)


def v_unit(g):
    return M0 + 2 * EG + 2 * EG * g if g < NG - 1 else NU - EG


VCOLS = [("b_ada", 96), ("norm1", DC), ("norm2", DC), ("final", DC), ("gn_lru", LC), ("gn_pool", LC),
         ("conv_w", CW * LC), ("conv_b", LC), ("ba", LC), ("bx", LC), ("lam", LC), ("pool_b", LC),
         ("pool_s", LC), ("cinv", 4 * HIST), ("h0", LC * NB)]
VOFF, _o = {}, 0
for _n, _w in VCOLS:
    VOFF[_n] = (_o, _w)
    _o += _w
NV = _o
NHIST = LC * NB * (CW - 1) + LC * NB * HIST


class Chain:

    def __init__(self, eng, sem):
        self.eng, self.sem, self.n, self.base = eng, sem, 0, None

    def done(self, ins):
        ins.then_inc(self.sem, 1)
        self.n += 1

    def wait(self):
        self.eng.wait_ge(self.sem, self.n if self.base is None else self.base + (self.n - self.start))

    def link(self, ins):
        self.done(ins)
        self.wait()

    @contextmanager
    def loop(self, first, end, per):
        count = end - first
        with self.eng.Fori(first, end) as i:
            self.start = self.n
            self.base = i * per + (self.n - first * per)
            yield i
            assert self.n - self.start == per, (self.n - self.start, per)
        self.n = self.start + count * per
        self.base = None


def at_least(eng, sem, value):
    if not isinstance(value, int) or value > 0:
        eng.wait_ge(sem, value)


def rounds(eng, n, body):
    body(0)
    with eng.Fori(1, n) as i:
        body(i)


def hybrid_step(nc, w_stream, vecs_d, c_d, hist_d, x_d, lruw_d, poolw_d, keys_d,
                o_y, o_conv, o_lru, o_pool):
    ctx = ExitStack()
    with ctx:
        def sb(name, shape, dt=F, scope=None):
            return (scope or ctx).enter_context(nc.sbuf_tensor(name, shape, dt))

        def sem(name):
            return ctx.enter_context(nc.semaphore(name))

        raw = sb("raw", [P, RAW, 2048])
        w_hi = sb("w_hi", [P, SPL, 2048], FR)
        w_lo = sb("w_lo", [P, SPL, 2048], FR)
        act_hi = sb("act_hi", [P, DC, T], FR)
        act_lo = sb("act_lo", [P, DC, T], FR)
        x = sb("x", [P, DC, T])
        vecs = sb("vecs", [P, NV])
        mod = sb("mod", [P, 6, DC, NC])
        scale1 = sb("scale1", [P, DC, NC])
        scale2 = sb("scale2", [P, DC, NC])
        ones = sb("ones", [P, P])
        ident = sb("ident", [P, P])
        iota = sb("iota", [P, P])
        epsc = sb("epsc", [P, 1])
        rstd = sb("rstd", [P, 2, T])
        soft = sb("soft", [P, 6, LC])
        fix = sb("fix", [P, 2, HIST])

        with ExitStack() as ada:
            csplit = sb("csplit", [P, DC, P], FR, ada)
        early = ExitStack()
        MIXN = 18700
        mix = sb("mix", [P, MIXN], F, early)
        early.close()
        gates_in = sb("gates_in", [P, 2, NCH, EG, TCH])
        acc = sb("acc", [P, DC, T])
        gw_hi = sb("gw_hi", [P, 2, EG, T], FR)
        gw_lo = sb("gw_lo", [P, 2, EG, T], FR)
        gel = sb("gel", [P, 2, T])
        prod = sb("prod", [P, 2, T])
        gates_dram = nc.dram_tensor("gates_dense", (NCH, P, P, TCH), F, kind="Internal").ap()

        ps = ctx.enter_context(nc.psum_tensor("ps", [P, 4096], F))

        def bank(b, n=512, at=0):
            return ps[:, b * 512 + at:b * 512 + at + n]

        def vec(name):
            o, w = VOFF[name]
            return vecs[:, o:o + w]

        at = [0]

        def carve(n):
            at[0] += n
            assert at[0] <= MIXN
            return at[0] - n

        pcat_o, ucat_o, gate_o, xc_o = carve(LC * PL), carve(LC * CL), carve(LC * T), carve(2538)
        ra_o, ii_o, wts_o = carve(LC * CL), carve(LC * PL), carve(2048)

        def view(o, *dims):
            n = int(np.prod(dims))
            v = mix[:, o:o + n]
            if len(dims) == 2:
                return v.rearrange("p (a b) -> p a b", b=dims[1])
            if len(dims) == 3:
                return v.rearrange("p (a b c) -> p a b c", b=dims[1], c=dims[2])
            return v

        pcat, ucat = view(pcat_o, LC, PL), view(ucat_o, LC, CL)
        gate, hist = view(gate_o, LC, T), view(gate_o, NHIST)
        xc_f, sB = view(xc_o, LC, CL), view(xc_o, 6, PL)
        ra_f, dd = view(ra_o, LC, CL), view(ra_o, LC, T)
        ii_f, sA = view(ii_o, LC, CL), view(ii_o, LC, PL)
        xc, ra, ii = xc_f[:, :, 0:XL], ra_f[:, :, 0:XL], ii_f[:, :, 0:XL]
        poolw = view(wts_o, 4, 2, 2 * P)
        lruw = view(wts_o, 2, LC, P)
        tanhs = ucat[:, :, 0:XL]
        y_pool, y_lru = view(pcat_o, LC, T), view(ucat_o, LC, T)
        ysq = view(ra_o, 2 * LC, T)
        work1 = view(xc_o, DC, T)
        work2 = view(pcat_o, DC, T)
        modrow = view(ra_o, 2048)
        hist_conv = view(gate_o, LC, NB, CW - 1)
        hist_pool = view(gate_o + LC * NB * (CW - 1), LC, NB, HIST)
        at[0] = 0
        qT = view(carve(DC * TP), DC, TP)
        keysT = view(carve(2048), DC, P)
        sc = view(carve(2048), DC, P)
        sc2 = view(carve(2048), DC, P)
        eq = view(carve(2 * TOPK * NCAND), 2, TOPK, NCAND)
        topv = view(carve(2 * HEADS * TOPK), HEADS, 2, TOPK)
        topi = view(carve(2 * HEADS * TOPK), HEADS, 2, TOPK)
        topf = view(carve(2 * HEADS * TOPK), HEADS, 2, TOPK)
        cand = view(carve(HEADS * NCAND), HEADS, NCAND)
        cand2 = view(carve(HEADS * NCAND), HEADS, NCAND)
        cidx = view(carve(HEADS * NCAND), HEADS, NCAND)
        best = view(carve(P), HEADS, TOPK)
        bpos = view(carve(P), HEADS, TOPK)
        bposf = view(carve(P), HEADS, TOPK)
        eidx = view(carve(P), HEADS, TOPK)
        eint = view(carve(P), P)
        eint2 = view(carve(P), P)
        sel = view(carve(3 * P), 3, P)
        gsum = view(carve(HEADS), HEADS)
        idT = view(carve(3 * TP), 3, TP)
        idT_end = at[0]
        at[0] = 0
        stage = view(carve(2 * P * TCH), 2, P, TCH)
        one1 = view(carve(2 * 8 * P), 2, 8, P)
        one2 = view(carve(2 * 8 * P), 2, 8, P)
        assert at[0] <= idT_end - 3 * TP
        o_cv = sb("o_cv", [P, LC, NC, CW - 1])
        o_hl = sb("o_hl", [P, LC, NC])

        raw_in = [sem(f"raw_in{i}") for i in range(RAW)]
        hi_ready, lo_ready = sem("hi_ready"), sem("lo_ready")
        pe_unit = sem("pe_unit")
        in_vecs, in_c, in_hist, in_x, in_lruw, in_poolw, in_keys = (
            sem(n) for n in ("in_vecs", "in_c", "in_hist", "in_x", "in_lruw", "in_poolw", "in_keys"))
        consts = sem("consts")
        csil_ready, chi_ready, clo_ready = sem("csil_ready"), sem("chi_ready"), sem("clo_ready")
        sq_ready, stat_ready, std_ready, rstd_ready = sem("sq_ready"), sem("stat_ready"), sem("std_ready"), sem("rstd_ready")
        rowa_ready, rowb_ready = sem("rowa_ready"), sem("rowb_ready")
        modT_done, mod_ready = sem("modT_done"), sem("mod_ready")
        bank_free = [sem("bank0_free"), sem("bank1_free")]
        t_ready, ahi_ready, alo_ready = sem("t_ready"), sem("ahi_ready"), sem("alo_ready")
        hist_ready = sem("hist_ready")
        states_saved, pool_saved = sem("states_saved"), sem("pool_saved")
        d_ready, pool_mm, ypool_ready = sem("d_ready"), sem("pool_mm"), sem("ypool_ready")
        conv_ready, lru_mm, sig_ready, loga_ready = sem("conv_ready"), sem("lru_mm"), sem("sig_ready"), sem("loga_ready")
        tanh_ready, a_ready, var_ready, mult_ready = sem("tanh_ready"), sem("a_ready"), sem("var_ready"), sem("mult_ready")
        soft_a, soft_b, soft_c = sem("soft_a"), sem("soft_b"), sem("soft_c")
        scan_ready, hl_saved = sem("scan_ready"), sem("hl_saved")
        score_mm, score_copied = sem("score_mm"), sem("score_copied")
        lists_ready, cidx_ready, cidx_used = sem("lists_ready"), sem("cidx_ready"), sem("cidx_used")
        dif_ready, exp_ready = sem("dif_ready"), sem("exp_ready")
        sel_ready, selT_done, idT_ready = sem("sel_ready"), sem("selT_done"), sem("idT_ready")
        onehots_ready, gcopied = sem("onehots_ready"), sem("gcopied")
        gmm = [[sem(f"gmm{h}{q}") for q in range(2)] for h in range(2)]
        stage_out = [sem("stage_out0"), sem("stage_out1")]
        gate_in = [sem("gate_in0"), sem("gate_in1")]
        prod_done, gwhi_ready, gw_ready = sem("prod_done"), sem("gwhi_ready"), sem("gw_ready")
        vhalf_done = sem("vhalf_done")
        vbank_free = [sem(f"vbank{b}_free") for b in range(4)]
        x2_ready, out_ready = sem("x2_ready"), sem("out_ready")
        out_sem = sem("out_sem")
        dve_steps, act_steps, pool_steps = sem("dve_steps"), sem("act_steps"), sem("pool_steps")

        def by_seq(t, start, step):
            return t[:, :, start:start + NB * step].rearrange("p c (b k) -> p c b k", k=step)

        def wait_evacuated(eng, n):
            eng.wait_ge(bank_free[0], n // 2 + 1)
            eng.wait_ge(bank_free[1], n // 2 + 1)

        block = ctx.enter_context(nc.Block())

        @block.sync
        def _(sp):
            for u in range(RAW):
                sp.dma_start(raw[:, u, :], w_stream[u]).then_inc(raw_in[u], 16)
            with sp.Fori(0, NU // RAW - 1) as i:
                for k in range(RAW):
                    sp.wait_ge(lo_ready, i * RAW + k + 1)
                    sp.dma_start(raw[:, k, :], w_stream[i * RAW + (RAW + k)]).then_inc(raw_in[k], 16)
            sp.wait_ge(states_saved, 2)
            sp.dma_start(o_conv, o_cv[:, :, :, :]).then_inc(out_sem, 16)
            sp.wait_ge(hl_saved, 2)
            sp.dma_start(o_lru, o_hl[:, :, :]).then_inc(out_sem, 16)
            sp.wait_ge(out_ready, 1)
            sp.dma_start(o_y, acc[:, :, :]).then_inc(out_sem, 16)
            sp.wait_ge(out_sem, 48)
            sp.wait_ge(pool_saved, 16)

        @block.gpsimd
        def _(pool):
            ch = Chain(pool, pool_steps)
            nc.gpsimd.memset(csplit[:, :, :].bitcast(F), 0.0).then_inc(consts, 1)
            nc.gpsimd.memset(ones[:, :], 1.0).then_inc(consts, 1)
            nc.gpsimd.memset(epsc[:, :], EPS).then_inc(consts, 1)
            nc.gpsimd.iota(iota[:, :], pattern=[[1, P]], base=0, channel_multiplier=0,
                           allow_small_or_imprecise_dtypes=True).then_inc(consts, 1)
            ch.link(nc.gpsimd.memset(ident[:, :], 0.0))
            nc.gpsimd.affine_select(out=ident[:, :], in_=ident[:, :], compare_op=ALU.not_equal, fill=1.0,
                                    base=0, pattern=[[-1, P]], channel_multiplier=1).then_inc(consts, 1)
            pool.wait_ge(in_hist, 16)
            pool.wait_ge(alo_ready, 1)
            nc.gpsimd.memset(ucat[:, :, 0:CW - 1], 0.0).then_inc(hist_ready, 1)
            nc.gpsimd.memset(pcat[:, :, 0:HIST], 0.0).then_inc(hist_ready, 1)
            for c in range(LC):
                nc.gpsimd.tensor_copy(ucat[:, c, CAT:CL].rearrange("p (b k) -> p b k", k=CS)[:, :, 0:CW - 1],
                                      hist_conv[:, c]).then_inc(hist_ready, 1)
                nc.gpsimd.tensor_copy(pcat[:, c, PAT:PL].rearrange("p (b k) -> p b k", k=PS)[:, :, 0:HIST],
                                      hist_pool[:, c]).then_inc(hist_ready, 1)
            wait_evacuated(pool, 16)
            pool.wait_ge(hist_ready, 2 + 2 * LC)
            pool.dma_start(o_pool, pcat).then_inc(pool_saved, 16)
            nc.gpsimd.tensor_copy(o_cv[:, :, 0, :], ucat[:, :, SEQ:SEQ + CW - 1]).then_inc(states_saved, 1)
            nc.gpsimd.tensor_copy(o_cv[:, :, 1:, :], by_seq(ucat, CAT, CS)[:, :, :, NS:]).then_inc(states_saved, 1)
            pool.wait_ge(scan_ready, LC)
            nc.gpsimd.tensor_copy(o_hl[:, :, 0], xc[:, :, SEQ - 1]).then_inc(hl_saved, 1)
            nc.gpsimd.tensor_copy(o_hl[:, :, 1:], by_seq(xc_f, CAT, CS)[:, :, :, NS - 1]).then_inc(hl_saved, 1)
            for i in range(TT):
                pool.wait_ge(lists_ready, i * 2 + 2)
                at_least(pool, cidx_used, i)
                for a, n in PAIRS:
                    o = sum(m for b, m in PAIRS if b < a)
                    nc.gpsimd.tensor_tensor(cidx[:, :, o:o + n], topf[:, :, 0, a:a + 1].to_broadcast([P, HEADS, n]),
                                            topf[:, :, 1, 0:n], ALU.add).then_inc(cidx_ready, 1)
                nc.gpsimd.tensor_tensor(cidx[:, :, NCAND - 8:], topf[:, :, 0, 8:TOPK],
                                        topf[:, :, 1, 0:1].to_broadcast([P, HEADS, 8]), ALU.add).then_inc(cidx_ready, 1)

        @block.scalar
        def _(act):
            ch = Chain(act, act_steps)
            act.dma_start(c_ap := view(gate_o + NHIST, DC, NC), c_d).then_inc(in_c, 16)
            act.dma_start(vecs[:, :], vecs_d).then_inc(in_vecs, 16)
            act.dma_start(x[:, :, :], x_d).then_inc(in_x, 16)
            act.dma_start(hist, hist_d).then_inc(in_hist, 16)
            act.dma_start(poolw, poolw_d).then_inc(in_poolw, 16)

            def hi(u, slot=None):
                s = (u if slot is None else slot) % RAW
                if slot is None:
                    act.wait_ge(raw_in[s], 16 * (u // RAW + 1))
                    if u >= SPL:
                        act.wait_ge(pe_unit, u - SPL + 1)
                    nc.scalar.activation(w_hi[:, s % SPL, :], raw[:, s, :], ACT.Copy).then_inc(hi_ready, 1)

            def hi_at(u, slot, u4):
                act.wait_ge(raw_in[slot], u4 * 16 + 16)
                at_least(act, pe_unit, u + (1 - SPL))
                nc.scalar.activation(w_hi[:, slot % SPL, :], raw[:, slot, :], ACT.Copy).then_inc(hi_ready, 1)

            def hi_next(u0, i, per, k):
                n = u0 + k + 1
                hi_at(i * per + n, n % RAW, i * (per // RAW) + n // RAW)

            def stats(n, out, width, bank_no):
                act.wait_ge(stat_ready, n)
                nc.scalar.activation(out, bank(bank_no, T), ACT.Sqrt, bias=epsc[:, :], scale=1.0 / width).then_inc(std_ready, 1)

            hi(0)
            act.wait_ge(in_c, 16)
            csil = view(gate_o + NHIST + DC * NC, DC, NC)
            nc.scalar.activation(csil, c_ap, ACT.Silu).then_inc(csil_ready, 1)
            act.wait_ge(csil_ready, 1)
            act.wait_ge(consts, 5)
            nc.scalar.activation(csplit[:, :, 0:NC], csil, ACT.Copy).then_inc(chi_ready, 1)
            def ada_part(m):
                for k in range(DC):
                    hi_next(ADA0, m, DC, k)
                act.wait_ge(pe_unit, m * DC + DC)
                at_least(act, modT_done, m)
                for b in range(2):
                    i = nc.scalar.activation(modrow[0:2 * NC, b * 512:(b + 1) * 512], bank(b)[0:2 * NC, :], ACT.Copy)
                i.then_inc(rowa_ready, 1)

            rounds(act, 6, ada_part)
            act.wait_ge(in_x, 16)
            act.wait_ge(modT_done, 6)
            nc.scalar.activation(work1, x[:, :, :], ACT.Square).then_inc(sq_ready, 1)
            stats(1, rstd[:, 0, :], D, 5)
            act.wait_ge(t_ready, 1)
            nc.scalar.activation(act_hi[:, :, :], work2, ACT.Copy).then_inc(ahi_ready, 1)
            with act.Fori(0, 4) as i:
                for k in range(4):
                    hi_next(Z0, i, 4, k)
            with act.Fori(0, 2) as i:
                for k in range(4):
                    hi_next(Z0 + 16, i, 4, k)
                    act.wait_ge(pe_unit, i * 4 + (Z0 + 16 + k + 1))
                    if k == 0:
                        act.wait_ge(hist_ready, 2 + 2 * LC)
                    nc.scalar.activation(gate[:, i * 4 + k, :], bank(k % 2, T), ACT.Gelu_apprx_tanh).then_inc(bank_free[k % 2], 1)
            act.wait_ge(in_vecs, 16)
            ch.link(nc.scalar.activation(soft[:, 0, :], vec("lam"), ACT.Abs))
            ch.link(nc.scalar.activation(soft[:, 1, :], soft[:, 0, :], ACT.Exp, scale=-1.0))
            nc.scalar.activation(soft[:, 2, :], soft[:, 1, :], ACT.Ln, bias=1.0).then_inc(soft_a, 1)
            act.wait_ge(pool_mm, LC)
            act.dma_start(lruw, lruw_d).then_inc(in_lruw, 16)
            for c in range(LC):
                act.wait_ge(lru_mm, c + 1)
                nc.scalar.activation(ra[:, c, :], bank(2 + c % 2, XL), ACT.Sigmoid, bias=vec("ba")[:, c:c + 1]).then_inc(act_steps, 1)
                nc.scalar.activation(ii[:, c, :], bank(6 + c % 2, XL), ACT.Sigmoid, bias=vec("bx")[:, c:c + 1]).then_inc(sig_ready, 1)
            act.wait_ge(loga_ready, 1)
            act.wait_ge(states_saved, 2)
            act.wait_ge(conv_ready, LC)
            nc.scalar.activation(tanhs, ra, ACT.Tanh, scale=-1.0).then_inc(tanh_ready, 1)
            act.wait_ge(tanh_ready, 1)
            nc.scalar.activation(ra, ra, ACT.Exp).then_inc(a_ready, 1)
            act.wait_ge(var_ready, 1)
            nc.scalar.activation(xc, xc, ACT.Sqrt).then_inc(mult_ready, 1)
            act.wait_ge(ypool_ready, LC + 1)
            nc.scalar.activation(ysq[:, 0:LC, :], y_lru, ACT.Square).then_inc(sq_ready, 1)
            nc.scalar.activation(ysq[:, LC:, :], y_pool, ACT.Square).then_inc(sq_ready, 1)
            stats(2, rstd[:, 0, :], D // 2, 5)
            stats(3, rstd[:, 1, :], D // 2, 4)
            act.wait_ge(t_ready, 3)
            nc.scalar.activation(act_hi[:, 0:LC, :], y_lru, ACT.Copy).then_inc(ahi_ready, 1)
            nc.scalar.activation(act_hi[:, LC:, :], y_pool, ACT.Copy).then_inc(ahi_ready, 1)
            with act.Fori(0, NO // 4) as i:
                for k in range(4):
                    hi_next(O0, i, 4, k)
            wait_evacuated(act, NZ + NO)
            act.wait_ge(hl_saved, 2)
            nc.scalar.activation(work1, x[:, :, :], ACT.Square).then_inc(sq_ready, 1)
            stats(4, rstd[:, 0, :], D, 5)
            act.wait_ge(t_ready, 4)
            nc.scalar.activation(act_hi[:, :, :], work2, ACT.Copy).then_inc(ahi_ready, 1)
            act.wait_ge(alo_ready, 3)
            act.dma_start(keysT, keys_d).then_inc(in_keys, 16)
            with act.Fori(0, NQ // 4) as i:
                for k in range(4):
                    hi_next(Q0, i, 4, k)
            for i in range(TT):
                act.wait_ge(score_mm, i + 1)
                at_least(act, lists_ready, i * 2)
                for b in range(4):
                    n = nc.scalar.activation(sc[:, 4 * b:4 * b + 4, :], bank(b).rearrange("p (a n) -> p a n", n=P), ACT.Copy)
                n.then_inc(score_copied, 1)
                act.wait_ge(dif_ready, i + 1)
                nc.scalar.activation(best, best, ACT.Exp).then_inc(exp_ready, 1)
            def gate_chunks(i):
                for c in range(2):
                    at_least(act, stage_out[c], i * 16)
                    for h in range(2):
                        for q in range(2):
                            act.wait_ge(gmm[h][q], i * 2 + (c + 1))
                            t0 = 8 * h + 4 * q
                            nc.scalar.activation(stage[:, c, :, t0:t0 + 4].rearrange("p n t -> p t n"),
                                                 bank(4 + 2 * h + q).rearrange("p (t n) -> p t n", n=P),
                                                 ACT.Copy).then_inc(gcopied, 1)
                    act.wait_ge(gcopied, i * 8 + (4 * c + 4))
                    act.dma_start(gates_dram[i * 2 + c], stage[:, c, :, :]).then_inc(stage_out[c], 16)

            rounds(act, NCH // 2, gate_chunks)

            def load_gates(g, par):
                act.dma_start(gates_in[:, par], gates_dram.rearrange("c p (g k) t -> g p c (k t)", k=EG)[g]
                              ).then_inc(gate_in[par], 16)

            for c in range(2):
                act.wait_ge(stage_out[c], 16 * (NCH // 2))
            load_gates(0, 0)

            def expert_tiles(hi_of, u, tile, par):
                for k in range(EG):
                    hi_of(k)
                    act.wait_ge(pe_unit, u(k) + 1)
                    nc.scalar.activation(gel[:, k % 2, :], bank(k % 2, T), ACT.Gelu_apprx_tanh).then_inc(bank_free[k % 2], 1)
                    act.wait_ge(prod_done, tile(k) + 1)
                    nc.scalar.activation(gw_hi[:, par, k, :], prod[:, k % 2, :], ACT.Copy).then_inc(gwhi_ready, 1)

            def hi_plain(u0):
                return lambda k: hi(u0 + k + 1)

            def hi_loop(u0, i):
                return lambda k: hi_next(u0, i, 4 * EG, k)

            load_gates(1, 1)
            expert_tiles(hi_plain(u_unit(0)), lambda k: u_unit(0) + k, lambda k: k, 0)
            with act.Fori(0, (NG - 2) // 2) as i:
                for j in range(2):
                    g0 = 1 + j
                    load_gates(i * 2 + (g0 + 1), (g0 + 1) % 2)
                    expert_tiles(hi_loop(u_unit(g0), i), lambda k: i * (4 * EG) + (u_unit(g0) + k),
                                 lambda k: i * (2 * EG) + (g0 * EG + k), g0 % 2)
                    for k in range(EG):
                        hi_next(v_unit(g0 - 1), i, 4 * EG, k)
            g = NG - 1
            expert_tiles(hi_plain(u_unit(g)), lambda k: u_unit(g) + k, lambda k: g * EG + k, g % 2)
            for k in range(2 * EG - 1):
                hi(v_unit(g - 1) + k + 1)
            act.wait_ge(x2_ready, 1)
            nc.scalar.activation(acc[:, :, :], x[:, :, :], ACT.Square).then_inc(sq_ready, 1)
            stats(5, rstd[:, 0, :], D, 6)

        @block.vector
        def _(dve):
            ch = Chain(dve, dve_steps)
            link = ch.link
            V = nc.vector

            def lo(u):
                s = u % RAW
                dve.wait_ge(hi_ready, u + 1)
                V.tensor_tensor(w_lo[:, s % SPL, :], raw[:, s, :], w_hi[:, s % SPL, :].bitcast(F), ALU.subtract).then_inc(lo_ready, 1)

            def lo_next(u0, i, per, k):
                n = u0 + k + 1
                s = n % RAW
                dve.wait_ge(hi_ready, i * per + (n + 1))
                V.tensor_tensor(w_lo[:, s % SPL, :], raw[:, s, :], w_hi[:, s % SPL, :].bitcast(F), ALU.subtract).then_inc(lo_ready, 1)

            def modulate(src, rs, scale, shift, out, ready):
                link(V.tensor_tensor(out, src, rs.unsqueeze(1).to_broadcast([P, DC, T]), ALU.mult))
                os = out[:, :, SEQ:T].rearrange("p c (b t) -> p c b t", t=NS)
                for c in range(DC):
                    ch.done(V.tensor_scalar(out[:, c, 0:SEQ], out[:, c, 0:SEQ], scale[:, c, 0:1], shift[:, c, 0:1],
                                            ALU.mult, ALU.add))
                link(V.tensor_tensor(os, os, scale[:, :, 1:].unsqueeze(3).to_broadcast([P, DC, NB, NS]), ALU.mult))
                V.tensor_tensor(os, os, shift[:, :, 1:].unsqueeze(3).to_broadcast([P, DC, NB, NS]), ALU.add).then_inc(ready, 1)

            def inv_std(n, r):
                dve.wait_ge(std_ready, n)
                link(V.reciprocal(r, r))

            lo(0)
            dve.wait_ge(chi_ready, 1)
            csil = view(gate_o + NHIST + DC * NC, DC, NC)
            V.tensor_tensor(csplit[:, :, NC:2 * NC], csil, csplit[:, :, 0:NC].bitcast(F), ALU.subtract).then_inc(clo_ready, 1)
            dve.wait_ge(in_vecs, 16)
            def ada_part(m):
                for k in range(DC):
                    lo_next(ADA0, m, DC, k)
                dve.wait_ge(pe_unit, m * DC + DC)
                at_least(dve, modT_done, m)
                for b in range(2, 4):
                    n = V.tensor_copy(modrow[0:2 * NC, b * 512:(b + 1) * 512], bank(b)[0:2 * NC, :])
                n.then_inc(rowb_ready, 1)
                dve.wait_ge(modT_done, m + 1)
                mt = bank(4, DC * 2 * NC).rearrange("p (c n) -> p c n", n=2 * NC)
                bias = vec("b_ada").rearrange("p (m c) -> p m c", m=6)
                link(V.tensor_tensor(mod[:, m, :, :], mt[:, :, 0:NC], bias[:, m, :].unsqueeze(2).to_broadcast([P, DC, NC]), ALU.add))
                V.tensor_tensor(mod[:, m, :, :], mod[:, m, :, :], mt[:, :, NC:2 * NC], ALU.add).then_inc(mod_ready, 1)

            ada_part(0)
            with ch.loop(1, 6, 1) as m:
                ada_part(m)
            dve.wait_ge(mod_ready, 6)
            for j, (s, m, g) in enumerate(((scale1, 1, "norm1"), (scale2, 4, "norm2"))):
                V.tensor_scalar(s[:, :, :], mod[:, m, :, :], 1.0, None, ALU.add).then_inc(bank_free[j], 1)
                dve.wait_ge(bank_free[j], 1)
                link(V.tensor_tensor(s[:, :, :], s[:, :, :], vec(g).unsqueeze(2).to_broadcast([P, DC, NC]), ALU.mult))
            inv_std(1, rstd[:, 0, :])
            modulate(x[:, :, :], rstd[:, 0, :], scale1, mod[:, 0], work2, t_ready)
            dve.wait_ge(ahi_ready, 1)
            dve.wait_ge(t_ready, 1)
            V.tensor_tensor(act_lo[:, :, :], work2, act_hi[:, :, :].bitcast(F), ALU.subtract).then_inc(alo_ready, 1)

            def z_out(dst, start, step, first):
                with dve.Fori(0, 2) as i:
                    for k in range(4):
                        lo_next(first, i, 4, k)
                        dve.wait_ge(pe_unit, i * 4 + (first + k + 1))
                        b = bank(k % 2, T)
                        V.tensor_copy(dst[:, i * 4 + k, step - NS:step - NS + SEQ], b[:, 0:SEQ])
                        V.tensor_copy(dst[:, i * 4 + k, start:start + NB * step].rearrange("p (b k) -> p b k", k=step)[:, :, step - NS:],
                                      b[:, SEQ:T].rearrange("p (b t) -> p b t", t=NS)).then_inc(bank_free[k % 2], 1)

            dve.wait_ge(alo_ready, 1)
            z_out(pcat, PAT, PS, Z0)
            z_out(ucat, CAT, CS, Z0 + 8)
            with dve.Fori(0, 2) as i:
                for k in range(4):
                    lo_next(Z0 + 16, i, 4, k)
            wait_evacuated(dve, 16)
            dve.wait_ge(hist_ready, 2 + 2 * LC)

            def double(dst, src, d0, s0, n, by, fr):
                link(V.tensor_tensor(dst[:, d0:d0 + n, fr:PL], src[:, s0:s0 + n, fr:PL], src[:, s0:s0 + n, fr - by:PL - by], ALU.add))

            def pooled(g, s, c0):
                win = WINDOWS[g]
                p = pcat[:, 2 * g:2 * g + 2, :]
                d = dd[:, 2 * g:2 * g + 2, :]
                s = s[:, c0:c0 + 2, :]
                link(V.scalar_tensor_tensor(out=d[:, :, 0:SEQ], in0=s[:, :, HIST:PAT], scalar=1.0 / win,
                                            in1=p[:, :, HIST:PAT], op0=ALU.mult, op1=ALU.subtract))
                ci = vec("cinv")[:, g * HIST:(g + 1) * HIST].unsqueeze(1).to_broadcast([P, 2, HIST])
                link(V.tensor_tensor(fix[:, :, :], s[:, :, HIST:2 * HIST], ci, ALU.mult))
                ch.done(V.tensor_tensor(d[:, :, 0:HIST], fix[:, :, :], p[:, :, HIST:2 * HIST], ALU.subtract))
                for c in range(2):
                    def tail(t):
                        return t[:, c, PAT:PL].rearrange("p (b k) -> p b k", k=PS)[:, :, HIST:]
                    n = V.scalar_tensor_tensor(out=d[:, c, SEQ:T].rearrange("p (b t) -> p b t", t=NS), in0=tail(s),
                                               scalar=1.0 / win, in1=tail(p), op0=ALU.mult, op1=ALU.subtract)
                    if c == 0:
                        ch.done(n)
                n.then_inc(d_ready, 1)
                ch.wait()

            double(sA, pcat, 0, 0, LC, 1, 1)
            pooled(0, sA, 0)
            double(sB, sA, 0, 2, 6, 2, 3)
            pooled(1, sB, 0)
            double(sA, sB, 4, 2, 4, 4, 7)
            pooled(2, sA, 4)
            double(sB, sA, 4, 6, 2, 8, 15)
            pooled(3, sB, 4)

            dve.wait_ge(soft_a, 1)
            u = soft[:, 1, :]
            link(V.tensor_scalar(soft[:, 3, :], u, 1.0, 1.0, ALU.add, ALU.subtract))
            link(V.tensor_scalar(soft[:, 4, :], soft[:, 3, :], 0.0, None, ALU.is_equal))
            link(V.tensor_tensor(soft[:, 3, :], soft[:, 3, :], soft[:, 4, :], ALU.add))
            link(V.reciprocal(soft[:, 3, :], soft[:, 3, :]))
            link(V.tensor_tensor(soft[:, 3, :], soft[:, 3, :], soft[:, 2, :], ALU.mult))
            link(V.tensor_tensor(soft[:, 3, :], soft[:, 3, :], soft[:, 4, :], ALU.add))
            link(V.tensor_tensor(soft[:, 3, :], soft[:, 3, :], u, ALU.mult))
            link(V.tensor_scalar(soft[:, 4, :], vec("lam"), -1.0, 0.0, ALU.mult, ALU.max))
            link(V.tensor_tensor(soft[:, 3, :], soft[:, 3, :], soft[:, 4, :], ALU.add))
            link(V.tensor_scalar(soft[:, 5, :], soft[:, 3, :], -8.0, None, ALU.mult))

            cw = vec("conv_w").rearrange("p (k c) -> p k c", k=CW)
            dve.wait_ge(d_ready, 4)
            for c in range(LC):
                link(V.tensor_scalar(xc[:, c, :], ucat[:, c, CW - 1:CL], cw[:, CW - 1, c:c + 1], vec("conv_b")[:, c:c + 1],
                                     ALU.mult, ALU.add))
                for k in range(CW - 1):
                    n = V.scalar_tensor_tensor(out=xc[:, c, :], in0=ucat[:, c, k:k + XL], scalar=cw[:, k, c:c + 1],
                                               in1=xc[:, c, :], op0=ALU.mult, op1=ALU.add)
                    if k < CW - 2:
                        link(n)
                n.then_inc(conv_ready, 1)

            dve.wait_ge(pool_saved, 16)
            for c in range(LC):
                dve.wait_ge(pool_mm, c + 1)
                V.tensor_scalar(y_pool[:, c, :], bank(4 + c % 2, T), vec("pool_b")[:, c:c + 1], vec("pool_s")[:, c:c + 1],
                                ALU.add, ALU.mult).then_inc(ypool_ready, 1)

            for c in range(LC):
                dve.wait_ge(sig_ready, c + 1)
                n = V.tensor_scalar(ra[:, c, :], ra[:, c, :], soft[:, 5, c:c + 1], None, ALU.mult)
            n.then_inc(loga_ready, 1)
            link(V.tensor_tensor(ii, ii, xc, ALU.mult))
            dve.wait_ge(a_ready, 1)
            link(V.tensor_tensor(xc, ra, ra, ALU.mult))
            V.scalar_tensor_tensor(out=xc, in0=xc, scalar=1.0, in1=tanhs, op0=ALU.add, op1=ALU.mult).then_inc(var_ready, 1)
            dve.wait_ge(mult_ready, 1)
            link(V.memset(xc[:, :, 0:1], 1.0))
            link(V.tensor_tensor(ii, ii, xc, ALU.mult))
            border = CAT - 1
            ch.done(V.memset(by_seq(ra_f, border, CS)[:, :, :, 0], 0.0))
            link(V.tensor_copy(by_seq(ii_f, border, CS)[:, :, :, 0], vec("h0").rearrange("p (c b) -> p c b", b=NB)))
            for c in range(LC):
                V.tensor_tensor_scan(xc[:, c, :], ra[:, c, :], ii[:, c, :], 0.0, ALU.mult, ALU.add).then_inc(scan_ready, 1)
            dve.wait_ge(scan_ready, LC)
            wait_evacuated(dve, NZ)
            link(V.tensor_tensor(y_lru[:, :, 0:SEQ], xc[:, :, 0:SEQ], gate[:, :, 0:SEQ], ALU.mult))
            V.tensor_tensor(by_seq(y_lru, SEQ, NS), by_seq(xc_f, CAT, CS)[:, :, :, 0:NS], by_seq(gate, SEQ, NS),
                            ALU.mult).then_inc(ypool_ready, 1)
            for n_, y, g, r in ((2, y_lru, "gn_lru", 0), (3, y_pool, "gn_pool", 1)):
                inv_std(n_, rstd[:, r, :])
                for c in range(LC):
                    n = V.scalar_tensor_tensor(out=y[:, c, :], in0=y[:, c, :], scalar=vec(g)[:, c:c + 1],
                                               in1=rstd[:, r, :], op0=ALU.mult, op1=ALU.mult)
                n.then_inc(t_ready, 1)
            dve.wait_ge(t_ready, 3)
            dve.wait_ge(ahi_ready, 3)
            link(V.tensor_tensor(act_lo[:, 0:LC, :], y_lru, act_hi[:, 0:LC, :].bitcast(F), ALU.subtract))
            V.tensor_tensor(act_lo[:, LC:, :], y_pool, act_hi[:, LC:, :].bitcast(F), ALU.subtract).then_inc(alo_ready, 1)

            def residual(c, src, m, ready):
                xs = x[:, c, SEQ:T].rearrange("p (b t) -> p b t", t=NS)
                V.scalar_tensor_tensor(out=x[:, c, 0:SEQ], in0=src[:, 0:SEQ], scalar=mod[:, m, c, 0:1],
                                       in1=x[:, c, 0:SEQ], op0=ALU.mult, op1=ALU.add)
                tmp = rstd[:, 1, 0:NB * NS].rearrange("p (b t) -> p b t", t=NS)
                link(V.tensor_tensor(tmp, src[:, SEQ:T].rearrange("p (b t) -> p b t", t=NS),
                                     mod[:, m, c, 1:].unsqueeze(2).to_broadcast([P, NB, NS]), ALU.mult))
                V.tensor_tensor(xs, xs, tmp, ALU.add).then_inc(ready, 1)

            with ch.loop(0, NO // 4, 4) as i:
                for k in range(4):
                    lo_next(O0, i, 4, k)
                    dve.wait_ge(pe_unit, i * 4 + (O0 + k + 1))
                    dve.wait_ge(bank_free[1 - k % 2], i * 2 + ((NZ + k + 1) // 2 + 1))
                    residual(i * 4 + k, bank(k % 2, T), 2, bank_free[k % 2])
            wait_evacuated(dve, NZ + NO)
            inv_std(4, rstd[:, 0, :])
            modulate(x[:, :, :], rstd[:, 0, :], scale2, mod[:, 3], work2, t_ready)
            dve.wait_ge(ahi_ready, 4)
            dve.wait_ge(t_ready, 4)
            V.tensor_tensor(act_lo[:, :, :], work2, act_hi[:, :, :].bitcast(F), ALU.subtract).then_inc(alo_ready, 1)
            dve.wait_ge(alo_ready, 3)

            link(V.memset(qT[:, :, T:TP], 0.0))
            with dve.Fori(0, NQ // 4) as i:
                for k in range(4):
                    lo_next(Q0, i, 4, k)
                    dve.wait_ge(pe_unit, i * 4 + (Q0 + k + 1))
                    V.tensor_copy(qT[:, i * 4 + k, 0:T], bank(k % 2, T)).then_inc(bank_free[k % 2], 1)

            pos50 = iota[:, 0:NCAND]

            def top16(src, tmp, vals, idx):
                link(V.max(vals[:, 0:8], src))
                ch.done(V.max_index(idx[:, 0:8], vals[:, 0:8], src))
                link(V.match_replace(tmp, vals[:, 0:8], src, -3.0e38))
                link(V.max(vals[:, 8:16], tmp))
                ch.done(V.max_index(idx[:, 8:16], vals[:, 8:16], tmp))

            for i in range(TT):
                dve.wait_ge(score_copied, i + 1)
                at_least(dve, cidx_ready, i * 9)
                for h in range(HEADS):
                    for p in range(2):
                        top16(sc[:, 2 * h + p, :], sc2[:, 2 * h + p, :], topv[:, h, p, :], topi[:, h, p, :].bitcast(U32))
                ch.wait()
                V.tensor_scalar(topf[:, :, 0, :], topi[:, :, 0, :].bitcast(U32), float(P), None, ALU.mult).then_inc(lists_ready, 1)
                V.tensor_copy(topf[:, :, 1, :], topi[:, :, 1, :].bitcast(U32)).then_inc(lists_ready, 1)
                o = 0
                for a, n in PAIRS:
                    ch.done(V.tensor_tensor(cand[:, :, o:o + n], topv[:, :, 0, a:a + 1].to_broadcast([P, HEADS, n]),
                                            topv[:, :, 1, 0:n], ALU.add))
                    o += n
                link(V.tensor_tensor(cand[:, :, o:], topv[:, :, 0, 8:TOPK], topv[:, :, 1, 0:1].to_broadcast([P, HEADS, 8]), ALU.add))
                at_least(dve, selT_done, i)
                for h in range(HEADS):
                    top16(cand[:, h, :], cand2[:, h, :], best[:, h, :], bpos[:, h, :].bitcast(U32))
                ch.wait()
                link(V.tensor_copy(bposf, bpos.bitcast(U32)))
                dve.wait_ge(cidx_ready, i * 9 + 9)
                for h in range(0, HEADS, 2):
                    link(V.tensor_tensor(eq, pos50.unsqueeze(1).unsqueeze(1).to_broadcast([P, 2, TOPK, NCAND]),
                                         bposf[:, h:h + 2, :].unsqueeze(3).to_broadcast([P, 2, TOPK, NCAND]), ALU.is_equal))
                    link(V.tensor_tensor(eq, eq, cidx[:, h:h + 2, :].unsqueeze(2).to_broadcast([P, 2, TOPK, NCAND]), ALU.mult))
                    link(V.reduce_sum(eidx[:, h:h + 2, :], eq, axis=AX.X))
                link(V.tensor_copy(gsum, best[:, :, 0]))
                V.tensor_tensor(best, best, gsum.unsqueeze(2).to_broadcast([P, HEADS, TOPK]), ALU.subtract).then_inc(dif_ready, 1)
                link(V.tensor_copy(eint.bitcast(I32), eidx.rearrange("p h k -> p (h k)")))
                ch.done(V.tensor_scalar(eint2.bitcast(I32), eint.bitcast(I32), 7, None, ALU.logical_shift_right))
                link(V.tensor_scalar(eint.bitcast(I32), eint.bitcast(I32), P - 1, None, ALU.bitwise_and))
                V.tensor_copy(sel[:, 0, :], eint2.bitcast(I32)).then_inc(cidx_used, 1)
                V.tensor_copy(sel[:, 1, :], eint.bitcast(I32))
                dve.wait_ge(exp_ready, i + 1)
                link(V.reduce_sum(gsum, best, axis=AX.X))
                link(V.reciprocal(gsum, gsum))
                n = V.tensor_tensor(sel[:, 2, :].rearrange("p (h k) -> p h k", k=TOPK), best,
                                    gsum.unsqueeze(2).to_broadcast([P, HEADS, TOPK]), ALU.mult)
                n.then_inc(sel_ready, 1)

            dve.wait_ge(selT_done, TT)
            for j in range(3):
                n = V.tensor_copy(idT[:, j, :], bank(4 + j, TP))
            n.then_inc(idT_ready, 1)
            dve.wait_ge(idT_ready, 1)

            def onehots(i):
                for h in range(2):
                    at_least(dve, gmm[h][1], i)

                    def col(j):
                        return idT[:, j, bass.ds(i * TCH + 8 * h, 8)].unsqueeze(2).to_broadcast([P, 8, P])
                    wide = iota[:, :].unsqueeze(1).to_broadcast([P, 8, P])
                    V.tensor_tensor(one1[:, h], wide, col(0), ALU.is_equal)
                    link(V.tensor_tensor(one2[:, h], wide, col(1), ALU.is_equal))
                    V.tensor_tensor(one2[:, h], one2[:, h], col(2), ALU.mult).then_inc(onehots_ready, 1)

            onehots(0)
            with ch.loop(1, NCH, 2) as i:
                onehots(i)
            for c in range(2):
                dve.wait_ge(stage_out[c], 16 * (NCH // 2))
            for b in range(4):
                V.memset(acc[:, b::4, :], 0.0).then_inc(vbank_free[b], 1)

            def expert_tiles(lo_of, tile, half, par, turn):
                dve.wait_ge(gate_in[par], turn)
                for k in range(EG):
                    lo_of(k)
                    dve.wait_ge(bank_free[k % 2], half + ((M0 - Z0) // 2 + k // 2 + 2))
                    V.tensor_tensor(prod[:, k % 2, :].rearrange("p (c t) -> p c t", t=TCH),
                                    gel[:, k % 2, :].rearrange("p (c t) -> p c t", t=TCH), gates_in[:, par, :, k, :],
                                    ALU.mult).then_inc(prod_done, 1)
                    dve.wait_ge(gwhi_ready, tile + (k + 1))
                    V.tensor_tensor(gw_lo[:, par, k, :], prod[:, k % 2, :], gw_hi[:, par, k, :].bitcast(F),
                                    ALU.subtract).then_inc(gw_ready, 1)

            def add_up(lo_of, unit, units, uses):
                for b in range(4):
                    dve.wait_ge(vbank_free[b], uses + 1)
                for k in range(EG):
                    lo_of(k)
                    dve.wait_ge(vhalf_done, units + (k + 1))
                    for h in range(2):
                        c = 2 * k + h
                        if h == 1:
                            dve.wait_ge(pe_unit, unit + (k + 1))
                        V.tensor_tensor(acc[:, c, :], acc[:, c, :], bank(2 + c % 4, T), ALU.add).then_inc(vbank_free[c % 4], 1)

            def lo_after(u0, last=NU):
                return lambda k: lo(u0 + k + 1) if u0 + k + 1 < last else None

            expert_tiles(lo_after(u_unit(0)), 0, 0, 0, 16)
            with dve.Fori(0, (NG - 2) // 2) as i:
                for j in range(2):
                    g = 1 + j
                    expert_tiles(lambda k: lo_next(u_unit(g), i, 4 * EG, k), i * (2 * EG) + g * EG, i * EG + g * EG // 2,
                                 g % 2, i * 16 + 16 * (g // 2 + 1))
                    add_up(lambda k: lo_next(v_unit(g - 1), i, 4 * EG, k), i * (4 * EG) + v_unit(g - 1),
                           i * (2 * EG) + (g - 1) * EG, i * (DC // 2) + (g - 1) * DC // 4)
            g = NG - 1
            expert_tiles(lo_after(u_unit(g)), g * EG, g * EG // 2, g % 2, 16 * (g // 2 + 1))
            add_up(lo_after(v_unit(g - 1)), v_unit(g - 1), (g - 1) * EG, (g - 1) * DC // 4)
            add_up(lo_after(v_unit(g)), v_unit(g), g * EG, g * DC // 4)
            for b in range(4):
                dve.wait_ge(vbank_free[b], NG * DC // 4 + 1)
            for c in range(DC):
                ch.done(V.scalar_tensor_tensor(out=x[:, c, 0:SEQ], in0=acc[:, c, 0:SEQ], scalar=mod[:, 5, c, 0:1],
                                               in1=x[:, c, 0:SEQ], op0=ALU.mult, op1=ALU.add))
            accs = acc[:, :, SEQ:T].rearrange("p c (b t) -> p c b t", t=NS)
            xs = x[:, :, SEQ:T].rearrange("p c (b t) -> p c b t", t=NS)
            link(V.tensor_tensor(accs, accs, mod[:, 5, :, 1:].unsqueeze(3).to_broadcast([P, DC, NB, NS]), ALU.mult))
            V.tensor_tensor(xs, xs, accs, ALU.add).then_inc(x2_ready, 1)
            dve.wait_ge(x2_ready, 1)
            inv_std(5, rstd[:, 0, :])
            dve.wait_ge(stat_ready, 5)
            for c in range(DC):
                n = V.scalar_tensor_tensor(out=acc[:, c, :], in0=x[:, c, :], scalar=vec("final")[:, c:c + 1],
                                           in1=rstd[:, 0, :], op0=ALU.mult, op1=ALU.mult)
            n.then_inc(out_ready, 1)

        @block.tensor
        def _(pe):
            mm = nc.tensor.matmul

            def project(slot, b):
                s = slot % SPL
                for c in range(DC):
                    w = slice(c * P, (c + 1) * P)
                    mm(bank(b, T), w_hi[:, s, w], act_hi[:, c, :], start=c == 0, stop=False)
                    mm(bank(b, T), w_hi[:, s, w], act_lo[:, c, :], start=False, stop=False)
                    n = mm(bank(b, T), w_lo[:, s, w], act_hi[:, c, :], start=False, stop=c == DC - 1)
                n.then_inc(pe_unit, 1)

            def sums(n, src, chunks, b):
                pe.wait_ge(sq_ready, n)
                for c in range(chunks):
                    i = mm(bank(b, T), ones[:, :], src[:, c, :], start=c == 0, stop=c == chunks - 1)
                i.then_inc(stat_ready, 1)

            pe.wait_ge(consts, 5)
            pe.wait_ge(clo_ready, 1)
            def ada_part(m):
                at_least(pe, rowa_ready, m)
                at_least(pe, rowb_ready, m)
                for k in range(DC):
                    pe.wait_ge(lo_ready, m * DC + (ADA0 + k + 1))
                    for w, first in ((w_hi, True), (w_lo, False)):
                        for b in range(4):
                            n = mm(bank(b), csplit[:, k, :], w[:, k % SPL, b * 512:(b + 1) * 512],
                                   start=k == 0 and first, stop=k == DC - 1 and not first)
                    n.then_inc(pe_unit, 1)
                pe.wait_ge(rowa_ready, m + 1)
                pe.wait_ge(rowb_ready, m + 1)
                at_least(pe, mod_ready, m)
                mm(bank(4, 2 * NC), modrow[0:2 * NC, 0:P], ident[0:2 * NC, 0:2 * NC], start=True, stop=True)
                for c in range(1, DC):
                    n = nc.tensor.transpose(bank(4, 2 * NC, c * 2 * NC), modrow[0:2 * NC, c * P:(c + 1) * P],
                                            ident[0:2 * NC, 0:2 * NC])
                n.then_inc(modT_done, 1)

            rounds(pe, 6, ada_part)
            sums(1, work1, DC, 5)

            def projections(first, count):
                with pe.Fori(0, count // 4) as i:
                    for k in range(4):
                        pe.wait_ge(lo_ready, i * 4 + (first + k + 1))
                        pe.wait_ge(bank_free[k % 2], i * 2 + ((first - Z0) // 2 + k // 2 + 1))
                        project(k, k % 2)

            pe.wait_ge(alo_ready, 1)
            projections(Z0, NZ)
            pe.wait_ge(in_poolw, 16)
            for c in range(LC):
                g, j = c // 2, c % 2
                pe.wait_ge(d_ready, g + 1)
                if c >= 2:
                    pe.wait_ge(ypool_ready, c - 1)
                for h in range(2):
                    n = mm(bank(4 + c % 2, T), poolw[:, g, h, j * P:(j + 1) * P], dd[:, 2 * g + h, :], start=h == 0, stop=h == 1)
                n.then_inc(pool_mm, 1)
            pe.wait_ge(in_lruw, 16)
            for c in range(LC):
                pe.wait_ge(conv_ready, c + 1)
                if c >= 2:
                    pe.wait_ge(sig_ready, c - 1)
                mm(bank(2 + c % 2, XL), lruw[:, 0, c, :], xc[:, c, :], start=True, stop=True)
                mm(bank(6 + c % 2, XL), lruw[:, 1, c, :], xc[:, c, :], start=True, stop=True).then_inc(lru_mm, 1)
            sums(2, ysq, LC, 5)
            sums(3, ysq[:, LC:, :], LC, 4)
            pe.wait_ge(alo_ready, 2)
            projections(O0, NO)
            sums(4, work1, DC, 5)
            pe.wait_ge(alo_ready, 3)
            projections(Q0, NQ)
            wait_evacuated(pe, M0 - Z0)
            pe.wait_ge(in_keys, 16)

            def scores(t):
                pe.wait_ge(score_copied, t)
                for j in range(DC):
                    n = mm(bank(j // 4, P, j % 4 * P), qT[:, j, t * P:(t + 1) * P], keysT[:, j, :], start=True, stop=True)
                n.then_inc(score_mm, 1)

            def transposes(t):
                pe.wait_ge(sel_ready, t + 1)
                for j in range(3):
                    n = nc.tensor.transpose(bank(4 + j, P, t * P), sel[:, j, :], ident[:, :])
                n.then_inc(selT_done, 1)

            scores(0)
            for t in range(1, TT):
                scores(t)
                transposes(t - 1)
            transposes(TT - 1)
            pe.wait_ge(idT_ready, 1)
            def dense_gates(i):
                for h in range(2):
                    pe.wait_ge(onehots_ready, i * 2 + (h + 1))
                    at_least(pe, gcopied, i * 4)
                    for q in range(2):
                        for t in range(4):
                            n = mm(bank(4 + 2 * h + q, P, t * P), one1[:, h, 4 * q + t, :], one2[:, h, 4 * q + t, :],
                                   start=True, stop=True)
                        n.then_inc(gmm[h][q], 1)

            rounds(pe, NCH, dense_gates)

            def first_product(unit, half):
                for k in range(EG):
                    pe.wait_ge(lo_ready, unit + (k + 1))
                    pe.wait_ge(bank_free[k % 2], half + ((M0 - Z0) // 2 + k // 2 + 1))
                    project(k, k % 2)

            def second_product(unit, tiles, par, uses):
                pe.wait_ge(gw_ready, tiles + EG)
                for k in range(EG):
                    pe.wait_ge(lo_ready, unit + (k + 1))
                    s = k % SPL
                    for h in range(2):
                        b = (2 * k + h) % 4
                        pe.wait_ge(vbank_free[b], uses + ((2 * k + h) // 4 + 1))
                        for e in range(EG):
                            w = slice(e * 2 * P + h * P, e * 2 * P + (h + 1) * P)
                            mm(bank(2 + b, T), w_hi[:, s, w], gw_hi[:, par, e, :], start=e == 0, stop=False)
                            mm(bank(2 + b, T), w_hi[:, s, w], gw_lo[:, par, e, :], start=False, stop=False)
                            n = mm(bank(2 + b, T), w_lo[:, s, w], gw_hi[:, par, e, :], start=False, stop=e == EG - 1)
                        n.then_inc(vhalf_done if h == 0 else pe_unit, 1)

            first_product(u_unit(0), 0)
            with pe.Fori(0, (NG - 2) // 2) as i:
                for j in range(2):
                    g = 1 + j
                    first_product(i * (4 * EG) + u_unit(g), i * EG + g * EG // 2)
                    second_product(i * (4 * EG) + v_unit(g - 1), i * (2 * EG) + (g - 1) * EG, (g - 1) % 2,
                                   i * (DC // 2) + (g - 1) * DC // 4)
            g = NG - 1
            first_product(u_unit(g), g * EG // 2)
            for gg in (g - 1, g):
                second_product(v_unit(gg), gg * EG, gg % 2, gg * DC // 4)
            sums(5, acc, DC, 6)


def kernel(**inputs):
    import concourse.bacc as _bacc
    from concourse.bass_utils import run_bass_kernel_spmd as _run

    a = {k: np.asarray(v) for k, v in inputs.items()}

    def cols(v):
        v = v.reshape(-1, v.shape[-1] // P, P)
        return v.transpose(2, 0, 1).reshape(P, -1)

    def proj(w, order):
        n = w.shape[1] // P
        return w.reshape(DC, P, n, P).transpose(2, 1, 0, 3).reshape(n, P, 2048)[order]

    u = a["peer_u"][0].reshape(P, P, DC, P).transpose(1, 3, 2, 0).reshape(NG, EG, P, 2048)
    v = a["peer_v"][0].reshape(P, NG, EG, EG, 2 * P).transpose(1, 3, 0, 2, 4).reshape(NG, EG, P, 2048)
    parts = [a["w_ada"][0].reshape(DC, P, 6, 2048).transpose(2, 0, 1, 3).reshape(NADA, P, 2048),
             proj(a["w_in"][0], list(range(16, 24)) + list(range(16))),
             proj(a["w_out"][0], list(range(DC))), proj(a["peer_wq"][0], list(range(DC))), u[0]]
    for g in range(1, NG):
        parts += [u[g], v[g - 1]]
    w_stream = np.concatenate(parts + [v[NG - 1]])

    tokens = np.concatenate([a["x_prompt"][0], a["x_sample"].reshape(NB * NS, D)])
    x_d = tokens.reshape(T, DC, P).transpose(2, 1, 0)
    c_d = np.concatenate([a["c_prompt"], a["c_sample"]]).reshape(NC, DC, P).transpose(2, 1, 0)
    hist_d = np.concatenate([a["state_conv"][0].reshape(NB, CW - 1, LC, P).transpose(3, 2, 0, 1).reshape(P, -1),
                             a["state_pool"][0].reshape(NB, HIST, LC, P).transpose(3, 2, 0, 1).reshape(P, -1)], axis=1)
    h0 = a["state_lru"][0].reshape(NB, LC, P).transpose(2, 1, 0).reshape(P, -1)
    cinv = np.array([[1.0 / min(t + 1, w) for t in range(HIST)] for w in WINDOWS], np.float32).reshape(1, -1)
    table = {"b_ada": cols(a["b_ada"]), "norm1": cols(a["norm1_g"]), "norm2": cols(a["norm2_g"]),
             "final": cols(a["final_g"]), "gn_lru": cols(a["gnorm_lru_g"]), "gn_pool": cols(a["gnorm_pool_g"]),
             "conv_w": cols(a["conv_w"][0]), "conv_b": cols(a["conv_b"]), "ba": cols(a["lru_ba"].reshape(1, -1)),
             "bx": cols(a["lru_bx"].reshape(1, -1)), "lam": cols(a["lru_lambda"]), "pool_b": cols(a["pool_b"].reshape(1, -1)),
             "pool_s": cols(a["pool_scale"]), "cinv": np.repeat(cinv, P, axis=0), "h0": h0}
    vecs_d = np.concatenate([table[n] for n, _ in VCOLS], axis=1)
    lruw_d = np.stack([a["lru_wa"][0], a["lru_wx"][0]]).transpose(2, 0, 1, 3)
    poolw_d = a["pool_w"][0].reshape(4, 2, P, 2 * P).transpose(2, 0, 1, 3)
    keys_d = a["peer_keys"][0].reshape(DC, P, P).transpose(2, 0, 1)

    nc = _bacc.Bacc("TRN2", target_bir_lowering=False, num_devices=1)
    arrays, args = {}, []
    for name, v_ in (("w_stream", w_stream), ("vecs", vecs_d), ("c", c_d), ("hist", hist_d), ("x", x_d),
                     ("lruw", lruw_d), ("poolw", poolw_d), ("keys", keys_d)):
        v_ = np.ascontiguousarray(v_)
        arrays[f"in_{name}_dram"] = v_
        args.append(nc.dram_tensor(f"in_{name}_dram", v_.shape, mybir.dt.from_np(v_.dtype), kind="ExternalInput").ap())
    for i, shape in enumerate([(P, DC, T), (P, LC, NC, CW - 1), (P, LC, NC), (P, LC, PL)]):
        args.append(nc.dram_tensor(f"out_{i}_dram", shape, F, kind="ExternalOutput").ap())
    hybrid_step(nc, *args)
    r = _run(nc, [arrays], core_ids=[0]).results[0]
    y, cv, hl, pc = (r[f"out_{i}_dram"] for i in range(4))
    y = y.transpose(2, 1, 0).reshape(T, D)
    cv = cv.transpose(2, 3, 1, 0).reshape(1, NC, CW - 1, LC * P)
    hl = hl.transpose(2, 1, 0).reshape(1, NC, LC * P)
    pc = pc.transpose(2, 1, 0).reshape(PL, LC * P)
    pool_s = np.stack([pc[PAT + PS * b + NS:PAT + PS * (b + 1)] for b in range(NB)])[None]
    return (y[:SEQ][None], y[SEQ:].reshape(NB, NS, D), cv[:, :1], hl[:, :1], pc[SEQ:PAT][None, None],
            cv[:, 1:], hl[:, 1:], pool_s)
```

```python
import numpy as np
import concourse.bass as bass
from concourse import mybir
from contextlib import ExitStack, contextmanager

F = mybir.dt.float32
FR = mybir.dt.float32r
I32 = mybir.dt.int32
U32 = mybir.dt.uint32
ALU = mybir.AluOpType
ACT = mybir.ActivationFunctionType
AX = mybir.AxisListType

P = 128
D = 2048
DC = D // P
SEQ = 256
NB, NS = 8, 4
T = SEQ + NB * NS
NC = 1 + NB
LC = 8
CW = 4
HIST = 15
WINDOWS = (2, 4, 8, 16)
HEADS, TOPK = 8, 16
EPS = 1e-6
CS = CW - 1 + NS
CAT = CW - 1 + SEQ
CL = CAT + NB * CS
XL = CL - (CW - 1)
PS = HIST + NS
PAT = HIST + SEQ
PL = PAT + NB * PS
PAIRS = [(a, TOPK // (a + 1)) for a in range(8)]
NCAND = sum(n for _, n in PAIRS) + 8
TT = 3
TP = TT * P

RAW, SPL = 4, 2
NZ = 24
ORDER = [("ada", m, k) for m in range(2) for k in range(DC)]
_ada = [("ada", m, k) for m in range(2, 5) for k in range(DC)]
ORDER += _ada[:4]
_a = 4
for _b in range(8):
    _n = 3 if _b < 4 else 4
    _zs, _as = [("z", 3 * _b + _j) for _j in range(3)], _ada[_a:_a + _n]
    _a += _n
    ORDER += _zs + _as if _b < 7 else _as + _zs
ORDER += _ada[_a:]
O0 = len(ORDER)
Q0 = O0 + DC
M0 = Q0 + 2 * DC
ZP = NZ + 2 * DC
EG = 8
NG = P // EG
EARLY = (2, 3, 0, 1)
NE = len(EARLY) * EG
ND = NE - 5
V0 = M0 + NE
B0 = V0 + 3 * EG
NU = V0 + 2 * P - NE
P0, P1 = M0 + 1, M0 + ND
SCORES_AT = (None, 0, 9)
ROWS_AT = (None, 6, 15)
LISTS_AT = (6, 15, 22)
EXPS_AT = (9, 18, 26)
TURN_AT = (12, 21, ND - 1)
GATED = (0, 3, 4, 4, 4)
TCH = 16
NCH = T // TCH


_z = [ORDER.index(("z", n)) for n in range(NZ)]
POOL_AT = [_z[16] + 1 + (c + 1) // 2 for c in range(8)]
LRUW_AT = POOL_AT[7] + 1
CONV_AT = [_z[16] - 1 + c for c in range(8)]
LRU_AT = [LRUW_AT + 2 + (5 * c) // 4 for c in range(8)]
TAIL_AT = _z[23] + 1
NQ = 4
T1, T2, T3 = NQ, NQ + 2, 2 * NQ + 2
L1, L2, L3 = NQ, NQ + 1, 2 * NQ + 1


def u_unit(g):
    return M0 + EARLY.index(g) * EG if g in EARLY else B0 + 2 * EG * (g - 4)


def v_unit(g):
    return V0 + EG * g if g < 3 else B0 + EG + 2 * EG * (g - 3) if g < NG - 1 else NU - EG


def lows(u):
    return u + 1 - (P1 - P0 if u >= P1 else 0)


VCOLS = [("b_ada", 96), ("norm1", DC), ("norm2", DC), ("final", DC), ("gn_lru", LC), ("gn_pool", LC),
         ("conv_w", CW * LC), ("conv_b", LC), ("ba", LC), ("bx", LC), ("lam", LC), ("pool_b", LC),
         ("pool_s", LC), ("cinv", 4 * HIST), ("h0", LC * NB)]
VOFF, _o = {}, 0
for _n, _w in VCOLS:
    VOFF[_n] = (_o, _w)
    _o += _w
NV = _o
NHIST = LC * NB * (CW - 1) + LC * NB * HIST


class Chain:

    def __init__(self, eng, sem):
        self.eng, self.sem, self.n, self.base = eng, sem, 0, None

    def done(self, ins):
        ins.then_inc(self.sem, 1)
        self.n += 1

    def wait(self):
        self.eng.wait_ge(self.sem, self.n if self.base is None else self.base + (self.n - self.start))

    def link(self, ins):
        self.done(ins)
        self.wait()

    @contextmanager
    def loop(self, first, end, per):
        count = end - first
        with self.eng.Fori(first, end) as i:
            self.start = self.n
            self.base = i * per + (self.n - first * per)
            yield i
            assert self.n - self.start == per, (self.n - self.start, per)
        self.n = self.start + count * per
        self.base = None


def at_least(eng, sem, value):
    if not isinstance(value, int) or value > 0:
        eng.wait_ge(sem, value)


def rounds(eng, n, body):
    body(0)
    with eng.Fori(1, n) as i:
        body(i)


def hybrid_step(nc, w_stream, vecs_d, c_d, hist_d, x_d, lruw_d, poolw_d, keys_d,
                o_y, o_conv, o_lru, o_pool):
    ctx = ExitStack()
    with ctx:
        def sb(name, shape, dt=F, scope=None):
            return (scope or ctx).enter_context(nc.sbuf_tensor(name, shape, dt))

        def sem(name):
            return ctx.enter_context(nc.semaphore(name))

        raw = sb("raw", [P, RAW, 2048])
        w_hi = sb("w_hi", [P, SPL, 2048], FR)
        w_lo = sb("w_lo", [P, SPL, 2048], FR)
        act_hi = sb("act_hi", [P, DC, T], FR)
        act_lo = sb("act_lo", [P, DC, T], FR)
        x = sb("x", [P, DC, T])
        vecs = sb("vecs", [P, NV])
        mod = sb("mod", [P, 6, DC, NC])
        scale1 = sb("scale1", [P, DC, NC])
        scale2 = sb("scale2", [P, DC, NC])
        ones = sb("ones", [P, P])
        ident = sb("ident", [P, P])
        iota = sb("iota", [P, P])
        epsc = sb("epsc", [P, 1])
        rstd = sb("rstd", [P, 2, T])
        soft = sb("soft", [P, 6, LC])
        fix = sb("fix", [P, 2, HIST])
        o_cv = sb("o_cv", [P, LC, NC, CW - 1])
        o_hl = sb("o_hl", [P, LC, NC])
        csplit = sb("csplit", [P, (DC - 1) * 2 * NC + P], FR)
        cpart = csplit[:, 0:DC * 2 * NC].rearrange("p (k n) -> p k n", n=2 * NC)

        early = ExitStack()
        MIXN = 18700 + 1024
        mix = sb("mix", [P, MIXN], F, early)
        early.close()
        gates_in = sb("gates_in", [P, 2, NCH, EG, TCH])
        gw_hi = sb("gw_hi", [P, 2, EG, T], FR)
        gw_lo = sb("gw_lo", [P, 2, EG, T], FR)
        gel = sb("gel", [P, 2, T])
        prod = sb("prod", [P, 2, T])
        acc = sb("acc", [P, DC, T])
        ROUTEN = (2 * T * EG + 2 * 2 * EG * T + 4 * T)
        gates_dram = nc.dram_tensor("gates_dense", (NCH, P, P, TCH), F, kind="Internal").ap()

        ps = ctx.enter_context(nc.psum_tensor("ps", [P, 4096], F))

        def bank(b, n=512, at=0):
            return ps[:, b * 512 + at:b * 512 + at + n]

        def vec(name):
            o, w = VOFF[name]
            return vecs[:, o:o + w]

        at = [0]

        def carve(n):
            at[0] += n
            assert at[0] <= MIXN
            return at[0] - n

        pcat_o, ucat_o, gate_o, xc_o = carve(LC * PL), carve(LC * CL), carve(LC * T), carve(2538)
        ra_o, ii_o, wts_o = carve(LC * CL), carve(LC * PL), carve(2048)

        def view(o, *dims):
            n = int(np.prod(dims))
            v = mix[:, o:o + n]
            if len(dims) == 2:
                return v.rearrange("p (a b) -> p a b", b=dims[1])
            if len(dims) == 3:
                return v.rearrange("p (a b c) -> p a b c", b=dims[1], c=dims[2])
            return v

        pcat, ucat = view(pcat_o, LC, PL), view(ucat_o, LC, CL)
        gate, hist = view(gate_o, LC, T), view(gate_o, NHIST)
        xc_f, sB = view(xc_o, LC, CL), view(xc_o, 6, PL)
        ra_f, dd = view(ra_o, LC, CL), view(ra_o, LC, T)
        ii_f, sA = view(ii_o, LC, CL), view(ii_o, LC, PL)
        xc, ra, ii = xc_f[:, :, 0:XL], ra_f[:, :, 0:XL], ii_f[:, :, 0:XL]
        poolw = view(wts_o, 4, 2, 2 * P)
        lruw = view(wts_o, 2, LC, P)
        tanhs = ucat[:, :, 0:XL]
        y_pool, y_lru = view(pcat_o, LC, T), view(ucat_o, LC, T)
        ysq = view(ra_o, 2 * LC, T)
        work1 = view(xc_o, DC, T)
        work2 = view(pcat_o, DC, T)
        modrow_o = carve(1024)
        modrow = [mix[0:2 * NC, modrow_o + 512 * b:modrow_o + 512 * (b + 1)] for b in range(2)]
        hist_conv = view(gate_o, LC, NB, CW - 1)
        hist_pool = view(gate_o + LC * NB * (CW - 1), LC, NB, HIST)
        at[0] = 0
        qT = view(carve(DC * T), DC, T)
        keysT = view(carve(2048), DC, P)
        sc = view(carve(2048), DC, P)
        sc2 = view(carve(2 * P), 2, P)
        eq = view(carve(2 * TOPK * NCAND), 2, TOPK, NCAND)
        topv = view(carve(2 * HEADS * TOPK), HEADS, 2, TOPK)
        topi = view(carve(2 * HEADS * TOPK), HEADS, 2, TOPK)
        topf = view(carve(2 * HEADS * TOPK), HEADS, 2, TOPK)
        cand = view(carve(HEADS * NCAND), HEADS, NCAND)
        cidx = view(carve(HEADS * NCAND), HEADS, NCAND)
        cand2 = view(carve(2 * NCAND), 2, NCAND)
        best = view(carve(P), HEADS, TOPK)
        bpos = view(carve(P), HEADS, TOPK)
        bposf = view(carve(P), HEADS, TOPK)
        eidx = view(carve(P), HEADS, TOPK)
        eint = view(carve(P), P)
        eint2 = view(carve(P), P)
        sel = view(carve(3 * P), 3, P)
        gsum = view(carve(HEADS), HEADS)
        idT = view(carve(3 * T), 3, T)
        assert at[0] <= ROUTEN
        idT_end = at[0]
        at[0] = 0
        stage = view(carve(2 * P * TCH), 2, P, TCH)
        one1 = view(carve(4 * 8 * P), 4, 8, P)
        one2 = view(carve(4 * 8 * P), 4, 8, P)
        assert at[0] <= idT_end - 3 * T
        gelq = acc
        gelu_dram = nc.dram_tensor("gelus", (2, P, EG, T), F, kind="Internal").ap()

        raw_in = [sem(f"raw_in{i}") for i in range(RAW)]
        hi_ready, lo_ready = sem("hi_ready"), sem("lo_ready")
        pe_hi = sem("pe_hi")
        pe_unit = sem("pe_unit")
        in_vecs, in_c, in_hist, in_x, in_lruw, in_poolw, in_keys = (
            sem(n) for n in ("in_vecs", "in_c", "in_hist", "in_x", "in_lruw", "in_poolw", "in_keys"))
        consts = sem("consts")
        csil_ready, chi_ready, clo_ready = sem("csil_ready"), sem("chi_ready"), sem("clo_ready")
        sq_ready, stat_ready, std_ready, rstd_ready = sem("sq_ready"), sem("stat_ready"), sem("std_ready"), sem("rstd_ready")
        normed_ready = sem("normed_ready")
        row_ready = sem("row_ready")
        lo_pool = sem("lo_pool")
        modT_done, mod_ready = sem("modT_done"), sem("mod_ready")
        bank_free = [sem("bank0_free"), sem("bank1_free")]
        t_ready, ahi_ready, alo_ready = sem("t_ready"), sem("ahi_ready"), sem("alo_ready")
        hist_ready = sem("hist_ready")
        gate_ready = sem("gate_ready")
        states_saved, pool_saved = sem("states_saved"), sem("pool_saved")
        d_ready, pool_mm, ypool_ready = sem("d_ready"), sem("pool_mm"), sem("ypool_ready")
        conv_ready, lru_mm, sig_ready, loga_ready = sem("conv_ready"), sem("lru_mm"), sem("sig_ready"), sem("loga_ready")
        tanh_ready, a_ready, var_ready, mult_ready = sem("tanh_ready"), sem("a_ready"), sem("var_ready"), sem("mult_ready")
        soft_a, soft_b, soft_c = sem("soft_a"), sem("soft_b"), sem("soft_c")
        scan_ready, hl_saved = sem("scan_ready"), sem("hl_saved")
        score_mm, score_copied = sem("score_mm"), sem("score_copied")
        lists_ready, cidx_ready, cidx_used = sem("lists_ready"), sem("cidx_ready"), sem("cidx_used")
        dif_ready, exp_ready = sem("dif_ready"), sem("exp_ready")
        sel_ready, selT_done, idT_ready = sem("sel_ready"), sem("selT_done"), sem("idT_ready")
        onehots_ready, gcopied = sem("onehots_ready"), sem("gcopied")
        pairs_ready = sem("pairs_ready")
        gmm = [[sem(f"gmm{h}{q}") for q in range(2)] for h in range(4)]
        stage_out = [sem("stage_out0"), sem("stage_out1")]
        gate_in = [sem("gate_in0"), sem("gate_in1")]
        gelu_out, gelu_in = [sem("gelu_out0"), sem("gelu_out1")], [sem("gelu_in0"), sem("gelu_in1")]
        prod_done, gwhi_ready, gw_ready = sem("prod_done"), sem("gwhi_ready"), sem("gw_ready")
        vhalf_done = sem("vhalf_done")
        vbank_free = [sem(f"vbank{b}_free") for b in range(4)]
        x2_ready, out_ready = sem("x2_ready"), sem("out_ready")
        out_sem = sem("out_sem")
        dve_steps, act_steps, pool_steps = sem("dve_steps"), sem("act_steps"), sem("pool_steps")

        def by_seq(t, start, step):
            return t[:, :, start:start + NB * step].rearrange("p c (b k) -> p c b k", k=step)

        def wait_evacuated(eng, n):
            eng.wait_ge(bank_free[0], n // 2)
            eng.wait_ge(bank_free[1], n // 2)

        block = ctx.enter_context(nc.Block())

        @block.sync
        def _(sp):
            for u in range(RAW):
                sp.dma_start(raw[:, u, :], w_stream[u]).then_inc(raw_in[u], 16)
            for u in range(RAW, V0 + RAW):
                if P0 <= u - RAW < P1:
                    sp.wait_ge(lo_pool, u - RAW - P0 + 1)
                else:
                    sp.wait_ge(lo_ready, lows(u - RAW))
                sp.dma_start(raw[:, u % RAW, :], w_stream[u]).then_inc(raw_in[u % RAW], 16)
            u0 = V0
            with sp.Fori(0, (NU - u0) // RAW - 1) as i:
                for k in range(RAW):
                    sp.wait_ge(lo_ready, i * RAW + lows(u0 + k))
                    sp.dma_start(raw[:, k, :], w_stream[i * RAW + (u0 + RAW + k)]).then_inc(raw_in[k], 16)
            sp.wait_ge(states_saved, 2)
            sp.dma_start(o_conv, o_cv[:, :, :, :]).then_inc(out_sem, 16)
            sp.wait_ge(hl_saved, 2)
            sp.dma_start(o_lru, o_hl[:, :, :]).then_inc(out_sem, 16)
            for q in range(NQ):
                c = slice(q * DC // NQ, (q + 1) * DC // NQ)
                sp.wait_ge(out_ready, q + 1)
                sp.dma_start(o_y[:, c], acc[:, c, :]).then_inc(out_sem, 16)
            sp.wait_ge(out_sem, 16 * (2 + NQ))
            sp.wait_ge(pool_saved, 16)

        @block.gpsimd
        def _(pool):
            ch = Chain(pool, pool_steps)
            nc.gpsimd.memset(csplit[:, :].bitcast(F), 0.0).then_inc(consts, 1)
            nc.gpsimd.memset(ones[:, :], 1.0).then_inc(consts, 1)
            nc.gpsimd.memset(epsc[:, :], EPS).then_inc(consts, 1)
            nc.gpsimd.iota(iota[:, :], pattern=[[1, P]], base=0, channel_multiplier=0,
                           allow_small_or_imprecise_dtypes=True).then_inc(consts, 1)
            ch.link(nc.gpsimd.memset(ident[:, :], 0.0))
            nc.gpsimd.affine_select(out=ident[:, :], in_=ident[:, :], compare_op=ALU.not_equal, fill=1.0,
                                    base=0, pattern=[[-1, P]], channel_multiplier=1).then_inc(consts, 1)
            pool.wait_ge(in_x, 16)
            ch.link(nc.gpsimd.tensor_tensor(rstd[:, 1, :], x[:, 0, :], x[:, 0, :], ALU.mult))
            for c in range(1, DC):
                ch.link(nc.gpsimd.tensor_tensor(work1[:, c, :], x[:, c, :], x[:, c, :], ALU.mult))
                n = nc.gpsimd.tensor_tensor(rstd[:, 1, :], rstd[:, 1, :], work1[:, c, :], ALU.add)
                if c < DC - 1:
                    ch.link(n)
            n.then_inc(sq_ready, 1)
            pool.wait_ge(rstd_ready, 1)
            nc.gpsimd.tensor_tensor(work2, x[:, :, :], rstd[:, 0, :].unsqueeze(1).to_broadcast([P, DC, T]),
                                    ALU.mult).then_inc(normed_ready, 1)
            pool.wait_ge(in_hist, 16)
            pool.wait_ge(alo_ready, L1)
            nc.gpsimd.memset(ucat[:, :, 0:CW - 1], 0.0).then_inc(hist_ready, 1)
            nc.gpsimd.memset(pcat[:, :, 0:HIST], 0.0).then_inc(hist_ready, 1)
            for c in range(LC):
                nc.gpsimd.tensor_copy(ucat[:, c, CAT:CL].rearrange("p (b k) -> p b k", k=CS)[:, :, 0:CW - 1],
                                      hist_conv[:, c]).then_inc(hist_ready, 1)
                nc.gpsimd.tensor_copy(pcat[:, c, PAT:PL].rearrange("p (b k) -> p b k", k=PS)[:, :, 0:HIST],
                                      hist_pool[:, c]).then_inc(hist_ready, 1)
            wait_evacuated(pool, 16)
            pool.wait_ge(hist_ready, 2 + 2 * LC)
            pool.dma_start(o_pool, pcat).then_inc(pool_saved, 16)
            nc.gpsimd.tensor_copy(o_cv[:, :, 0, :], ucat[:, :, SEQ:SEQ + CW - 1]).then_inc(states_saved, 1)
            nc.gpsimd.tensor_copy(o_cv[:, :, 1:, :], by_seq(ucat, CAT, CS)[:, :, :, NS:]).then_inc(states_saved, 1)
            pool.wait_ge(scan_ready, LC)
            nc.gpsimd.tensor_copy(o_hl[:, :, 0], xc[:, :, SEQ - 1]).then_inc(hl_saved, 1)
            nc.gpsimd.tensor_copy(o_hl[:, :, 1:], by_seq(xc_f, CAT, CS)[:, :, :, NS - 1]).then_inc(hl_saved, 1)
            def pair_indices(i):
                r = P if i < TT - 1 else T - (TT - 1) * P
                pool.wait_ge(lists_ready, i * 2 + 2)
                at_least(pool, cidx_used, i)
                for a, n in PAIRS:
                    o = sum(m for b, m in PAIRS if b < a)
                    nc.gpsimd.tensor_tensor(cidx[0:r, :, o:o + n], topf[0:r, :, 0, a:a + 1].to_broadcast([r, HEADS, n]),
                                            topf[0:r, :, 1, 0:n], ALU.add).then_inc(cidx_ready, 1)
                nc.gpsimd.tensor_tensor(cidx[0:r, :, NCAND - 8:], topf[0:r, :, 0, 8:TOPK],
                                        topf[0:r, :, 1, 0:1].to_broadcast([r, HEADS, 8]), ALU.add).then_inc(cidx_ready, 1)

            def lo_units(first, end):
                for u in range(first, end):
                    s = u % RAW
                    pool.wait_ge(hi_ready, u + 1)
                    pool.wait_ge(pe_unit, u - SPL + 1)
                    nc.gpsimd.tensor_tensor(w_lo[:, s % SPL, :], raw[:, s, :], w_hi[:, s % SPL, :].bitcast(F),
                                            ALU.subtract).then_inc(lo_pool, 1)

            lo_units(P0, M0 + LISTS_AT[0])
            pair_indices(0)
            lo_units(M0 + LISTS_AT[0], M0 + LISTS_AT[1])
            pair_indices(1)
            lo_units(M0 + LISTS_AT[1], M0 + LISTS_AT[2])
            pair_indices(2)
            lo_units(M0 + LISTS_AT[2], P1)

            def times_gates(i):
                for h in range(4):
                    pool.wait_ge(pairs_ready, i * 4 + (h + 1))
                    g = idT[:, 2, bass.ds(i * 32 + 8 * h, 8)].unsqueeze(2).to_broadcast([P, 8, P])
                    nc.gpsimd.tensor_tensor(one2[:, h], one2[:, h], g, ALU.mult).then_inc(onehots_ready, 1)

            with pool.Fori(0, T // 32) as i:
                times_gates(i)

        @block.scalar
        def _(act):
            ch = Chain(act, act_steps)
            act.dma_start(c_ap := view(gate_o + NHIST, DC, NC), c_d).then_inc(in_c, 16)
            act.dma_start(vecs[:, :], vecs_d).then_inc(in_vecs, 16)
            act.dma_start(x[:, :, :], x_d).then_inc(in_x, 16)

            def low_made(u, i=0, per=0):
                if P0 <= u < P1 and isinstance(i, int):
                    act.wait_ge(lo_pool, u - P0 + 1)
                else:
                    act.wait_ge(lo_ready, i * per + lows(u))

            def hi(u):
                s = u % RAW
                act.wait_ge(raw_in[s], 16 * (u // RAW + 1))
                if u >= SPL:
                    act.wait_ge(pe_hi, u - SPL + 1)
                    low_made(u - SPL)
                nc.scalar.activation(w_hi[:, s % SPL, :], raw[:, s, :], ACT.Copy).then_inc(hi_ready, 1)

            def hi_at(u, slot, u4):
                act.wait_ge(raw_in[slot], u4 * 16 + 16)
                act.wait_ge(pe_hi, u + (1 - SPL))
                nc.scalar.activation(w_hi[:, slot % SPL, :], raw[:, slot, :], ACT.Copy).then_inc(hi_ready, 1)

            def hi_next(u0, i, per, k):
                n = u0 + k + 1
                low_made(n - SPL, i, per)
                hi_at(i * per + n, n % RAW, i * (per // RAW) + n // RAW)

            def stats(n, out, width, bank_no):
                act.wait_ge(stat_ready, n)
                nc.scalar.activation(out, bank(bank_no, T), ACT.Sqrt, bias=epsc[:, :], scale=1.0 / width).then_inc(std_ready, 1)

            hi(0)
            act.wait_ge(in_c, 16)
            csil = view(gate_o + NHIST + DC * NC, DC, NC)
            nc.scalar.activation(csil, c_ap, ACT.Silu).then_inc(csil_ready, 1)
            act.wait_ge(csil_ready, 1)
            act.wait_ge(consts, 5)
            nc.scalar.activation(cpart[:, :, 0:NC], csil, ACT.Copy).then_inc(chi_ready, 1)
            def rows(part, base, bs):
                for b in bs:
                    at_least(act, modT_done, 4 * part + b - 1)
                    nc.scalar.activation(modrow[b % 2], bank(base + b)[0:2 * NC, :], ACT.Copy).then_inc(row_ready, 1)

            def high_quarters(before, between=lambda q: None):
                for q in range(NQ):
                    c = slice(q * DC // NQ, (q + 1) * DC // NQ)
                    act.wait_ge(t_ready, before + q + 1)
                    nc.scalar.activation(act_hi[:, c, :], work2[:, c, :], ACT.Copy).then_inc(ahi_ready, 1)
                    between(q)

            for u in range(2 * DC):
                hi(u + 1)
                if u == 24:
                    act.dma_start(hist, hist_d).then_inc(in_hist, 16)
                if u == 11:
                    stats(1, rstd[:, 0, :], D, 2)
                if u == DC - 1:
                    act.wait_ge(pe_unit, u + 1)
                    rows(0, 4, (0, 1))
                if u == DC:
                    rows(0, 4, (2, 3))
                if u == 2 * DC - 1:
                    act.wait_ge(pe_unit, u + 1)
                    rows(1, 0, range(4))
            hi(2 * DC + 1)
            high_quarters(0, lambda q: hi(2 * DC + 2) if q == 1 else None)
            act.wait_ge(in_vecs, 16)
            ch.link(nc.scalar.activation(soft[:, 0, :], vec("lam"), ACT.Abs))
            ch.link(nc.scalar.activation(soft[:, 1, :], soft[:, 0, :], ACT.Exp, scale=-1.0))
            nc.scalar.activation(soft[:, 2, :], soft[:, 1, :], ACT.Ln, bias=1.0).then_inc(soft_a, 1)

            def lru_weights():
                act.wait_ge(pool_mm, LC)
                act.dma_start(lruw, lruw_d).then_inc(in_lruw, 16)

            def lru_gate(c):
                act.wait_ge(lru_mm, c + 1)
                nc.scalar.activation(ra[:, c, :], bank(2, XL), ACT.Sigmoid, bias=vec("ba")[:, c:c + 1]).then_inc(act_steps, 1)
                nc.scalar.activation(ii[:, c, :], bank(3, XL), ACT.Sigmoid, bias=vec("bx")[:, c:c + 1]).then_inc(sig_ready, 1)

            def tanh_exp():
                act.wait_ge(loga_ready, 1)
                act.wait_ge(states_saved, 2)
                nc.scalar.activation(tanhs, ra, ACT.Tanh, scale=-1.0).then_inc(tanh_ready, 1)
                act.wait_ge(tanh_ready, 1)
                nc.scalar.activation(ra, ra, ACT.Exp).then_inc(a_ready, 1)

            def gate_gelu():
                wait_evacuated(act, NZ)
                nc.scalar.activation(gate, gate, ACT.Gelu_apprx_tanh).then_inc(gate_ready, 1)

            def multiplier():
                act.wait_ge(var_ready, 1)
                nc.scalar.activation(xc, xc, ACT.Sqrt).then_inc(mult_ready, 1)

            def group_squares(n, y):
                act.wait_ge(ypool_ready, LC + (n == 0))
                nc.scalar.activation(ysq[:, n * LC:(n + 1) * LC, :], y, ACT.Square).then_inc(sq_ready, 1)

            def group_high(n, y):
                act.wait_ge(t_ready, T1 + n + 1)
                nc.scalar.activation(act_hi[:, n * LC:(n + 1) * LC, :], y, ACT.Copy).then_inc(ahi_ready, 1)

            extra = {}

            def at_unit(u, f):
                extra[u] = extra.get(u, []) + [f]

            at_unit(LRUW_AT, lru_weights)
            for c in range(LC):
                at_unit(LRU_AT[c], lambda c=c: lru_gate(c))
            at_unit(TAIL_AT, tanh_exp)
            at_unit(TAIL_AT + 1, multiplier)
            at_unit(TAIL_AT + 2, gate_gelu)
            at_unit(TAIL_AT + 6, lambda: group_squares(0, y_lru))
            at_unit(TAIL_AT + 7, lambda: group_squares(1, y_pool))
            at_unit(TAIL_AT + 9, lambda: stats(2, rstd[:, 0, :], D // 2, 2))
            at_unit(TAIL_AT + 9, lambda: stats(3, rstd[:, 1, :], D // 2, 3))
            at_unit(TAIL_AT + 11, lambda: group_high(0, y_lru))
            at_unit(TAIL_AT + 12, lambda: group_high(1, y_pool))
            for u in range(2 * DC, O0):
                if u > 2 * DC + 1:
                    hi(u + 1)
                if u == _z[7]:
                    act.dma_start(poolw, poolw_d).then_inc(in_poolw, 16)
                kind = ORDER[u - 1]
                if kind[0] == "z" and kind[1] >= 16:
                    n = kind[1]
                    act.wait_ge(pe_unit, u)
                    if n == 16:
                        act.wait_ge(hist_ready, 2 + 2 * LC)
                    nc.scalar.activation(gate[:, n - 16, :], bank(n % 2, T), ACT.Copy).then_inc(bank_free[n % 2], 1)
                for back, bs in ((0, (0, 1)), (1, (2, 3))):
                    k = ORDER[u - back]
                    if k[0] == "ada" and k[2] == DC - 1 and u - back >= 2 * DC and u < O0 - 1:
                        act.wait_ge(pe_unit, u - back + 1)
                        rows(k[1], 4, bs)
                for f in extra.get(u, []):
                    f()
            act.wait_ge(pe_unit, O0)
            rows(4, 4, range(4))
            with act.Fori(0, DC // 4) as i:
                for k in range(4):
                    hi_next(O0, i, 4, k)
            stats(4, rstd[:, 0, :], D, 2)
            high_quarters(T2)
            act.wait_ge(alo_ready, L3)
            act.dma_start(keysT, keys_d).then_inc(in_keys, 16)
            with act.Fori(0, 2 * DC // 4) as i:
                for k in range(4):
                    hi_next(Q0, i, 4, k)
            act.wait_ge(pe_unit, M0)
            rows(5, 4, range(4))

            def score_rows(i):
                r = P if i < TT - 1 else T - (TT - 1) * P
                act.wait_ge(score_mm, i + 1)
                at_least(act, lists_ready, i * 2)
                for b in range(4):
                    n = nc.scalar.activation(sc[0:r, 4 * b:4 * b + 4, :], bank(4 + b)[0:r, :].rearrange("p (a n) -> p a n", n=P),
                                             ACT.Copy)
                n.then_inc(score_copied, 1)

            def exps(i):
                r = P if i < TT - 1 else T - (TT - 1) * P
                act.wait_ge(dif_ready, i + 1)
                nc.scalar.activation(best[0:r], best[0:r], ACT.Exp).then_inc(exp_ready, 1)

            def early_gelu(n):
                nc.scalar.activation(gelq[:, n % (2 * EG), :], bank(n % 2, T), ACT.Gelu_apprx_tanh).then_inc(bank_free[n % 2], 1)

            def early_tile(n):
                g, k = EARLY[n // EG], n % EG
                hi(M0 + n + 1)
                act.wait_ge(pe_unit, M0 + n + 1)
                if n >= 2 * EG and k == 0:
                    act.wait_ge(gelu_out[n // EG % 2], 16)
                early_gelu(n)
                if g >= 2 and k == EG - 1:
                    wait_evacuated(act, ZP + n + 1)
                    h = n // EG
                    act.dma_start(gelu_dram[g - 2], gelq[:, h * EG:(h + 1) * EG, :]).then_inc(gelu_out[h], 16)

            score_rows(0)
            for n in range(ND):
                early_tile(n)
                for i in range(TT):
                    if n == ROWS_AT[i]:
                        score_rows(i)
                    if n == EXPS_AT[i]:
                        exps(i)

            def gate_chunks(i):
                for c in range(2):
                    at_least(act, stage_out[c], i * 16)
                    for h in range(2):
                        for q in range(2):
                            act.wait_ge(gmm[2 * c + h][q], i + 1)
                            t0 = 8 * h + 4 * q
                            nc.scalar.activation(stage[:, c, :, t0:t0 + 4].rearrange("p n t -> p t n"),
                                                 bank(4 + 2 * h + q).rearrange("p (t n) -> p t n", n=P),
                                                 ACT.Copy).then_inc(gcopied, 1)
                    act.wait_ge(gcopied, i * 8 + (4 * c + 4))
                    act.dma_start(gates_dram[i * 2 + c], stage[:, c, :, :]).then_inc(stage_out[c], 16)

            rounds(act, NCH // 2, gate_chunks)

            def load_gates(g, par):
                act.dma_start(gates_in[:, par], gates_dram.rearrange("c p (g k) t -> g p c (k t)", k=EG)[g]
                              ).then_inc(gate_in[par], 16)

            for c in range(2):
                act.wait_ge(stage_out[c], 16 * (NCH // 2))
            load_gates(0, 0)

            def expert_tiles(hi_of, u, tile, par):
                for k in range(EG):
                    hi_of(k)
                    act.wait_ge(pe_unit, u(k) + 1)
                    nc.scalar.activation(gel[:, k % 2, :], bank(k % 2, T), ACT.Gelu_apprx_tanh).then_inc(bank_free[k % 2], 1)
                    act.wait_ge(prod_done, tile(k) + 1)
                    nc.scalar.activation(gw_hi[:, par, k, :], prod[:, k % 2, :], ACT.Copy).then_inc(gwhi_ready, 1)

            load_gates(1, 1)

            def gated(tile):
                act.wait_ge(prod_done, tile + 1)
                nc.scalar.activation(gw_hi[:, tile // EG % 2, tile % EG, :], prod[:, tile % 2, :], ACT.Copy).then_inc(gwhi_ready, 1)

            t = 0
            for n, count in enumerate(GATED):
                hi(M0 + ND + n + 1)
                for _ in range(count):
                    gated(t)
                    t += 1
                act.wait_ge(pe_unit, M0 + ND + n + 1)
                early_gelu(ND + n)
            gated(t)
            load_gates(2, 0)
            load_gates(3, 1)

            def load_gelu(tile):
                act.wait_ge(prod_done, tile - 1)
                act.dma_start(gel[:, tile % 2, :], gelu_dram[tile // EG - 2, :, tile % EG, :]).then_inc(gelu_in[tile % 2], 16)

            for k in range(EG):
                hi(v_unit(0) + k + 1)
            for c in range(2):
                act.wait_ge(gelu_out[c], 16)
            load_gelu(2 * EG)
            load_gelu(2 * EG + 1)
            for g in (1, 2):
                act.wait_ge(pe_unit, v_unit(g))
                for k in range(EG):
                    hi(v_unit(g) + k + 1)
                    tile = (g + 1) * EG + k
                    gated(tile)
                    if tile + 2 < 4 * EG:
                        load_gelu(tile + 2)
            with act.Fori(0, (NG - 4) // 2) as i:
                for j in range(2):
                    g = 4 + j
                    load_gates(i * 2 + g, j)
                    expert_tiles(lambda k: hi_next(u_unit(g), i, 4 * EG, k), lambda k: i * (4 * EG) + (u_unit(g) + k),
                                 lambda k: i * (2 * EG) + (g * EG + k), j)
                    for k in range(EG):
                        hi_next(v_unit(g - 1), i, 4 * EG, k)
            for k in range(EG - 1):
                hi(v_unit(NG - 1) + k + 1)
            stats(5, rstd[:, 0, :], D, 6)

        @block.vector
        def _(dve):
            ch = Chain(dve, dve_steps)
            link = ch.link
            V = nc.vector

            def lo(u):
                s = u % RAW
                dve.wait_ge(hi_ready, u + 1)
                at_least(dve, pe_unit, u - SPL + 1)
                V.tensor_tensor(w_lo[:, s % SPL, :], raw[:, s, :], w_hi[:, s % SPL, :].bitcast(F), ALU.subtract).then_inc(lo_ready, 1)

            def lo_next(u0, i, per, k):
                n = u0 + k + 1
                s = n % RAW
                dve.wait_ge(hi_ready, i * per + (n + 1))
                dve.wait_ge(pe_unit, i * per + (n - SPL + 1))
                V.tensor_tensor(w_lo[:, s % SPL, :], raw[:, s, :], w_hi[:, s % SPL, :].bitcast(F), ALU.subtract).then_inc(lo_ready, 1)

            def modulate_quarters(out, scale, shift, before, lows_before, normed_too, between):
                def quarter(q):
                    c0, n = q * DC // NQ, DC // NQ
                    o = out[:, c0:c0 + n, :]
                    if normed_too:
                        link(V.tensor_tensor(o, x[:, c0:c0 + n, :], rstd[:, 0, :].unsqueeze(1).to_broadcast([P, n, T]), ALU.mult))
                    os = o[:, :, SEQ:T].rearrange("p c (b t) -> p c b t", t=NS)
                    for c in range(c0, c0 + n):
                        ch.done(V.tensor_scalar(out[:, c, 0:SEQ], out[:, c, 0:SEQ], scale[:, c, 0:1], shift[:, c, 0:1],
                                                ALU.mult, ALU.add))
                    link(V.tensor_tensor(os, os, scale[:, c0:c0 + n, 1:].unsqueeze(3).to_broadcast([P, n, NB, NS]), ALU.mult))
                    V.tensor_tensor(os, os, shift[:, c0:c0 + n, 1:].unsqueeze(3).to_broadcast([P, n, NB, NS]), ALU.add).then_inc(t_ready, 1)

                def low(q):
                    c = slice(q * DC // NQ, (q + 1) * DC // NQ)
                    dve.wait_ge(ahi_ready, before + q + 1)
                    dve.wait_ge(t_ready, before + q + 1)
                    V.tensor_tensor(act_lo[:, c, :], out[:, c, :], act_hi[:, c, :].bitcast(F), ALU.subtract).then_inc(alo_ready, 1)

                quarter(0)
                for q in range(1, NQ):
                    quarter(q)
                    low(q - 1)
                    between(q)
                low(NQ - 1)
                dve.wait_ge(alo_ready, lows_before + NQ)

            def inv_std(n, r):
                dve.wait_ge(std_ready, n)
                link(V.reciprocal(r, r))

            lo(0)
            dve.wait_ge(chi_ready, 1)
            csil = view(gate_o + NHIST + DC * NC, DC, NC)
            V.tensor_tensor(cpart[:, :, NC:], csil, cpart[:, :, 0:NC].bitcast(F), ALU.subtract).then_inc(clo_ready, 1)
            dve.wait_ge(in_vecs, 16)
            bias = vec("b_ada").rearrange("p (m c) -> p m c", m=6)

            def mod_part(m, base):
                dve.wait_ge(modT_done, 4 * m + 4)
                mt = bank(base, DC * 2 * NC).rearrange("p (c n) -> p c n", n=2 * NC)
                link(V.tensor_tensor(mod[:, m, :, :], mt[:, :, 0:NC], bias[:, m, :].unsqueeze(2).to_broadcast([P, DC, NC]), ALU.add))
                V.tensor_tensor(mod[:, m, :, :], mod[:, m, :, :], mt[:, :, NC:2 * NC], ALU.add).then_inc(mod_ready, 1)
                if m in (1, 4):
                    dve.wait_ge(mod_ready, m + 1)
                    s, g = (scale1, "norm1") if m == 1 else (scale2, "norm2")
                    link(V.tensor_scalar(s[:, :, :], mod[:, m, :, :], 1.0, None, ALU.add))
                    link(V.tensor_tensor(s[:, :, :], s[:, :, :], vec(g).unsqueeze(2).to_broadcast([P, DC, NC]), ALU.mult))

            for u in range(2 * DC):
                lo(u + 1)
                if u == 12:
                    dve.wait_ge(std_ready, 1)
                    V.reciprocal(rstd[:, 0, :], rstd[:, 0, :]).then_inc(rstd_ready, 1)
                if u == DC + 2:
                    mod_part(0, 4)
            mod_part(1, 0)
            dve.wait_ge(normed_ready, 1)
            modulate_quarters(work2, scale1, mod[:, 0], 0, 0, False, lambda q: lo(2 * DC + q) if q < 3 else None)

            def double(dst, src, d0, s0, n, by, fr):
                link(V.tensor_tensor(dst[:, d0:d0 + n, fr:PL], src[:, s0:s0 + n, fr:PL], src[:, s0:s0 + n, fr - by:PL - by], ALU.add))

            def pooled(g, s, c0):
                win = WINDOWS[g]
                p = pcat[:, 2 * g:2 * g + 2, :]
                d = dd[:, 2 * g:2 * g + 2, :]
                s = s[:, c0:c0 + 2, :]
                link(V.scalar_tensor_tensor(out=d[:, :, 0:SEQ], in0=s[:, :, HIST:PAT], scalar=1.0 / win,
                                            in1=p[:, :, HIST:PAT], op0=ALU.mult, op1=ALU.subtract))
                ci = vec("cinv")[:, g * HIST:(g + 1) * HIST].unsqueeze(1).to_broadcast([P, 2, HIST])
                link(V.tensor_tensor(fix[:, :, :], s[:, :, HIST:2 * HIST], ci, ALU.mult))
                ch.done(V.tensor_tensor(d[:, :, 0:HIST], fix[:, :, :], p[:, :, HIST:2 * HIST], ALU.subtract))
                for c in range(2):
                    def tail(t):
                        return t[:, c, PAT:PL].rearrange("p (b k) -> p b k", k=PS)[:, :, HIST:]
                    n = V.scalar_tensor_tensor(out=d[:, c, SEQ:T].rearrange("p (b t) -> p b t", t=NS), in0=tail(s),
                                               scalar=1.0 / win, in1=tail(p), op0=ALU.mult, op1=ALU.subtract)
                    if c == 0:
                        ch.done(n)
                n.then_inc(d_ready, 1)
                ch.wait()

            def sums2():
                wait_evacuated(dve, 8)
                dve.wait_ge(hist_ready, 2 + 2 * LC)
                double(sA, pcat, 0, 0, LC, 1, 1)

            def sums8():
                double(sA, sB, 4, 2, 4, 4, 7)
                pooled(2, sA, 4)

            def sums16():
                double(sB, sA, 4, 6, 2, 8, 15)
                pooled(3, sB, 4)

            def softplus8():
                dve.wait_ge(soft_a, 1)
                u = soft[:, 1, :]
                link(V.tensor_scalar(soft[:, 3, :], u, 1.0, 1.0, ALU.add, ALU.subtract))
                link(V.tensor_scalar(soft[:, 4, :], soft[:, 3, :], 0.0, None, ALU.is_equal))
                link(V.tensor_tensor(soft[:, 3, :], soft[:, 3, :], soft[:, 4, :], ALU.add))
                link(V.reciprocal(soft[:, 3, :], soft[:, 3, :]))
                link(V.tensor_tensor(soft[:, 3, :], soft[:, 3, :], soft[:, 2, :], ALU.mult))
                link(V.tensor_tensor(soft[:, 3, :], soft[:, 3, :], soft[:, 4, :], ALU.add))
                link(V.tensor_tensor(soft[:, 3, :], soft[:, 3, :], u, ALU.mult))
                link(V.tensor_scalar(soft[:, 4, :], vec("lam"), -1.0, 0.0, ALU.mult, ALU.max))
                link(V.tensor_tensor(soft[:, 3, :], soft[:, 3, :], soft[:, 4, :], ALU.add))
                link(V.tensor_scalar(soft[:, 5, :], soft[:, 3, :], -8.0, None, ALU.mult))

            cw = vec("conv_w").rearrange("p (k c) -> p k c", k=CW)

            def conv(c):
                dve.wait_ge(d_ready, 4)
                wait_evacuated(dve, 8 + 2 * (c // 2 + 1))
                link(V.tensor_scalar(xc[:, c, :], ucat[:, c, CW - 1:CL], cw[:, CW - 1, c:c + 1], vec("conv_b")[:, c:c + 1],
                                     ALU.mult, ALU.add))
                for k in range(CW - 1):
                    n = V.scalar_tensor_tensor(out=xc[:, c, :], in0=ucat[:, c, k:k + XL], scalar=cw[:, k, c:c + 1],
                                               in1=xc[:, c, :], op0=ALU.mult, op1=ALU.add)
                    if k < CW - 2:
                        link(n)
                n.then_inc(conv_ready, 1)

            def pool_out(c):
                dve.wait_ge(pool_saved, 16)
                dve.wait_ge(pool_mm, c + 1)
                V.tensor_scalar(y_pool[:, c, :], bank(2 + c % 2, T), vec("pool_b")[:, c:c + 1], vec("pool_s")[:, c:c + 1],
                                ALU.add, ALU.mult).then_inc(ypool_ready, 1)

            def log_a(c):
                dve.wait_ge(sig_ready, c + 1)
                ch.done(V.tensor_scalar(ra[:, c, :], ra[:, c, :], soft[:, 5, c:c + 1], None, ALU.mult))
                ch.done(V.tensor_tensor(ii[:, c, :], ii[:, c, :], xc[:, c, :], ALU.mult))

            extra = {}

            def at_unit(u, *fs):
                extra[u] = extra.get(u, []) + list(fs)

            z8 = ORDER.index(("z", 7))
            at_unit(z8 + 2, sums2)
            at_unit(z8 + 4, lambda: pooled(0, sA, 0), lambda: double(sB, sA, 0, 2, 6, 2, 3))
            at_unit(z8 + 7, lambda: pooled(1, sB, 0), sums8)
            at_unit(z8 + 8, sums16)
            at_unit(z8 + 9, softplus8)
            for c in range(LC):
                at_unit(POOL_AT[c] + 1, lambda c=c: pool_out(c))
                at_unit(CONV_AT[c], lambda c=c: conv(c))
                at_unit(LRU_AT[c] + 1, lambda c=c: log_a(c))
            def recurrence_input():
                dve.wait_ge(a_ready, 1)
                link(V.tensor_tensor(xc, ra, ra, ALU.mult))
                V.scalar_tensor_tensor(out=xc, in0=xc, scalar=1.0, in1=tanhs, op0=ALU.add, op1=ALU.mult).then_inc(var_ready, 1)

            def times_multiplier():
                dve.wait_ge(mult_ready, 1)
                link(V.memset(xc[:, :, 0:1], 1.0))
                link(V.tensor_tensor(ii, ii, xc, ALU.mult))
                border = CAT - 1
                ch.done(V.memset(by_seq(ra_f, border, CS)[:, :, :, 0], 0.0))
                link(V.tensor_copy(by_seq(ii_f, border, CS)[:, :, :, 0], vec("h0").rearrange("p (c b) -> p c b", b=NB)))

            def scan(c):
                V.tensor_tensor_scan(xc[:, c, :], ra[:, c, :], ii[:, c, :], 0.0, ALU.mult, ALU.add).then_inc(scan_ready, 1)

            def times_gate():
                dve.wait_ge(scan_ready, LC)
                dve.wait_ge(gate_ready, 1)
                link(V.tensor_tensor(y_lru[:, :, 0:SEQ], xc[:, :, 0:SEQ], gate[:, :, 0:SEQ], ALU.mult))
                V.tensor_tensor(by_seq(y_lru, SEQ, NS), by_seq(xc_f, CAT, CS)[:, :, :, 0:NS], by_seq(gate, SEQ, NS),
                                ALU.mult).then_inc(ypool_ready, 1)

            def group_norm(n_, y, g, r):
                inv_std(n_, rstd[:, r, :])
                for c in range(LC):
                    n = V.scalar_tensor_tensor(out=y[:, c, :], in0=y[:, c, :], scalar=vec(g)[:, c:c + 1],
                                               in1=rstd[:, r, :], op0=ALU.mult, op1=ALU.mult)
                n.then_inc(t_ready, 1)

            def group_lows():
                dve.wait_ge(t_ready, T2)
                dve.wait_ge(ahi_ready, T2)
                link(V.tensor_tensor(act_lo[:, 0:LC, :], y_lru, act_hi[:, 0:LC, :].bitcast(F), ALU.subtract))
                V.tensor_tensor(act_lo[:, LC:, :], y_pool, act_hi[:, LC:, :].bitcast(F), ALU.subtract).then_inc(alo_ready, 1)

            def loga_done():
                V.tensor_copy(soft[:, 0, 0:1], soft[:, 5, 0:1]).then_inc(loga_ready, 1)

            at_unit(LRU_AT[7] + 2, loga_done)
            at_unit(TAIL_AT, recurrence_input)
            at_unit(TAIL_AT + 2, times_multiplier)
            for c in range(LC):
                at_unit(TAIL_AT + 3 + c // 4, lambda c=c: scan(c))
            at_unit(TAIL_AT + 5, times_gate)
            at_unit(TAIL_AT + 10, lambda: group_norm(2, y_lru, "gn_lru", 0))
            at_unit(TAIL_AT + 11, lambda: group_norm(3, y_pool, "gn_pool", 1))
            at_unit(TAIL_AT + 13, group_lows)
            for u in range(2 * DC, O0):
                if u > 2 * DC + 1:
                    lo(u + 1)
                kind = ORDER[u - 1]
                if kind[0] == "z" and kind[1] < 16:
                    n = kind[1]
                    dst, start, step = (pcat, PAT, PS) if n < 8 else (ucat, CAT, CS)
                    dve.wait_ge(pe_unit, u)
                    V.tensor_copy(dst[:, n % 8, step - NS:step - NS + SEQ], bank(n % 2, SEQ))
                    V.tensor_copy(dst[:, n % 8, start:start + NB * step].rearrange("p (b k) -> p b k", k=step)[:, :, step - NS:],
                                  bank(n % 2, NB * NS, SEQ).rearrange("p (b t) -> p b t", t=NS)).then_inc(bank_free[n % 2], 1)
                k = ORDER[u - 3]
                if k[0] == "ada" and k[2] == DC - 1 and u - 3 >= 2 * DC:
                    mod_part(k[1], 4)
                for f in extra.get(u, []):
                    f()
            mod_part(4, 4)
            def residual(c, src, m):
                xs = x[:, c, SEQ:T].rearrange("p (b t) -> p b t", t=NS)
                V.scalar_tensor_tensor(out=x[:, c, 0:SEQ], in0=src[:, 0:SEQ], scalar=mod[:, m, c, 0:1],
                                       in1=x[:, c, 0:SEQ], op0=ALU.mult, op1=ALU.add)
                tmp = rstd[:, 1, 0:NB * NS].rearrange("p (b t) -> p b t", t=NS)
                link(V.tensor_tensor(tmp, src[:, SEQ:T].rearrange("p (b t) -> p b t", t=NS),
                                     mod[:, m, c, 1:].unsqueeze(2).to_broadcast([P, NB, NS]), ALU.mult))
                return V.tensor_tensor(xs, xs, tmp, ALU.add)

            def add_square(c, square):
                link(V.tensor_tensor(square, x[:, c, :], x[:, c, :], ALU.mult))
                link(V.tensor_tensor(rstd[:, 0, :], rstd[:, 0, :], square, ALU.add))

            dve.wait_ge(hl_saved, 2)
            link(V.memset(rstd[:, 0, :], 0.0))
            with ch.loop(0, DC // 4, 12) as i:
                for k in range(4):
                    lo_next(O0, i, 4, k)
                    dve.wait_ge(pe_unit, i * 4 + (O0 + k + 1))
                    residual(i * 4 + k, bank(k % 2, T), 2).then_inc(bank_free[k % 2], 1)
                    dve.wait_ge(bank_free[k % 2], i * 2 + ((NZ + k) // 2 + 1))
                    add_square(i * 4 + k, work1[:, 0, :])
            V.tensor_copy(work1[:, 1, :], rstd[:, 0, :]).then_inc(sq_ready, 1)
            inv_std(4, rstd[:, 0, :])
            modulate_quarters(work2, scale2, mod[:, 3], T2, L2, True, lambda q: None)

            with dve.Fori(0, 2 * DC // 4) as i:
                for k in range(4):
                    lo_next(Q0, i, 4, k)
                    if k % 2:
                        dve.wait_ge(pe_unit, i * 4 + (Q0 + k))
                        V.tensor_copy(qT[:, i * 2 + k // 2, 0:T], bank(k // 2, T)).then_inc(bank_free[k // 2], 1)
            mod_part(5, 2)

            pos50 = iota[:, 0:NCAND]

            def top16(src, tmp, vals, idx):
                link(V.max(vals[:, 0:8], src))
                ch.done(V.max_index(idx[:, 0:8], vals[:, 0:8], src))
                link(V.match_replace(tmp, vals[:, 0:8], src, -3.0e38))
                link(V.max(vals[:, 8:16], tmp))
                ch.done(V.max_index(idx[:, 8:16], vals[:, 8:16], tmp))

            def route(i, between):
                r = P if i < TT - 1 else T - (TT - 1) * P
                dve.wait_ge(score_copied, i + 1)
                at_least(dve, cidx_ready, i * 9)
                for n in range(2 * HEADS):
                    h, p = n // 2, n % 2
                    top16(sc[0:r, n, :], sc2[0:r, n % 2, :], topv[0:r, h, p, :], topi[0:r, h, p, :].bitcast(U32))
                    between(n)
                ch.wait()
                V.tensor_scalar(topf[0:r, :, 0, :], topi[0:r, :, 0, :].bitcast(U32), float(P), None, ALU.mult).then_inc(lists_ready, 1)
                V.tensor_copy(topf[0:r, :, 1, :], topi[0:r, :, 1, :].bitcast(U32)).then_inc(lists_ready, 1)
                o = 0
                for a, n in PAIRS:
                    ch.done(V.tensor_tensor(cand[0:r, :, o:o + n], topv[0:r, :, 0, a:a + 1].to_broadcast([r, HEADS, n]),
                                            topv[0:r, :, 1, 0:n], ALU.add))
                    o += n
                link(V.tensor_tensor(cand[0:r, :, o:], topv[0:r, :, 0, 8:TOPK], topv[0:r, :, 1, 0:1].to_broadcast([r, HEADS, 8]), ALU.add))
                for h in range(HEADS):
                    top16(cand[0:r, h, :], cand2[0:r, h % 2, :], best[0:r, h, :], bpos[0:r, h, :].bitcast(U32))
                ch.wait()
                link(V.tensor_copy(bposf[0:r], bpos[0:r].bitcast(U32)))
                dve.wait_ge(cidx_ready, i * 9 + 9)
                for h in range(0, HEADS, 2):
                    link(V.tensor_tensor(eq[0:r], pos50[0:r].unsqueeze(1).unsqueeze(1).to_broadcast([r, 2, TOPK, NCAND]),
                                         bposf[0:r, h:h + 2, :].unsqueeze(3).to_broadcast([r, 2, TOPK, NCAND]), ALU.is_equal))
                    link(V.tensor_tensor(eq[0:r], eq[0:r], cidx[0:r, h:h + 2, :].unsqueeze(2).to_broadcast([r, 2, TOPK, NCAND]), ALU.mult))
                    link(V.reduce_sum(eidx[0:r, h:h + 2, :], eq[0:r], axis=AX.X))
                link(V.tensor_copy(gsum[0:r], best[0:r, :, 0]))
                V.tensor_tensor(best[0:r], best[0:r], gsum[0:r].unsqueeze(2).to_broadcast([r, HEADS, TOPK]), ALU.subtract).then_inc(dif_ready, 1)
                e1, e2 = eint[0:r].bitcast(I32), eint2[0:r].bitcast(I32)
                link(V.tensor_copy(e1, eidx[0:r].rearrange("p h k -> p (h k)")))
                ch.done(V.tensor_scalar(e2, e1, 7, None, ALU.logical_shift_right))
                link(V.tensor_scalar(e1, e1, P - 1, None, ALU.bitwise_and))
                at_least(dve, selT_done, i)
                V.tensor_copy(sel[0:r, 0, :], e2).then_inc(cidx_used, 1)
                ch.done(V.tensor_copy(sel[0:r, 1, :], e1))

            def gates_of(i):
                r = P if i < TT - 1 else T - (TT - 1) * P
                dve.wait_ge(exp_ready, i + 1)
                link(V.reduce_sum(gsum[0:r], best[0:r], axis=AX.X))
                link(V.reciprocal(gsum[0:r], gsum[0:r]))
                V.tensor_tensor(sel[0:r, 2, :].rearrange("p (h k) -> p h k", k=TOPK), best[0:r],
                                gsum[0:r].unsqueeze(2).to_broadcast([r, HEADS, TOPK]), ALU.mult).then_inc(sel_ready, 1)

            def choice_out(i):
                r = P if i < TT - 1 else T - (TT - 1) * P
                dve.wait_ge(selT_done, i + 1)
                V.tensor_copy(idT[:, :, i * P:i * P + r], bank(2 + i % 2, 3 * r).rearrange("p (j t) -> p j t", j=3)).then_inc(idT_ready, 1)

            def weave(i):
                def between(n):
                    if n == 5:
                        gates_of(i)
                    if n == 14:
                        choice_out(i)
                return between

            route(0, lambda n: None)
            route(1, weave(0))
            route(2, weave(1))
            gates_of(2)
            choice_out(2)
            dve.wait_ge(idT_ready, TT)

            wide = iota[:, :].unsqueeze(1).to_broadcast([P, 8, P])

            def onehots(i):
                for h in range(4):
                    at_least(dve, gmm[h][1], i)

                    def col(j):
                        return idT[:, j, bass.ds(i * 32 + 8 * h, 8)].unsqueeze(2).to_broadcast([P, 8, P])
                    V.tensor_tensor(one1[:, h], wide, col(0), ALU.is_equal)
                    V.tensor_tensor(one2[:, h], wide, col(1), ALU.is_equal).then_inc(pairs_ready, 1)

            rounds(dve, T // 32, onehots)
            lo(M0 + ND)
            for c in range(2):
                dve.wait_ge(stage_out[c], 16 * (NCH // 2))

            def gated(t, gelu):
                dve.wait_ge(gate_in[t // EG % 2], 16 * (t // (2 * EG) + 1))
                if t >= 2:
                    dve.wait_ge(gw_ready, t - 1)
                V.tensor_tensor(prod[:, t % 2, :].rearrange("p (c t) -> p c t", t=TCH),
                                gelu.rearrange("p (c t) -> p c t", t=TCH), gates_in[:, t // EG % 2, :, t % EG, :],
                                ALU.mult).then_inc(prod_done, 1)

            def gated_low(t):
                dve.wait_ge(gwhi_ready, t + 1)
                V.tensor_tensor(gw_lo[:, t // EG % 2, t % EG, :], prod[:, t % 2, :],
                                gw_hi[:, t // EG % 2, t % EG, :].bitcast(F), ALU.subtract).then_inc(gw_ready, 1)

            def with_low(t):
                if t >= 2:
                    gated_low(t - 2)
                for b in range(2):
                    dve.wait_ge(bank_free[b], (ZP + 2 * EG + t + 2 - b) // 2)
                gated(t, gelq[:, t, :])

            t = 0
            for n, count in enumerate(GATED):
                lo(M0 + ND + n + 1)
                for _ in range(count):
                    with_low(t)
                    t += 1
            with_low(t)
            gated_low(t - 1)
            gated_low(t)
            dve.wait_ge(prod_done, 2 * EG)
            for b in range(4):
                V.memset(acc[:, b::4, :], 0.0).then_inc(vbank_free[b], 1)

            def expert_tiles(lo_of, tile, half, par, turn):
                dve.wait_ge(gate_in[par], turn)
                for k in range(EG):
                    lo_of(k)
                    dve.wait_ge(bank_free[k % 2], half + (ZP // 2 + k // 2 + 1))
                    V.tensor_tensor(prod[:, k % 2, :].rearrange("p (c t) -> p c t", t=TCH),
                                    gel[:, k % 2, :].rearrange("p (c t) -> p c t", t=TCH), gates_in[:, par, :, k, :],
                                    ALU.mult).then_inc(prod_done, 1)
                    dve.wait_ge(gwhi_ready, tile + (k + 1))
                    V.tensor_tensor(gw_lo[:, par, k, :], prod[:, k % 2, :], gw_hi[:, par, k, :].bitcast(F),
                                    ALU.subtract).then_inc(gw_ready, 1)

            def add_up(lo_of, unit, units, uses, also=lambda k: None, last=None):
                for b in range(4):
                    dve.wait_ge(vbank_free[b], uses + 1)
                for k in range(EG):
                    lo_of(k)
                    also(k)
                    dve.wait_ge(vhalf_done, units + (k + 1))
                    for h in range(2):
                        c = 2 * k + h
                        if h == 1:
                            dve.wait_ge(pe_unit, unit + (k + 1))
                        V.tensor_tensor(acc[:, c, :], acc[:, c, :], bank(2 + c % 4, T), ALU.add).then_inc(vbank_free[c % 4], 1)
                    if last:
                        last(2 * k)
                        last(2 * k + 1)

            def lo_after(u0, last=NU):
                return lambda k: lo(u0 + k + 1) if u0 + k + 1 < last else None

            def stored(g):
                def tile(k):
                    t = g * EG + k
                    dve.wait_ge(gelu_in[k % 2], 16 * ((t - 2 * EG) // 2 + 1))
                    gated(t, gel[:, k % 2, :])
                    gated_low(t)
                return tile

            add_up(lo_after(v_unit(0)), v_unit(0), 0, 0)
            add_up(lo_after(v_unit(1)), v_unit(1), EG, DC // 4, stored(2))
            add_up(lo_after(v_unit(2)), v_unit(2), 2 * EG, 2 * DC // 4, stored(3))
            with dve.Fori(0, (NG - 4) // 2) as i:
                for j in range(2):
                    g = 4 + j
                    expert_tiles(lambda k: lo_next(u_unit(g), i, 4 * EG, k), i * (2 * EG) + g * EG, i * EG + g * EG // 2,
                                 j, i * 16 + 48)
                    add_up(lambda k: lo_next(v_unit(g - 1), i, 4 * EG, k), i * (4 * EG) + v_unit(g - 1),
                           i * (2 * EG) + (g - 1) * EG, i * (DC // 2) + (g - 1) * DC // 4)
            g = NG - 1

            def finish(c):
                dve.wait_ge(vbank_free[c % 4], 1 + (NG - 1) * DC // 4 + c // 4 + 1)
                link(residual(c, acc[:, c, :], 5))
                add_square(c, prod[:, 0, :])

            dve.wait_ge(gw_ready, NG * EG)
            link(V.memset(rstd[:, 0, :], 0.0))
            add_up(lo_after(v_unit(g)), v_unit(g), g * EG, g * DC // 4, last=finish)
            V.tensor_copy(prod[:, 1, :], rstd[:, 0, :]).then_inc(sq_ready, 1)
            inv_std(5, rstd[:, 0, :])
            for c in range(DC):
                n = V.scalar_tensor_tensor(out=acc[:, c, :], in0=x[:, c, :], scalar=vec("final")[:, c:c + 1],
                                           in1=rstd[:, 0, :], op0=ALU.mult, op1=ALU.mult)
                if c % (DC // NQ) == DC // NQ - 1:
                    n.then_inc(out_ready, 1)

        @block.tensor
        def _(pe):
            mm = nc.tensor.matmul

            def hi_there(u):
                pe.wait_ge(hi_ready, u + 1)

            def lo_there(u, late=False):
                if late:
                    pe.wait_ge(lo_ready, u + (1 - (P1 - P0)))
                elif isinstance(u, int) and P0 <= u < P1:
                    pe.wait_ge(lo_pool, u - P0 + 1)
                else:
                    pe.wait_ge(lo_ready, u + 1)

            def project(u, slot, b, quarters=None, late=False):
                s = slot % SPL
                hi_there(u)
                for c in range(DC):
                    w = slice(c * P, (c + 1) * P)
                    if quarters is not None and c % (DC // NQ) == 0:
                        pe.wait_ge(alo_ready, quarters + c // (DC // NQ) + 1)
                    mm(bank(b, T), w_hi[:, s, w], act_hi[:, c, :], start=c == 0, stop=False)
                    n = mm(bank(b, T), w_hi[:, s, w], act_lo[:, c, :], start=False, stop=False)
                n.then_inc(pe_hi, 1)
                lo_there(u, late)
                for c in range(DC):
                    w = slice(c * P, (c + 1) * P)
                    n = mm(bank(b, T), w_lo[:, s, w], act_hi[:, c, :], start=False, stop=c == DC - 1)
                n.then_inc(pe_unit, 1)

            def sums(n, src, chunks, b):
                pe.wait_ge(sq_ready, n)
                for c in range(chunks):
                    i = mm(bank(b, T), ones[:, :], src[:, c, :], start=c == 0, stop=c == chunks - 1)
                i.then_inc(stat_ready, 1)

            pe.wait_ge(consts, 5)
            pe.wait_ge(clo_ready, 1)
            def ada_unit(u, slot, m, k, base, first=False, last=False):
                hi_there(u)
                if first and m in (2, 3, 4):
                    before = 0 if m == 2 else m - 1
                    pe.wait_ge(row_ready, 4 * before + 4)
                    pe.wait_ge(mod_ready, before + 1)
                for w, there in ((w_hi, None), (w_lo, lo_there)):
                    if there:
                        there(u)
                    for b in range(4):
                        n = mm(bank(base + b), csplit[:, k * 2 * NC:k * 2 * NC + P], w[:, slot % SPL, b * 512:(b + 1) * 512],
                               start=first and not there, stop=last and there is not None)
                    if not there:
                        n.then_inc(pe_hi, 1)
                n.then_inc(pe_unit, 1)

            def turn_rows(m, base, bs):
                for b in bs:
                    pe.wait_ge(row_ready, 4 * m + b + 1)
                    for c in range(4):
                        n = nc.tensor.transpose(bank(base, 2 * NC, (4 * b + c) * 2 * NC),
                                                modrow[b % 2][:, c * P:(c + 1) * P], ident[0:2 * NC, 0:2 * NC])
                    n.then_inc(modT_done, 1)

            for u in range(2 * DC):
                m, k = u // DC, u % DC
                ada_unit(u, u, m, k, 4 * (1 - m), k == 0, k == DC - 1)
                if u == 10:
                    sums(1, rstd[:, 1:2, :], 1, 2)
                if u == DC:
                    turn_rows(0, 4, (0, 1))
                if u == DC + 1:
                    turn_rows(0, 4, (2, 3))
            turn_rows(1, 0, range(4))

            def projections(first, count, before):
                with pe.Fori(0, count // 4) as i:
                    for k in range(4):
                        pe.wait_ge(bank_free[k % 2], i * 2 + (before // 2 + k // 2))
                        project(i * 4 + (first + k), k, k % 2)

            def pool_mm_of(c):
                g, j = c // 2, c % 2
                pe.wait_ge(in_poolw, 16)
                pe.wait_ge(d_ready, g + 1)
                if c >= 2:
                    pe.wait_ge(ypool_ready, c - 1)
                for h in range(2):
                    n = mm(bank(2 + c % 2, T), poolw[:, g, h, j * P:(j + 1) * P], dd[:, 2 * g + h, :], start=h == 0, stop=h == 1)
                n.then_inc(pool_mm, 1)

            def lru_mm_of(c):
                pe.wait_ge(in_lruw, 16)
                pe.wait_ge(ypool_ready, LC)
                pe.wait_ge(conv_ready, c + 1)
                if c >= 1:
                    pe.wait_ge(sig_ready, c)
                mm(bank(2, XL), lruw[:, 0, c, :], xc[:, c, :], start=True, stop=True)
                mm(bank(3, XL), lruw[:, 1, c, :], xc[:, c, :], start=True, stop=True).then_inc(lru_mm, 1)

            extra = {}
            extra[TAIL_AT + 7] = [lambda: sums(2, ysq, LC, 2)]
            extra[TAIL_AT + 8] = [lambda: sums(3, ysq[:, LC:, :], LC, 3)]
            for c in range(LC):
                extra[POOL_AT[c]] = extra.get(POOL_AT[c], []) + [lambda c=c: pool_mm_of(c)]
                extra[LRU_AT[c]] = extra.get(LRU_AT[c], []) + [lambda c=c: lru_mm_of(c)]
            for u in range(2 * DC, O0):
                kind = ORDER[u]
                if kind[0] == "ada":
                    ada_unit(u, u, kind[1], kind[2], 4, kind[2] == 0, kind[2] == DC - 1)
                else:
                    if kind[1] == 0:
                        pe.wait_ge(alo_ready, L1)
                    at_least(pe, bank_free[kind[1] % 2], kind[1] // 2)
                    project(u, u, kind[1] % 2)
                for back, bs in ((1, (0, 1)), (2, (2, 3))):
                    k = ORDER[u - back]
                    if k[0] == "ada" and k[2] == DC - 1 and u - back >= 2 * DC:
                        turn_rows(k[1], 4, bs)
                for f in extra.get(u, []):
                    f()
            turn_rows(4, 4, range(4))
            pe.wait_ge(alo_ready, L2)
            projections(O0, DC, NZ)
            sums(4, work1[:, 1:2, :], 1, 2)
            def queries(i, k, quarters=None, first=False, last=False):
                pe.wait_ge(bank_free[k], i + (NZ + DC) // 2)
                project(i * 4 + (Q0 + 2 * k), 2 * k, k, quarters)
                ada_unit(i * 4 + (Q0 + 2 * k + 1), 2 * k + 1, 5, i * 2 + k, 4, first, last)

            queries(0, 0, L2, first=True)
            queries(0, 1)
            for i in range(1, DC // 2 - 1):
                queries(i, 0)
                queries(i, 1)
            queries(DC // 2 - 1, 0)
            queries(DC // 2 - 1, 1, last=True)
            turn_rows(5, 2, range(4))
            wait_evacuated(pe, ZP)
            pe.wait_ge(in_keys, 16)

            def scores(t):
                r = P if t < TT - 1 else T - (TT - 1) * P
                at_least(pe, score_copied, t)
                for j in range(DC):
                    n = mm(bank(4 + j // 4, P, j % 4 * P)[0:r, :], qT[:, j, t * P:t * P + r], keysT[:, j, :], start=True, stop=True)
                n.then_inc(score_mm, 1)

            def transposes(t):
                r = P if t < TT - 1 else T - (TT - 1) * P
                pe.wait_ge(sel_ready, t + 1)
                at_least(pe, idT_ready, t - 1)
                if t == 0:
                    pe.wait_ge(mod_ready, 6)
                for j in range(3):
                    n = nc.tensor.transpose(bank(2 + t % 2, r, j * r), sel[0:r, j, :], ident[0:r, 0:r])
                n.then_inc(selT_done, 1)

            scores(0)
            def early_product(n):
                pe.wait_ge(bank_free[n % 2], (ZP + n) // 2)
                project(M0 + n, M0 + n, n % 2, late=n >= ND)

            for n in range(ND):
                early_product(n)
                for i in range(TT):
                    if n == SCORES_AT[i]:
                        scores(i)
                    if n == TURN_AT[i]:
                        transposes(i)

            def dense_gates(i):
                for h in range(4):
                    pe.wait_ge(onehots_ready, i * 4 + (h + 1))
                    for q in range(2):
                        b = 2 * h + q
                        at_least(pe, gcopied, i * 8 + (b - 3))
                        for t in range(4):
                            n = mm(bank(4 + b % 4, P, t * P), one1[:, h, 4 * q + t, :], one2[:, h, 4 * q + t, :],
                                   start=True, stop=True)
                        n.then_inc(gmm[h][q], 1)

            rounds(pe, T // 32, dense_gates)

            for n in range(ND, NE):
                early_product(n)

            def first_product(unit, half):
                for k in range(EG):
                    pe.wait_ge(bank_free[k % 2], half + (ZP // 2 + k // 2))
                    project(unit + k, k, k % 2, late=True)

            def second_product(unit, tiles, par, uses):
                pe.wait_ge(gw_ready, tiles + EG)
                for k in range(EG):
                    s = k % SPL
                    hi_there(unit + k)
                    for h in range(2):
                        b = (2 * k + h) % 4
                        pe.wait_ge(vbank_free[b], uses + ((2 * k + h) // 4 + 1))
                        for e in range(EG):
                            w = slice(e * 2 * P + h * P, e * 2 * P + (h + 1) * P)
                            mm(bank(2 + b, T), w_hi[:, s, w], gw_hi[:, par, e, :], start=e == 0, stop=False)
                            n = mm(bank(2 + b, T), w_hi[:, s, w], gw_lo[:, par, e, :], start=False, stop=False)
                    n.then_inc(pe_hi, 1)
                    lo_there(unit + k, late=True)
                    for h in range(2):
                        b = (2 * k + h) % 4
                        for e in range(EG):
                            w = slice(e * 2 * P + h * P, e * 2 * P + (h + 1) * P)
                            n = mm(bank(2 + b, T), w_lo[:, s, w], gw_hi[:, par, e, :], start=False, stop=e == EG - 1)
                        n.then_inc(vhalf_done if h == 0 else pe_unit, 1)

            for g in range(3):
                second_product(v_unit(g), g * EG, g % 2, g * DC // 4)
            with pe.Fori(0, (NG - 4) // 2) as i:
                for j in range(2):
                    g = 4 + j
                    first_product(i * (4 * EG) + u_unit(g), i * EG + g * EG // 2)
                    second_product(i * (4 * EG) + v_unit(g - 1), i * (2 * EG) + (g - 1) * EG, (g - 1) % 2,
                                   i * (DC // 2) + (g - 1) * DC // 4)
            g = NG - 1
            second_product(v_unit(g), g * EG, g % 2, g * DC // 4)
            sums(5, prod[:, 1:2, :], 1, 6)


def kernel(**inputs):
    import concourse.bacc as _bacc
    from concourse.bass_utils import run_bass_kernel_spmd as _run

    a = {k: np.asarray(v) for k, v in inputs.items()}

    def cols(v):
        v = v.reshape(-1, v.shape[-1] // P, P)
        return v.transpose(2, 0, 1).reshape(P, -1)

    def proj(w, order):
        n = w.shape[1] // P
        return w.reshape(DC, P, n, P).transpose(2, 1, 0, 3).reshape(n, P, 2048)[order]

    u = a["peer_u"][0].reshape(P, P, DC, P).transpose(1, 3, 2, 0).reshape(NG, EG, P, 2048)
    v = a["peer_v"][0].reshape(P, NG, EG, EG, 2 * P).transpose(1, 3, 0, 2, 4).reshape(NG, EG, P, 2048)
    ada = a["w_ada"][0].reshape(DC, P, 6, 2048).transpose(2, 0, 1, 3)
    z = proj(a["w_in"][0], list(range(16, 24)) + list(range(16)))
    parts = [np.stack([ada[k[1], k[2]] if k[0] == "ada" else z[k[1]] for k in ORDER]),
             proj(a["w_out"][0], list(range(DC))), np.stack([proj(a["peer_wq"][0], list(range(DC))), ada[5]], axis=1).reshape(2 * DC, P, 2048)]
    parts += [u[g] for g in EARLY] + [v[0], v[1], v[2]]
    for g in range(len(EARLY), NG):
        parts += [u[g], v[g - 1]]
    w_stream = np.concatenate(parts + [v[NG - 1]])

    tokens = np.concatenate([a["x_prompt"][0], a["x_sample"].reshape(NB * NS, D)])
    x_d = tokens.reshape(T, DC, P).transpose(2, 1, 0)
    c_d = np.concatenate([a["c_prompt"], a["c_sample"]]).reshape(NC, DC, P).transpose(2, 1, 0)
    hist_d = np.concatenate([a["state_conv"][0].reshape(NB, CW - 1, LC, P).transpose(3, 2, 0, 1).reshape(P, -1),
                             a["state_pool"][0].reshape(NB, HIST, LC, P).transpose(3, 2, 0, 1).reshape(P, -1)], axis=1)
    h0 = a["state_lru"][0].reshape(NB, LC, P).transpose(2, 1, 0).reshape(P, -1)
    cinv = np.array([[1.0 / min(t + 1, w) for t in range(HIST)] for w in WINDOWS], np.float32).reshape(1, -1)
    table = {"b_ada": cols(a["b_ada"]), "norm1": cols(a["norm1_g"]), "norm2": cols(a["norm2_g"]),
             "final": cols(a["final_g"]), "gn_lru": cols(a["gnorm_lru_g"]), "gn_pool": cols(a["gnorm_pool_g"]),
             "conv_w": cols(a["conv_w"][0]), "conv_b": cols(a["conv_b"]), "ba": cols(a["lru_ba"].reshape(1, -1)),
             "bx": cols(a["lru_bx"].reshape(1, -1)), "lam": cols(a["lru_lambda"]), "pool_b": cols(a["pool_b"].reshape(1, -1)),
             "pool_s": cols(a["pool_scale"]), "cinv": np.repeat(cinv, P, axis=0), "h0": h0}
    vecs_d = np.concatenate([table[n] for n, _ in VCOLS], axis=1)
    lruw_d = np.stack([a["lru_wa"][0], a["lru_wx"][0]]).transpose(2, 0, 1, 3)
    poolw_d = a["pool_w"][0].reshape(4, 2, P, 2 * P).transpose(2, 0, 1, 3)
    keys_d = a["peer_keys"][0].reshape(DC, P, P).transpose(2, 0, 1)

    nc = _bacc.Bacc("TRN2", target_bir_lowering=False, num_devices=1)
    arrays, args = {}, []
    for name, v_ in (("w_stream", w_stream), ("vecs", vecs_d), ("c", c_d), ("hist", hist_d), ("x", x_d),
                     ("lruw", lruw_d), ("poolw", poolw_d), ("keys", keys_d)):
        v_ = np.ascontiguousarray(v_)
        arrays[f"in_{name}_dram"] = v_
        args.append(nc.dram_tensor(f"in_{name}_dram", v_.shape, mybir.dt.from_np(v_.dtype), kind="ExternalInput").ap())
    for i, shape in enumerate([(P, DC, T), (P, LC, NC, CW - 1), (P, LC, NC), (P, LC, PL)]):
        args.append(nc.dram_tensor(f"out_{i}_dram", shape, F, kind="ExternalOutput").ap())
    hybrid_step(nc, *args)
    r = _run(nc, [arrays], core_ids=[0]).results[0]
    y, cv, hl, pc = (r[f"out_{i}_dram"] for i in range(4))
    y = y.transpose(2, 1, 0).reshape(T, D)
    cv = cv.transpose(2, 3, 1, 0).reshape(1, NC, CW - 1, LC * P)
    hl = hl.transpose(2, 1, 0).reshape(1, NC, LC * P)
    pc = pc.transpose(2, 1, 0).reshape(PL, LC * P)
    pool_s = np.stack([pc[PAT + PS * b + NS:PAT + PS * (b + 1)] for b in range(NB)])[None]
    return (y[:SEQ][None], y[SEQ:].reshape(NB, NS, D), cv[:, :1], hl[:, :1], pc[SEQ:PAT][None, None],
            cv[:, 1:], hl[:, 1:], pool_s)
```

```python
import numpy as np
import concourse.bass as bass
from concourse import mybir
from contextlib import ExitStack, contextmanager

F = mybir.dt.float32
FR = mybir.dt.float32r
I32 = mybir.dt.int32
U32 = mybir.dt.uint32
ALU = mybir.AluOpType
ACT = mybir.ActivationFunctionType
AX = mybir.AxisListType

P = 128
D = 2048
DC = D // P
SEQ = 256
NB, NS = 8, 4
T = SEQ + NB * NS
NC = 1 + NB
LC = 8
CW = 4
HIST = 15
WINDOWS = (2, 4, 8, 16)
HEADS, TOPK = 8, 16
EPS = 1e-6
CS = CW - 1 + NS
CAT = CW - 1 + SEQ
CL = CAT + NB * CS
XL = CL - (CW - 1)
PS = HIST + NS
PAT = HIST + SEQ
PL = PAT + NB * PS
PAIRS = [(a, TOPK // (a + 1)) for a in range(8)]
NCAND = sum(n for _, n in PAIRS) + 8
TT = 3

RAW, SPL = 4, 2
NZ = 24
ORDER = [("ada", m, k) for m in range(2) for k in range(DC)]
_ada = [("ada", m, k) for m in range(2, 5) for k in range(DC)]
ORDER += _ada[:4]
_a = 4
for _b in range(8):
    _n = 3 if _b < 4 else 4
    _zs, _as = [("z", 3 * _b + _j) for _j in range(3)], _ada[_a:_a + _n]
    _a += _n
    ORDER += _zs + _as if _b < 7 else _as + _zs
ORDER += _ada[_a:]
O0 = len(ORDER)
Q0 = O0 + DC
M0 = Q0 + 2 * DC
ZP = NZ + 2 * DC
EG = 8
NG = P // EG
EARLY = (2, 3, 0, 1)
NE = len(EARLY) * EG
ND = NE - 8
V0 = M0 + NE
B0 = V0 + 3 * EG
NU = V0 + 2 * P - NE
QORDER = [("a", 0), ("a", 1), ("a", 2), ("q", 0), ("q", 1), ("q", 2), ("q", 3), ("a", 3)]
for _n in range(4, DC):
    QORDER += [("q", _n), ("a", _n)]
SCORES_AT = (None, 0, 9)
ROWS_AT = (None, 6, 15)
LISTS_AT = (6, 15, 20)
EXPS_AT = (9, 18, 20)
TURN_AT = (12, 20, 22)
GATED = (0, 2, 3, 3, 3, 2, 1, 1)
TCH = 16
NCH = T // TCH


_z = [ORDER.index(("z", n)) for n in range(NZ)]
POOL_AT = [_z[16] + 1 + (c + 1) // 2 for c in range(8)]
LRUW_AT = POOL_AT[7] + 1
CONV_AT = [_z[16] - 1 + c for c in range(8)]
LRU_AT = [LRUW_AT + 2 + (5 * c) // 4 for c in range(8)]
TAIL_AT = _z[23] + 1
P0, P1 = M0 + 1, M0 + ND
POOLED = ([2 * DC + 1, 2 * DC + 2, 2 * DC + 3]
          + [u for u in range(_z[7], TAIL_AT) if ORDER[u][0] == "ada" and ORDER[u][2] % 4 == 2]
          + list(range(TAIL_AT + 1, O0, 2)) + [Q0 + 1, Q0 + 2, Q0 + 3] + list(range(P0, P1)))
NQ = 4
T1, T2 = NQ, NQ + 2
L1, L2, L3 = NQ, NQ + 1, 2 * NQ + 1


def u_unit(g):
    return M0 + EARLY.index(g) * EG if g in EARLY else B0 + 2 * EG * (g - 4)


def v_unit(g):
    return V0 + EG * g if g < 3 else B0 + EG + 2 * EG * (g - 3) if g < NG - 1 else NU - EG


def tile_shape(i):
    return (P, HEADS) if i < TT - 1 else (P, HEADS * NB * NS // P)


def pool_lows(u):
    return sum(1 for v in POOLED if v <= u)


def lows(u):
    return u + 1 - pool_lows(u)


def wait_low(eng, lo_pool, lo_ready, u, moved=0):
    if u in POOLED:
        eng.wait_ge(lo_pool, pool_lows(u))
    else:
        eng.wait_ge(lo_ready, moved + lows(u))


VCOLS = [("b_ada", 96), ("norm1", DC), ("norm2", DC), ("final", DC), ("gn_lru", LC), ("gn_pool", LC),
         ("conv_w", CW * LC), ("conv_b", LC), ("ba", LC), ("bx", LC), ("lam", LC), ("pool_b", LC),
         ("pool_s", LC), ("cinv", 4 * HIST), ("h0", LC * NB)]
VOFF, _o = {}, 0
for _n, _w in VCOLS:
    VOFF[_n] = (_o, _w)
    _o += _w
NV = _o
NHIST = LC * NB * (CW - 1) + LC * NB * HIST


class Chain:

    def __init__(self, eng, sem):
        self.eng, self.sem, self.n, self.base = eng, sem, 0, None

    def done(self, ins):
        ins.then_inc(self.sem, 1)
        self.n += 1

    def wait(self):
        self.eng.wait_ge(self.sem, self.n if self.base is None else self.base + (self.n - self.start))

    def link(self, ins):
        self.done(ins)
        self.wait()

    @contextmanager
    def loop(self, first, end, per):
        count = end - first
        with self.eng.Fori(first, end) as i:
            self.start = self.n
            self.base = i * per + (self.n - first * per)
            yield i
            assert self.n - self.start == per, (self.n - self.start, per)
        self.n = self.start + count * per
        self.base = None


def at_least(eng, sem, value):
    if not isinstance(value, int) or value > 0:
        eng.wait_ge(sem, value)


def rounds(eng, n, body):
    body(0)
    with eng.Fori(1, n) as i:
        body(i)


def hybrid_step(nc, w_stream, vecs_d, c_d, hist_d, x_d, lruw_d, poolw_d, keys_d,
                o_y, o_conv, o_lru, o_pool):
    ctx = ExitStack()
    with ctx:
        def sb(name, shape, dt=F, scope=None):
            return (scope or ctx).enter_context(nc.sbuf_tensor(name, shape, dt))

        def sem(name):
            return ctx.enter_context(nc.semaphore(name))

        raw = sb("raw", [P, RAW, 2048])
        w_hi = sb("w_hi", [P, SPL, 2048], FR)
        w_lo = sb("w_lo", [P, SPL, 2048], FR)
        act_hi = sb("act_hi", [P, DC, T], FR)
        act_lo = sb("act_lo", [P, DC, T], FR)
        x = sb("x", [P, DC, T])
        vecs = sb("vecs", [P, NV])
        mod = sb("mod", [P, 6, DC, NC])
        scale1 = sb("scale1", [P, DC, NC])
        scale2 = sb("scale2", [P, DC, NC])
        ones = sb("ones", [P, P])
        ident = sb("ident", [P, P])
        iota = sb("iota", [P, P])
        epsc = sb("epsc", [P, 1])
        rstd = sb("rstd", [P, 2, T])
        soft = sb("soft", [P, 6, LC])
        fix = sb("fix", [P, 2, HIST])
        o_cv = sb("o_cv", [P, LC, NC, CW - 1])
        o_hl = sb("o_hl", [P, LC, NC])
        csplit = sb("csplit", [P, (DC - 1) * 2 * NC + P], FR)
        cpart = csplit[:, 0:DC * 2 * NC].rearrange("p (k n) -> p k n", n=2 * NC)

        MIXN = 18700 + 2 * 512
        with ExitStack() as early:
            mix = sb("mix", [P, MIXN], F, early)
        gates_in = sb("gates_in", [P, 2, NCH, EG, TCH])
        gw_hi = sb("gw_hi", [P, 2, EG, T], FR)
        gw_lo = sb("gw_lo", [P, 2, EG, T], FR)
        gel = sb("gel", [P, 2, T])
        prod = sb("prod", [P, 2, T])
        acc = sb("acc", [P, DC, T])
        ROUTEN = 2 * T * EG + 2 * 2 * EG * T + 4 * T
        gates_dram = nc.dram_tensor("gates_dense", (NCH, P, P, TCH), F, kind="Internal").ap()

        ps = ctx.enter_context(nc.psum_tensor("ps", [P, 4096], F))

        def bank(b, n=512, at=0):
            return ps[:, b * 512 + at:b * 512 + at + n]

        def vec(name):
            o, w = VOFF[name]
            return vecs[:, o:o + w]

        at = [0]

        def carve(n):
            at[0] += n
            assert at[0] <= MIXN
            return at[0] - n

        pcat_o, ucat_o, gate_o, xc_o = carve(LC * PL), carve(LC * CL), carve(LC * T), carve(2538)
        ra_o, ii_o, wts_o = carve(LC * CL), carve(LC * PL), carve(2048)

        def view(o, *dims):
            n = int(np.prod(dims))
            v = mix[:, o:o + n]
            if len(dims) == 2:
                return v.rearrange("p (a b) -> p a b", b=dims[1])
            if len(dims) == 3:
                return v.rearrange("p (a b c) -> p a b c", b=dims[1], c=dims[2])
            return v

        pcat, ucat = view(pcat_o, LC, PL), view(ucat_o, LC, CL)
        gate, hist = view(gate_o, LC, T), view(gate_o, NHIST)
        xc_f, sB = view(xc_o, LC, CL), view(xc_o, 6, PL)
        ra_f, dd = view(ra_o, LC, CL), view(ra_o, LC, T)
        ii_f, sA = view(ii_o, LC, CL), view(ii_o, LC, PL)
        xc, ra, ii = xc_f[:, :, 0:XL], ra_f[:, :, 0:XL], ii_f[:, :, 0:XL]
        poolw = view(wts_o, 4, 2, 2 * P)
        lruw = view(wts_o, 2, LC, P)
        tanhs = ucat[:, :, 0:XL]
        y_pool, y_lru = view(pcat_o, LC, T), view(ucat_o, LC, T)
        ysq = view(ra_o, 2 * LC, T)
        work1 = view(xc_o, DC, T)
        work2 = view(pcat_o, DC, T)
        modrow_o = carve(2 * 512)
        modrow = [mix[0:2 * NC, modrow_o + 512 * b:modrow_o + 512 * (b + 1)] for b in range(2)]
        hist_conv = view(gate_o, LC, NB, CW - 1)
        hist_pool = view(gate_o + LC * NB * (CW - 1), LC, NB, HIST)
        at[0] = 0
        qT = view(carve(DC * T), DC, T)
        keysT = view(carve(2048), DC, P)
        sc = view(carve(2048), DC, P)
        sc2 = view(carve(2 * P), 2, P)
        eq = view(carve(2 * TOPK * NCAND), 2, TOPK, NCAND)
        topv = view(carve(2 * HEADS * TOPK), HEADS, 2, TOPK)
        topi = view(carve(2 * HEADS * TOPK), HEADS, 2, TOPK)
        topf = view(carve(2 * HEADS * TOPK), HEADS, 2, TOPK)
        cand = view(carve(HEADS * NCAND), HEADS, NCAND)
        cidx = view(carve(HEADS * NCAND), HEADS, NCAND)
        cand2 = view(carve(2 * NCAND), 2, NCAND)
        best = view(carve(P), HEADS, TOPK)
        bpos = view(carve(P), HEADS, TOPK)
        bposf = view(carve(P), HEADS, TOPK)
        eidx = view(carve(P), HEADS, TOPK)
        eint = view(carve(P), P)
        eint2 = view(carve(P), P)
        sel = view(carve(3 * P), 3, P)
        gsum = view(carve(HEADS), HEADS)
        idT = view(carve(3 * T), 3, T)
        assert at[0] <= ROUTEN
        idT_end = at[0]
        loose = keysT[0:NB * NS]
        at[0] = 0
        stage = view(carve(2 * P * TCH), 2, P, TCH)
        one1 = view(carve(4 * 8 * P), 4, 8, P)
        one2 = view(carve(4 * 8 * P), 4, 8, P)
        assert at[0] <= idT_end - 3 * T
        gelq = acc
        gelu_dram = nc.dram_tensor("gelus", (2, P, EG, T), F, kind="Internal").ap()

        raw_in = [sem(f"raw_in{i}") for i in range(RAW)]
        hi_ready, lo_ready = sem("hi_ready"), sem("lo_ready")
        pe_hi = sem("pe_hi")
        pe_unit = sem("pe_unit")
        in_vecs, in_c, in_hist, in_x, in_lruw, in_poolw, in_keys = (
            sem(n) for n in ("in_vecs", "in_c", "in_hist", "in_x", "in_lruw", "in_poolw", "in_keys"))
        consts = sem("consts")
        csil_ready, chi_ready, clo_ready = sem("csil_ready"), sem("chi_ready"), sem("clo_ready")
        sq_ready, stat_ready, std_ready = sem("sq_ready"), sem("stat_ready"), sem("std_ready")
        rstd_ready, normed_ready = sem("rstd_ready"), sem("normed_ready")
        row_ready = sem("row_ready")
        lo_pool = sem("lo_pool")
        modT_done, mod_ready = sem("modT_done"), sem("mod_ready")
        bank_free = [sem("bank0_free"), sem("bank1_free")]
        t_ready, ahi_ready, alo_ready = sem("t_ready"), sem("ahi_ready"), sem("alo_ready")
        hist_ready = sem("hist_ready")
        gate_ready = sem("gate_ready")
        states_saved, pool_saved = sem("states_saved"), sem("pool_saved")
        d_ready, pool_mm, ypool_ready = sem("d_ready"), sem("pool_mm"), sem("ypool_ready")
        conv_ready, lru_mm, sig_ready, loga_ready = sem("conv_ready"), sem("lru_mm"), sem("sig_ready"), sem("loga_ready")
        tanh_ready, a_ready, var_ready, mult_ready = sem("tanh_ready"), sem("a_ready"), sem("var_ready"), sem("mult_ready")
        soft_a = sem("soft_a")
        scan_ready, hl_saved = sem("scan_ready"), sem("hl_saved")
        score_mm, score_copied, lists_ready = sem("score_mm"), sem("score_copied"), sem("lists_ready")
        cidx_ready, cidx_used = sem("cidx_ready"), sem("cidx_used")
        dif_ready, exp_ready = sem("dif_ready"), sem("exp_ready")
        packed, unpacked = sem("packed"), sem("unpacked")
        sel_ready, selT_done, idT_ready = sem("sel_ready"), sem("selT_done"), sem("idT_ready")
        pairs_ready, onehots_ready = sem("pairs_ready"), sem("onehots_ready")
        gmm = [[sem(f"gmm{h}{q}") for q in range(2)] for h in range(4)]
        gcopied = sem("gcopied")
        stage_out = [sem("stage_out0"), sem("stage_out1")]
        gate_in = [sem("gate_in0"), sem("gate_in1")]
        gelu_out = [sem("gelu_out0"), sem("gelu_out1")]
        gelu_in = [sem("gelu_in0"), sem("gelu_in1")]
        prod_done, gwhi_ready, gw_ready = sem("prod_done"), sem("gwhi_ready"), sem("gw_ready")
        vhalf_done = sem("vhalf_done")
        vbank_free = [sem(f"vbank{b}_free") for b in range(4)]
        out_ready = sem("out_ready")
        out_sem = sem("out_sem")
        dve_steps, act_steps, pool_steps = sem("dve_steps"), sem("act_steps"), sem("pool_steps")

        def by_seq(t, start, step):
            return t[:, :, start:start + NB * step].rearrange("p c (b k) -> p c b k", k=step)

        def wait_evacuated(eng, n):
            eng.wait_ge(bank_free[0], n // 2)
            eng.wait_ge(bank_free[1], n // 2)

        block = ctx.enter_context(nc.Block())

        @block.sync
        def _(sp):
            for u in range(RAW):
                sp.dma_start(raw[:, u, :], w_stream[u]).then_inc(raw_in[u], 16)
            for u in range(RAW, V0 + RAW):
                wait_low(sp, lo_pool, lo_ready, u - RAW)
                sp.dma_start(raw[:, u % RAW, :], w_stream[u]).then_inc(raw_in[u % RAW], 16)
            u0 = V0
            with sp.Fori(0, (NU - u0) // RAW - 1) as i:
                for k in range(RAW):
                    sp.wait_ge(lo_ready, i * RAW + lows(u0 + k))
                    sp.dma_start(raw[:, k, :], w_stream[i * RAW + (u0 + RAW + k)]).then_inc(raw_in[k], 16)
            sp.wait_ge(states_saved, 2)
            sp.dma_start(o_conv, o_cv[:, :, :, :]).then_inc(out_sem, 16)
            sp.wait_ge(hl_saved, 2)
            sp.dma_start(o_lru, o_hl[:, :, :]).then_inc(out_sem, 16)
            for q in range(NQ):
                c = slice(q * DC // NQ, (q + 1) * DC // NQ)
                sp.wait_ge(out_ready, q + 1)
                sp.dma_start(o_y[:, c], acc[:, c, :]).then_inc(out_sem, 16)
            sp.wait_ge(out_sem, 16 * (2 + NQ))
            sp.wait_ge(pool_saved, 16)

        @block.gpsimd
        def _(pool):
            ch = Chain(pool, pool_steps)
            nc.gpsimd.memset(csplit[:, :].bitcast(F), 0.0).then_inc(consts, 1)
            nc.gpsimd.memset(ones[:, :], 1.0).then_inc(consts, 1)
            nc.gpsimd.memset(epsc[:, :], EPS).then_inc(consts, 1)
            nc.gpsimd.iota(iota[:, :], pattern=[[1, P]], base=0, channel_multiplier=0,
                           allow_small_or_imprecise_dtypes=True).then_inc(consts, 1)
            ch.link(nc.gpsimd.memset(ident[:, :], 0.0))
            nc.gpsimd.affine_select(out=ident[:, :], in_=ident[:, :], compare_op=ALU.not_equal, fill=1.0,
                                    base=0, pattern=[[-1, P]], channel_multiplier=1).then_inc(consts, 1)
            pool.wait_ge(in_x, 16)
            ch.link(nc.gpsimd.tensor_tensor(rstd[:, 1, :], x[:, 0, :], x[:, 0, :], ALU.mult))
            for c in range(1, DC):
                ch.link(nc.gpsimd.tensor_tensor(work1[:, c, :], x[:, c, :], x[:, c, :], ALU.mult))
                n = nc.gpsimd.tensor_tensor(rstd[:, 1, :], rstd[:, 1, :], work1[:, c, :], ALU.add)
                if c < DC - 1:
                    ch.link(n)
            n.then_inc(sq_ready, 1)
            pool.wait_ge(rstd_ready, 1)
            nc.gpsimd.tensor_tensor(work2, x[:, :, :], rstd[:, 0, :].unsqueeze(1).to_broadcast([P, DC, T]),
                                    ALU.mult).then_inc(normed_ready, 1)
            def lo_units(first, end):
                for u in range(first, end):
                    if u in POOLED:
                        s = u % RAW
                        pool.wait_ge(hi_ready, u + 1)
                        pool.wait_ge(pe_unit, u - SPL + 1)
                        nc.gpsimd.tensor_tensor(w_lo[:, s % SPL, :], raw[:, s, :], w_hi[:, s % SPL, :].bitcast(F),
                                                ALU.subtract).then_inc(lo_pool, 1)

            lo_units(2 * DC, 2 * DC + 4)
            pool.wait_ge(in_hist, 16)
            pool.wait_ge(alo_ready, L1)
            nc.gpsimd.memset(ucat[:, :, 0:CW - 1], 0.0).then_inc(hist_ready, 1)
            nc.gpsimd.memset(pcat[:, :, 0:HIST], 0.0).then_inc(hist_ready, 1)
            for c in range(LC):
                nc.gpsimd.tensor_copy(ucat[:, c, CAT:CL].rearrange("p (b k) -> p b k", k=CS)[:, :, 0:CW - 1],
                                      hist_conv[:, c]).then_inc(hist_ready, 1)
                nc.gpsimd.tensor_copy(pcat[:, c, PAT:PL].rearrange("p (b k) -> p b k", k=PS)[:, :, 0:HIST],
                                      hist_pool[:, c]).then_inc(hist_ready, 1)
            def new_states():
                wait_evacuated(pool, 16)
                pool.wait_ge(hist_ready, 2 + 2 * LC)
                pool.dma_start(o_pool, pcat).then_inc(pool_saved, 16)
                nc.gpsimd.tensor_copy(o_cv[:, :, 0, :], ucat[:, :, SEQ:SEQ + CW - 1]).then_inc(states_saved, 1)
                nc.gpsimd.tensor_copy(o_cv[:, :, 1:, :], by_seq(ucat, CAT, CS)[:, :, :, NS:]).then_inc(states_saved, 1)

            def new_lru_state():
                pool.wait_ge(scan_ready, LC)
                nc.gpsimd.tensor_copy(o_hl[:, :, 0], xc[:, :, SEQ - 1]).then_inc(hl_saved, 1)
                nc.gpsimd.tensor_copy(o_hl[:, :, 1:], by_seq(xc_f, CAT, CS)[:, :, :, NS - 1]).then_inc(hl_saved, 1)

            for u in range(2 * DC + 4, O0):
                lo_units(u, u + 1)
                if u == _z[15] + 1:
                    new_states()
                if u == TAIL_AT + 5:
                    new_lru_state()
            lo_units(Q0, Q0 + 4)

            def pair_indices(i):
                r, H = tile_shape(i)
                pool.wait_ge(lists_ready, i * 2 + 2)
                at_least(pool, cidx_used, i)
                for a, n in PAIRS:
                    o = sum(m for b, m in PAIRS if b < a)
                    nc.gpsimd.tensor_tensor(cidx[0:r, 0:H, o:o + n], topf[0:r, 0:H, 0, a:a + 1].to_broadcast([r, H, n]),
                                            topf[0:r, 0:H, 1, 0:n], ALU.add).then_inc(cidx_ready, 1)
                nc.gpsimd.tensor_tensor(cidx[0:r, 0:H, NCAND - 8:], topf[0:r, 0:H, 0, 8:TOPK],
                                        topf[0:r, 0:H, 1, 0:1].to_broadcast([r, H, 8]), ALU.add).then_inc(cidx_ready, 1)

            lo_units(P0, M0 + LISTS_AT[0])
            pair_indices(0)
            lo_units(M0 + LISTS_AT[0], M0 + LISTS_AT[1])
            pair_indices(1)
            lo_units(M0 + LISTS_AT[1], M0 + LISTS_AT[2])
            pair_indices(2)
            lo_units(M0 + LISTS_AT[2], P1)

            def times_gates(i):
                for h in range(4):
                    pool.wait_ge(pairs_ready, i * 4 + (h + 1))
                    g = idT[:, 2, bass.ds(i * 32 + 8 * h, 8)].unsqueeze(2).to_broadcast([P, 8, P])
                    nc.gpsimd.tensor_tensor(one2[:, h], one2[:, h], g, ALU.mult).then_inc(onehots_ready, 1)

            with pool.Fori(0, T // 32) as i:
                times_gates(i)

        @block.scalar
        def _(act):
            ch = Chain(act, act_steps)
            act.dma_start(c_ap := view(gate_o + NHIST, DC, NC), c_d).then_inc(in_c, 16)
            act.dma_start(vecs[:, :], vecs_d).then_inc(in_vecs, 16)
            act.dma_start(x[:, :, :], x_d).then_inc(in_x, 16)

            def low_made(u, moved=0):
                if isinstance(moved, int):
                    wait_low(act, lo_pool, lo_ready, u)
                else:
                    act.wait_ge(lo_ready, moved + lows(u))

            def hi(u):
                s = u % RAW
                act.wait_ge(raw_in[s], 16 * (u // RAW + 1))
                if u >= SPL:
                    act.wait_ge(pe_hi, u - SPL + 1)
                    low_made(u - SPL)
                nc.scalar.activation(w_hi[:, s % SPL, :], raw[:, s, :], ACT.Copy).then_inc(hi_ready, 1)

            def hi_at(u, slot, u4):
                act.wait_ge(raw_in[slot], u4 * 16 + 16)
                act.wait_ge(pe_hi, u + (1 - SPL))
                nc.scalar.activation(w_hi[:, slot % SPL, :], raw[:, slot, :], ACT.Copy).then_inc(hi_ready, 1)

            def hi_next(u0, i, per, k):
                n = u0 + k + 1
                low_made(n - SPL, i * per)
                hi_at(i * per + n, n % RAW, i * (per // RAW) + n // RAW)

            def stats(n, out, width, bank_no):
                act.wait_ge(stat_ready, n)
                nc.scalar.activation(out, bank(bank_no, T), ACT.Sqrt, bias=epsc[:, :], scale=1.0 / width).then_inc(std_ready, 1)

            hi(0)
            act.wait_ge(in_c, 16)
            csil = view(gate_o + NHIST + DC * NC, DC, NC)
            nc.scalar.activation(csil, c_ap, ACT.Silu).then_inc(csil_ready, 1)
            act.wait_ge(csil_ready, 1)
            act.wait_ge(consts, 5)
            nc.scalar.activation(cpart[:, :, 0:NC], csil, ACT.Copy).then_inc(chi_ready, 1)
            def rows(part, base, bs):
                for b in bs:
                    at_least(act, modT_done, 4 * part + b - 1)
                    nc.scalar.activation(modrow[b % 2], bank(base + b)[0:2 * NC, :], ACT.Copy).then_inc(row_ready, 1)

            def high_quarters(before, between=lambda q: None):
                for q in range(NQ):
                    c = slice(q * DC // NQ, (q + 1) * DC // NQ)
                    act.wait_ge(t_ready, before + q + 1)
                    nc.scalar.activation(act_hi[:, c, :], work2[:, c, :], ACT.Copy).then_inc(ahi_ready, 1)
                    between(q)

            for u in range(2 * DC):
                hi(u + 1)
                if u == 2 * DC - 1:
                    act.dma_start(hist, hist_d).then_inc(in_hist, 16)
                if u == 11:
                    stats(1, rstd[:, 0, :], D, 2)
                if u == DC - 1:
                    act.wait_ge(pe_unit, u + 1)
                    rows(0, 4, (0, 1))
                if u == DC:
                    rows(0, 4, (2, 3))
                if u == 2 * DC - 1:
                    act.wait_ge(pe_unit, u + 1)
                    rows(1, 0, range(4))
            hi(2 * DC + 1)
            high_quarters(0, lambda q: hi(2 * DC + 2) if q == 1 else None)
            act.wait_ge(in_vecs, 16)
            ch.link(nc.scalar.activation(soft[:, 0, :], vec("lam"), ACT.Abs))
            ch.link(nc.scalar.activation(soft[:, 1, :], soft[:, 0, :], ACT.Exp, scale=-1.0))
            nc.scalar.activation(soft[:, 2, :], soft[:, 1, :], ACT.Ln, bias=1.0).then_inc(soft_a, 1)

            def lru_weights():
                act.wait_ge(pool_mm, LC)
                act.dma_start(lruw, lruw_d).then_inc(in_lruw, 16)

            def lru_gate(c):
                act.wait_ge(lru_mm, c + 1)
                nc.scalar.activation(ra[:, c, :], bank(2, XL), ACT.Sigmoid, bias=vec("ba")[:, c:c + 1]).then_inc(act_steps, 1)
                nc.scalar.activation(ii[:, c, :], bank(3, XL), ACT.Sigmoid, bias=vec("bx")[:, c:c + 1]).then_inc(sig_ready, 1)

            def tanh_exp():
                act.wait_ge(loga_ready, 1)
                act.wait_ge(states_saved, 2)
                nc.scalar.activation(tanhs, ra, ACT.Tanh, scale=-1.0).then_inc(tanh_ready, 1)
                act.wait_ge(tanh_ready, 1)
                nc.scalar.activation(ra, ra, ACT.Exp).then_inc(a_ready, 1)

            def gate_gelu():
                wait_evacuated(act, NZ)
                nc.scalar.activation(gate, gate, ACT.Gelu_apprx_tanh).then_inc(gate_ready, 1)

            def multiplier():
                act.wait_ge(var_ready, 1)
                nc.scalar.activation(xc, xc, ACT.Sqrt).then_inc(mult_ready, 1)

            def group_squares(n, y):
                act.wait_ge(ypool_ready, LC + (n == 0))
                nc.scalar.activation(ysq[:, n * LC:(n + 1) * LC, :], y, ACT.Square).then_inc(sq_ready, 1)

            def group_high(n, y):
                act.wait_ge(t_ready, T1 + n + 1)
                nc.scalar.activation(act_hi[:, n * LC:(n + 1) * LC, :], y, ACT.Copy).then_inc(ahi_ready, 1)

            extra = {}

            def at_unit(u, f):
                extra[u] = extra.get(u, []) + [f]

            at_unit(LRUW_AT, lru_weights)
            for c in range(LC):
                at_unit(LRU_AT[c], lambda c=c: lru_gate(c))
            at_unit(TAIL_AT, tanh_exp)
            at_unit(TAIL_AT + 1, multiplier)
            at_unit(TAIL_AT + 2, gate_gelu)
            at_unit(TAIL_AT + 6, lambda: group_squares(0, y_lru))
            at_unit(TAIL_AT + 7, lambda: group_squares(1, y_pool))
            at_unit(TAIL_AT + 9, lambda: stats(2, rstd[:, 0, :], D // 2, 2))
            at_unit(TAIL_AT + 9, lambda: stats(3, rstd[:, 1, :], D // 2, 3))
            at_unit(TAIL_AT + 11, lambda: group_high(0, y_lru))
            at_unit(TAIL_AT + 12, lambda: group_high(1, y_pool))
            for u in range(2 * DC, O0):
                if u > 2 * DC + 1:
                    hi(u + 1)
                if u == _z[7]:
                    act.dma_start(poolw, poolw_d).then_inc(in_poolw, 16)
                kind = ORDER[u - 1]
                if kind[0] == "z" and kind[1] >= 16:
                    n = kind[1]
                    act.wait_ge(pe_unit, u)
                    if n == 16:
                        act.wait_ge(hist_ready, 2 + 2 * LC)
                    nc.scalar.activation(gate[:, n - 16, :], bank(n % 2, T), ACT.Copy).then_inc(bank_free[n % 2], 1)
                for back, bs in ((0, (0, 1)), (1, (2, 3))):
                    k = ORDER[u - back]
                    if k[0] == "ada" and k[2] == DC - 1 and u - back >= 2 * DC and u < O0 - 1:
                        act.wait_ge(pe_unit, u - back + 1)
                        rows(k[1], 4, bs)
                for f in extra.get(u, []):
                    f()
            act.wait_ge(pe_unit, O0)
            rows(4, 4, range(4))
            low_made(O0 - 1)
            with act.Fori(0, DC // 4) as i:
                for k in range(4):
                    hi_next(O0, i, 4, k)
            hi(Q0 + 1)
            stats(4, rstd[:, 0, :], D, 2)
            hi(Q0 + 2)
            high_quarters(T2, lambda q: hi(Q0 + 3) if q == 1 else None)
            act.wait_ge(alo_ready, L3)
            act.dma_start(keysT, keys_d).then_inc(in_keys, 16)
            for u in range(Q0 + 3, Q0 + 8):
                hi(u + 1)
            with act.Fori(0, 2 * DC // 4 - 2) as i:
                for k in range(4):
                    hi_next(Q0 + 8, i, 4, k)
            act.wait_ge(pe_unit, M0)
            rows(5, 4, range(4))

            def score_rows(i):
                r, out = (P, sc) if i < TT - 1 else (T - (TT - 1) * P, loose)
                act.wait_ge(score_mm, i + 1)
                at_least(act, lists_ready, i * 2)
                for b in range(4):
                    n = nc.scalar.activation(out[0:r, 4 * b:4 * b + 4, :], bank(4 + b)[0:r, :].rearrange("p (a n) -> p a n", n=P),
                                             ACT.Copy)
                n.then_inc(score_copied, 1)
                if i == TT - 1:
                    act.wait_ge(score_copied, TT)
                    for g in range(4):
                        act.dma_start(sc[32 * g:32 * g + 32, 0:4, :], loose[:, 4 * g:4 * g + 4, :]).then_inc(packed, 16)

            def exps(i):
                r, H = tile_shape(i)
                act.wait_ge(dif_ready, i + 1)
                nc.scalar.activation(best[0:r, 0:H], best[0:r, 0:H], ACT.Exp).then_inc(exp_ready, 1)

            def early_gelu(n):
                if n >= 2 * EG and n % EG == 0:
                    act.wait_ge(gelu_out[n // EG % 2], 16)
                nc.scalar.activation(gelq[:, n % (2 * EG), :], bank(n % 2, T), ACT.Gelu_apprx_tanh).then_inc(bank_free[n % 2], 1)

            def early_tile(n):
                g, k = EARLY[n // EG], n % EG
                hi(M0 + n + 1)
                act.wait_ge(pe_unit, M0 + n + 1)
                early_gelu(n)
                if g >= 2 and k == EG - 1:
                    wait_evacuated(act, ZP + n + 1)
                    h = n // EG
                    act.dma_start(gelu_dram[g - 2], gelq[:, h * EG:(h + 1) * EG, :]).then_inc(gelu_out[h], 16)

            score_rows(0)
            for n in range(ND):
                early_tile(n)
                for i in range(TT):
                    if n == ROWS_AT[i]:
                        score_rows(i)
                    if n == EXPS_AT[i]:
                        exps(i)
                if n == EXPS_AT[TT - 1] + 1:
                    act.wait_ge(sel_ready, TT)
                    for g in range(4):
                        act.dma_start(loose[:, 0:3, 32 * g:32 * g + 32], sel[32 * g:32 * g + 32, :, 0:32]).then_inc(unpacked, 16)

            def gate_chunks(i):
                for c in range(2):
                    at_least(act, stage_out[c], i * 16)
                    for h in range(2):
                        for q in range(2):
                            act.wait_ge(gmm[2 * c + h][q], i + 1)
                            t0 = 8 * h + 4 * q
                            nc.scalar.activation(stage[:, c, :, t0:t0 + 4].rearrange("p n t -> p t n"),
                                                 bank(4 + 2 * h + q).rearrange("p (t n) -> p t n", n=P),
                                                 ACT.Copy).then_inc(gcopied, 1)
                    act.wait_ge(gcopied, i * 8 + (4 * c + 4))
                    act.dma_start(gates_dram[i * 2 + c], stage[:, c, :, :]).then_inc(stage_out[c], 16)

            rounds(act, NCH // 2, gate_chunks)

            def load_gates(g, par):
                act.dma_start(gates_in[:, par], gates_dram.rearrange("c p (g k) t -> g p c (k t)", k=EG)[g]
                              ).then_inc(gate_in[par], 16)

            for c in range(2):
                act.wait_ge(stage_out[c], 16 * (NCH // 2))
            load_gates(0, 0)

            def expert_tiles(hi_of, u, tile, par):
                for k in range(EG):
                    hi_of(k)
                    act.wait_ge(pe_unit, u(k) + 1)
                    nc.scalar.activation(gel[:, k % 2, :], bank(k % 2, T), ACT.Gelu_apprx_tanh).then_inc(bank_free[k % 2], 1)
                    act.wait_ge(prod_done, tile(k) + 1)
                    nc.scalar.activation(gw_hi[:, par, k, :], prod[:, k % 2, :], ACT.Copy).then_inc(gwhi_ready, 1)

            load_gates(1, 1)

            def gated(tile):
                act.wait_ge(prod_done, tile + 1)
                nc.scalar.activation(gw_hi[:, tile // EG % 2, tile % EG, :], prod[:, tile % 2, :], ACT.Copy).then_inc(gwhi_ready, 1)

            t = 0
            for n, count in enumerate(GATED):
                hi(M0 + ND + n + 1)
                for _ in range(count):
                    gated(t)
                    t += 1
                act.wait_ge(pe_unit, M0 + ND + n + 1)
                early_gelu(ND + n)
            gated(t)
            load_gates(2, 0)
            load_gates(3, 1)

            def load_gelu(tile):
                act.wait_ge(prod_done, tile - 1)
                act.dma_start(gel[:, tile % 2, :], gelu_dram[tile // EG - 2, :, tile % EG, :]).then_inc(gelu_in[tile % 2], 16)

            for k in range(EG):
                hi(v_unit(0) + k + 1)
            for c in range(2):
                act.wait_ge(gelu_out[c], 16)
            load_gelu(2 * EG)
            load_gelu(2 * EG + 1)
            for g in (1, 2):
                act.wait_ge(pe_unit, v_unit(g))
                for k in range(EG):
                    hi(v_unit(g) + k + 1)
                    tile = (g + 1) * EG + k
                    gated(tile)
                    if tile + 2 < 4 * EG:
                        load_gelu(tile + 2)
            with act.Fori(0, (NG - 4) // 2) as i:
                for j in range(2):
                    g = 4 + j
                    load_gates(i * 2 + g, j)
                    expert_tiles(lambda k: hi_next(u_unit(g), i, 4 * EG, k), lambda k: i * (4 * EG) + (u_unit(g) + k),
                                 lambda k: i * (2 * EG) + (g * EG + k), j)
                    for k in range(EG):
                        hi_next(v_unit(g - 1), i, 4 * EG, k)
            for k in range(EG - 1):
                hi(v_unit(NG - 1) + k + 1)
            stats(5, rstd[:, 0, :], D, 6)

        @block.vector
        def _(dve):
            ch = Chain(dve, dve_steps)
            link = ch.link
            V = nc.vector

            def lo(u):
                s = u % RAW
                dve.wait_ge(hi_ready, u + 1)
                at_least(dve, pe_unit, u - SPL + 1)
                V.tensor_tensor(w_lo[:, s % SPL, :], raw[:, s, :], w_hi[:, s % SPL, :].bitcast(F), ALU.subtract).then_inc(lo_ready, 1)

            def lo_next(u0, i, per, k):
                n = u0 + k + 1
                s = n % RAW
                dve.wait_ge(hi_ready, i * per + (n + 1))
                dve.wait_ge(pe_unit, i * per + (n - SPL + 1))
                V.tensor_tensor(w_lo[:, s % SPL, :], raw[:, s, :], w_hi[:, s % SPL, :].bitcast(F), ALU.subtract).then_inc(lo_ready, 1)

            def modulate_quarters(out, scale, shift, before, lows_before, normed_too, between):
                def quarter(q):
                    c0, n = q * DC // NQ, DC // NQ
                    o = out[:, c0:c0 + n, :]
                    if normed_too:
                        link(V.tensor_tensor(o, x[:, c0:c0 + n, :], rstd[:, 0, :].unsqueeze(1).to_broadcast([P, n, T]), ALU.mult))
                    os = o[:, :, SEQ:T].rearrange("p c (b t) -> p c b t", t=NS)
                    for c in range(c0, c0 + n):
                        ch.done(V.tensor_scalar(out[:, c, 0:SEQ], out[:, c, 0:SEQ], scale[:, c, 0:1], shift[:, c, 0:1],
                                                ALU.mult, ALU.add))
                    link(V.tensor_tensor(os, os, scale[:, c0:c0 + n, 1:].unsqueeze(3).to_broadcast([P, n, NB, NS]), ALU.mult))
                    V.tensor_tensor(os, os, shift[:, c0:c0 + n, 1:].unsqueeze(3).to_broadcast([P, n, NB, NS]), ALU.add).then_inc(t_ready, 1)

                def low(q):
                    c = slice(q * DC // NQ, (q + 1) * DC // NQ)
                    dve.wait_ge(ahi_ready, before + q + 1)
                    dve.wait_ge(t_ready, before + q + 1)
                    V.tensor_tensor(act_lo[:, c, :], out[:, c, :], act_hi[:, c, :].bitcast(F), ALU.subtract).then_inc(alo_ready, 1)

                quarter(0)
                for q in range(1, NQ):
                    quarter(q)
                    low(q - 1)
                    between(q)
                low(NQ - 1)
                dve.wait_ge(alo_ready, lows_before + NQ)

            def inv_std(n, r):
                dve.wait_ge(std_ready, n)
                link(V.reciprocal(r, r))

            lo(0)
            dve.wait_ge(chi_ready, 1)
            csil = view(gate_o + NHIST + DC * NC, DC, NC)
            V.tensor_tensor(cpart[:, :, NC:], csil, cpart[:, :, 0:NC].bitcast(F), ALU.subtract).then_inc(clo_ready, 1)
            dve.wait_ge(in_vecs, 16)
            bias = vec("b_ada").rearrange("p (m c) -> p m c", m=6)

            def mod_part(m, base):
                dve.wait_ge(modT_done, 4 * m + 4)
                mt = bank(base, DC * 2 * NC).rearrange("p (c n) -> p c n", n=2 * NC)
                link(V.tensor_tensor(mod[:, m, :, :], mt[:, :, 0:NC], bias[:, m, :].unsqueeze(2).to_broadcast([P, DC, NC]), ALU.add))
                V.tensor_tensor(mod[:, m, :, :], mod[:, m, :, :], mt[:, :, NC:2 * NC], ALU.add).then_inc(mod_ready, 1)
                if m in (1, 4):
                    dve.wait_ge(mod_ready, m + 1)
                    s, g = (scale1, "norm1") if m == 1 else (scale2, "norm2")
                    link(V.tensor_scalar(s[:, :, :], mod[:, m, :, :], 1.0, None, ALU.add))
                    link(V.tensor_tensor(s[:, :, :], s[:, :, :], vec(g).unsqueeze(2).to_broadcast([P, DC, NC]), ALU.mult))

            for u in range(2 * DC):
                lo(u + 1)
                if u == 12:
                    dve.wait_ge(std_ready, 1)
                    V.reciprocal(rstd[:, 0, :], rstd[:, 0, :]).then_inc(rstd_ready, 1)
                if u == DC + 2:
                    mod_part(0, 4)
            mod_part(1, 0)
            dve.wait_ge(normed_ready, 1)
            modulate_quarters(work2, scale1, mod[:, 0], 0, 0, False, lambda q: None)

            def double(dst, src, d0, s0, n, by, fr):
                link(V.tensor_tensor(dst[:, d0:d0 + n, fr:PL], src[:, s0:s0 + n, fr:PL], src[:, s0:s0 + n, fr - by:PL - by], ALU.add))

            def pooled(g, s, c0):
                win = WINDOWS[g]
                p = pcat[:, 2 * g:2 * g + 2, :]
                d = dd[:, 2 * g:2 * g + 2, :]
                s = s[:, c0:c0 + 2, :]
                link(V.scalar_tensor_tensor(out=d[:, :, 0:SEQ], in0=s[:, :, HIST:PAT], scalar=1.0 / win,
                                            in1=p[:, :, HIST:PAT], op0=ALU.mult, op1=ALU.subtract))
                ci = vec("cinv")[:, g * HIST:(g + 1) * HIST].unsqueeze(1).to_broadcast([P, 2, HIST])
                link(V.tensor_tensor(fix[:, :, :], s[:, :, HIST:2 * HIST], ci, ALU.mult))
                ch.done(V.tensor_tensor(d[:, :, 0:HIST], fix[:, :, :], p[:, :, HIST:2 * HIST], ALU.subtract))
                for c in range(2):
                    def tail(t):
                        return t[:, c, PAT:PL].rearrange("p (b k) -> p b k", k=PS)[:, :, HIST:]
                    n = V.scalar_tensor_tensor(out=d[:, c, SEQ:T].rearrange("p (b t) -> p b t", t=NS), in0=tail(s),
                                               scalar=1.0 / win, in1=tail(p), op0=ALU.mult, op1=ALU.subtract)
                    if c == 0:
                        ch.done(n)
                n.then_inc(d_ready, 1)
                ch.wait()

            def sums2():
                wait_evacuated(dve, 8)
                dve.wait_ge(hist_ready, 2 + 2 * LC)
                double(sA, pcat, 0, 0, LC, 1, 1)

            def sums8():
                double(sA, sB, 4, 2, 4, 4, 7)
                pooled(2, sA, 4)

            def sums16():
                double(sB, sA, 4, 6, 2, 8, 15)
                pooled(3, sB, 4)

            def softplus8():
                dve.wait_ge(soft_a, 1)
                u = soft[:, 1, :]
                link(V.tensor_scalar(soft[:, 3, :], u, 1.0, 1.0, ALU.add, ALU.subtract))
                link(V.tensor_scalar(soft[:, 4, :], soft[:, 3, :], 0.0, None, ALU.is_equal))
                link(V.tensor_tensor(soft[:, 3, :], soft[:, 3, :], soft[:, 4, :], ALU.add))
                link(V.reciprocal(soft[:, 3, :], soft[:, 3, :]))
                link(V.tensor_tensor(soft[:, 3, :], soft[:, 3, :], soft[:, 2, :], ALU.mult))
                link(V.tensor_tensor(soft[:, 3, :], soft[:, 3, :], soft[:, 4, :], ALU.add))
                link(V.tensor_tensor(soft[:, 3, :], soft[:, 3, :], u, ALU.mult))
                link(V.tensor_scalar(soft[:, 4, :], vec("lam"), -1.0, 0.0, ALU.mult, ALU.max))
                link(V.tensor_tensor(soft[:, 3, :], soft[:, 3, :], soft[:, 4, :], ALU.add))
                link(V.tensor_scalar(soft[:, 5, :], soft[:, 3, :], -8.0, None, ALU.mult))

            cw = vec("conv_w").rearrange("p (k c) -> p k c", k=CW)

            def conv(c):
                dve.wait_ge(d_ready, 4)
                wait_evacuated(dve, 8 + 2 * (c // 2 + 1))
                link(V.tensor_scalar(xc[:, c, :], ucat[:, c, CW - 1:CL], cw[:, CW - 1, c:c + 1], vec("conv_b")[:, c:c + 1],
                                     ALU.mult, ALU.add))
                for k in range(CW - 1):
                    n = V.scalar_tensor_tensor(out=xc[:, c, :], in0=ucat[:, c, k:k + XL], scalar=cw[:, k, c:c + 1],
                                               in1=xc[:, c, :], op0=ALU.mult, op1=ALU.add)
                    if k < CW - 2:
                        link(n)
                n.then_inc(conv_ready, 1)

            def pool_out(c):
                dve.wait_ge(pool_saved, 16)
                dve.wait_ge(pool_mm, c + 1)
                V.tensor_scalar(y_pool[:, c, :], bank(2 + c % 2, T), vec("pool_b")[:, c:c + 1], vec("pool_s")[:, c:c + 1],
                                ALU.add, ALU.mult).then_inc(ypool_ready, 1)

            def log_a(c):
                dve.wait_ge(sig_ready, c + 1)
                ch.done(V.tensor_scalar(ra[:, c, :], ra[:, c, :], soft[:, 5, c:c + 1], None, ALU.mult))
                ch.done(V.tensor_tensor(ii[:, c, :], ii[:, c, :], xc[:, c, :], ALU.mult))

            extra = {}

            def at_unit(u, *fs):
                extra[u] = extra.get(u, []) + list(fs)

            z8 = ORDER.index(("z", 7))
            at_unit(z8 + 2, sums2)
            at_unit(z8 + 4, lambda: pooled(0, sA, 0), lambda: double(sB, sA, 0, 2, 6, 2, 3))
            at_unit(z8 + 7, lambda: pooled(1, sB, 0), sums8)
            at_unit(z8 + 8, sums16)
            at_unit(z8 + 9, softplus8)
            for c in range(LC):
                at_unit(POOL_AT[c] + 1, lambda c=c: pool_out(c))
                at_unit(CONV_AT[c], lambda c=c: conv(c))
                at_unit(LRU_AT[c] + 1, lambda c=c: log_a(c))
            def recurrence_input():
                dve.wait_ge(a_ready, 1)
                link(V.tensor_tensor(xc, ra, ra, ALU.mult))
                V.scalar_tensor_tensor(out=xc, in0=xc, scalar=1.0, in1=tanhs, op0=ALU.add, op1=ALU.mult).then_inc(var_ready, 1)

            def times_multiplier():
                dve.wait_ge(mult_ready, 1)
                link(V.memset(xc[:, :, 0:1], 1.0))
                link(V.tensor_tensor(ii, ii, xc, ALU.mult))
                border = CAT - 1
                ch.done(V.memset(by_seq(ra_f, border, CS)[:, :, :, 0], 0.0))
                link(V.tensor_copy(by_seq(ii_f, border, CS)[:, :, :, 0], vec("h0").rearrange("p (c b) -> p c b", b=NB)))

            def scan(c):
                V.tensor_tensor_scan(xc[:, c, :], ra[:, c, :], ii[:, c, :], 0.0, ALU.mult, ALU.add).then_inc(scan_ready, 1)

            def times_gate():
                dve.wait_ge(scan_ready, LC)
                dve.wait_ge(gate_ready, 1)
                link(V.tensor_tensor(y_lru[:, :, 0:SEQ], xc[:, :, 0:SEQ], gate[:, :, 0:SEQ], ALU.mult))
                V.tensor_tensor(by_seq(y_lru, SEQ, NS), by_seq(xc_f, CAT, CS)[:, :, :, 0:NS], by_seq(gate, SEQ, NS),
                                ALU.mult).then_inc(ypool_ready, 1)

            def group_norm(n_, y, g, r):
                inv_std(n_, rstd[:, r, :])
                for c in range(LC):
                    n = V.scalar_tensor_tensor(out=y[:, c, :], in0=y[:, c, :], scalar=vec(g)[:, c:c + 1],
                                               in1=rstd[:, r, :], op0=ALU.mult, op1=ALU.mult)
                n.then_inc(t_ready, 1)

            def group_lows():
                dve.wait_ge(t_ready, T2)
                dve.wait_ge(ahi_ready, T2)
                link(V.tensor_tensor(act_lo[:, 0:LC, :], y_lru, act_hi[:, 0:LC, :].bitcast(F), ALU.subtract))
                V.tensor_tensor(act_lo[:, LC:, :], y_pool, act_hi[:, LC:, :].bitcast(F), ALU.subtract).then_inc(alo_ready, 1)

            def loga_done():
                V.tensor_copy(soft[:, 0, 0:1], soft[:, 5, 0:1]).then_inc(loga_ready, 1)

            at_unit(LRU_AT[7] + 2, loga_done)
            at_unit(TAIL_AT, recurrence_input)
            at_unit(TAIL_AT + 2, times_multiplier)
            for c in range(LC):
                at_unit(TAIL_AT + 3 + c // 4, lambda c=c: scan(c))
            at_unit(TAIL_AT + 5, times_gate)
            at_unit(TAIL_AT + 10, lambda: group_norm(2, y_lru, "gn_lru", 0))
            at_unit(TAIL_AT + 11, lambda: group_norm(3, y_pool, "gn_pool", 1))
            at_unit(TAIL_AT + 13, group_lows)
            for u in range(2 * DC, O0):
                if u + 1 not in POOLED:
                    lo(u + 1)
                kind = ORDER[u - 1]
                if kind[0] == "z" and kind[1] < 16:
                    n = kind[1]
                    dst, start, step = (pcat, PAT, PS) if n < 8 else (ucat, CAT, CS)
                    dve.wait_ge(pe_unit, u)
                    V.tensor_copy(dst[:, n % 8, step - NS:step - NS + SEQ], bank(n % 2, SEQ))
                    V.tensor_copy(dst[:, n % 8, start:start + NB * step].rearrange("p (b k) -> p b k", k=step)[:, :, step - NS:],
                                  bank(n % 2, NB * NS, SEQ).rearrange("p (b t) -> p b t", t=NS)).then_inc(bank_free[n % 2], 1)
                k = ORDER[u - 3]
                if k[0] == "ada" and k[2] == DC - 1 and u - 3 >= 2 * DC:
                    mod_part(k[1], 4)
                for f in extra.get(u, []):
                    f()
            mod_part(4, 4)
            def residual(c, src, m):
                xs = x[:, c, SEQ:T].rearrange("p (b t) -> p b t", t=NS)
                V.scalar_tensor_tensor(out=x[:, c, 0:SEQ], in0=src[:, 0:SEQ], scalar=mod[:, m, c, 0:1],
                                       in1=x[:, c, 0:SEQ], op0=ALU.mult, op1=ALU.add)
                tmp = rstd[:, 1, 0:NB * NS].rearrange("p (b t) -> p b t", t=NS)
                link(V.tensor_tensor(tmp, src[:, SEQ:T].rearrange("p (b t) -> p b t", t=NS),
                                     mod[:, m, c, 1:].unsqueeze(2).to_broadcast([P, NB, NS]), ALU.mult))
                return V.tensor_tensor(xs, xs, tmp, ALU.add)

            def add_square(c, square):
                link(V.tensor_tensor(square, x[:, c, :], x[:, c, :], ALU.mult))
                link(V.tensor_tensor(rstd[:, 0, :], rstd[:, 0, :], square, ALU.add))

            dve.wait_ge(hl_saved, 2)
            link(V.memset(rstd[:, 0, :], 0.0))
            with ch.loop(0, DC // 4, 12) as i:
                for k in range(4):
                    lo_next(O0, i, 4, k)
                    dve.wait_ge(pe_unit, i * 4 + (O0 + k + 1))
                    residual(i * 4 + k, bank(k % 2, T), 2).then_inc(bank_free[k % 2], 1)
                    dve.wait_ge(bank_free[k % 2], i * 2 + ((NZ + k) // 2 + 1))
                    add_square(i * 4 + k, work1[:, 0, :])
            V.tensor_copy(work1[:, 1, :], rstd[:, 0, :]).then_inc(sq_ready, 1)
            inv_std(4, rstd[:, 0, :])
            modulate_quarters(work2, scale2, mod[:, 3], T2, L2, True, lambda q: None)

            for u in range(Q0 + 3, Q0 + 8):
                lo(u + 1)
                kind, n = QORDER[u - Q0 - 1]
                if kind == "q":
                    dve.wait_ge(pe_unit, u)
                    V.tensor_copy(qT[:, n, :], bank(n % 2, T)).then_inc(bank_free[n % 2], 1)
            with dve.Fori(0, 2 * DC // 4 - 2) as i:
                for k in range(4):
                    lo_next(Q0 + 8, i, 4, k)
                    if k % 2:
                        dve.wait_ge(pe_unit, i * 4 + (Q0 + 8 + k))
                        V.tensor_copy(qT[:, i * 2 + (4 + k // 2), :], bank(k // 2, T)).then_inc(bank_free[k // 2], 1)
            mod_part(5, 2)

            pos50 = iota[:, 0:NCAND]

            def top16(src, tmp, vals, idx):
                link(V.max(vals[:, 0:8], src))
                ch.done(V.max_index(idx[:, 0:8], vals[:, 0:8], src))
                link(V.match_replace(tmp, vals[:, 0:8], src, -3.0e38))
                link(V.max(vals[:, 8:16], tmp))
                ch.done(V.max_index(idx[:, 8:16], vals[:, 8:16], tmp))

            def route(i, between):
                r, H = tile_shape(i)
                if i < TT - 1:
                    dve.wait_ge(score_copied, i + 1)
                else:
                    dve.wait_ge(packed, 64)
                at_least(dve, cidx_ready, i * 9)
                for n in range(2 * H):
                    h, p = n // 2, n % 2
                    top16(sc[0:r, n, :], sc2[0:r, n % 2, :], topv[0:r, h, p, :], topi[0:r, h, p, :].bitcast(U32))
                    between(n)
                ch.wait()
                V.tensor_scalar(topf[0:r, 0:H, 0, :], topi[0:r, 0:H, 0, :].bitcast(U32), float(P), None, ALU.mult).then_inc(lists_ready, 1)
                V.tensor_copy(topf[0:r, 0:H, 1, :], topi[0:r, 0:H, 1, :].bitcast(U32)).then_inc(lists_ready, 1)
                o = 0
                for a, n in PAIRS:
                    ch.done(V.tensor_tensor(cand[0:r, 0:H, o:o + n], topv[0:r, 0:H, 0, a:a + 1].to_broadcast([r, H, n]),
                                            topv[0:r, 0:H, 1, 0:n], ALU.add))
                    o += n
                link(V.tensor_tensor(cand[0:r, 0:H, o:], topv[0:r, 0:H, 0, 8:TOPK], topv[0:r, 0:H, 1, 0:1].to_broadcast([r, H, 8]), ALU.add))
                for h in range(H):
                    top16(cand[0:r, h, :], cand2[0:r, h % 2, :], best[0:r, h, :], bpos[0:r, h, :].bitcast(U32))
                ch.wait()
                link(V.tensor_copy(bposf[0:r, 0:H], bpos[0:r, 0:H].bitcast(U32)))
                dve.wait_ge(cidx_ready, i * 9 + 9)
                for h in range(0, H, 2):
                    link(V.tensor_tensor(eq[0:r], pos50[0:r].unsqueeze(1).unsqueeze(1).to_broadcast([r, 2, TOPK, NCAND]),
                                         bposf[0:r, h:h + 2, :].unsqueeze(3).to_broadcast([r, 2, TOPK, NCAND]), ALU.is_equal))
                    link(V.tensor_tensor(eq[0:r], eq[0:r], cidx[0:r, h:h + 2, :].unsqueeze(2).to_broadcast([r, 2, TOPK, NCAND]), ALU.mult))
                    link(V.reduce_sum(eidx[0:r, h:h + 2, :], eq[0:r], axis=AX.X))
                link(V.tensor_copy(gsum[0:r, 0:H], best[0:r, 0:H, 0]))
                V.tensor_tensor(best[0:r, 0:H], best[0:r, 0:H], gsum[0:r, 0:H].unsqueeze(2).to_broadcast([r, H, TOPK]), ALU.subtract).then_inc(dif_ready, 1)
                k = H * TOPK
                e1, e2 = eint[0:r, 0:k].bitcast(I32), eint2[0:r, 0:k].bitcast(I32)
                link(V.tensor_copy(e1, eidx[0:r, 0:H].rearrange("p h k -> p (h k)")))
                ch.done(V.tensor_scalar(e2, e1, 7, None, ALU.logical_shift_right))
                link(V.tensor_scalar(e1, e1, P - 1, None, ALU.bitwise_and))
                at_least(dve, selT_done, i)
                V.tensor_copy(sel[0:r, 0, 0:k], e2).then_inc(cidx_used, 1)
                ch.done(V.tensor_copy(sel[0:r, 1, 0:k], e1))

            def gates_of(i):
                r, H = tile_shape(i)
                dve.wait_ge(exp_ready, i + 1)
                link(V.reduce_sum(gsum[0:r, 0:H], best[0:r, 0:H], axis=AX.X))
                link(V.reciprocal(gsum[0:r, 0:H], gsum[0:r, 0:H]))
                V.tensor_tensor(sel[0:r, 2, 0:H * TOPK].rearrange("p (h k) -> p h k", k=TOPK), best[0:r, 0:H],
                                gsum[0:r, 0:H].unsqueeze(2).to_broadcast([r, H, TOPK]), ALU.mult).then_inc(sel_ready, 1)

            def choice_out(i):
                r = P if i < TT - 1 else T - (TT - 1) * P
                dve.wait_ge(selT_done, i + 1)
                V.tensor_copy(idT[:, :, i * P:i * P + r], bank(2 + i % 2, 3 * r).rearrange("p (j t) -> p j t", j=3)).then_inc(idT_ready, 1)

            def first_choice(n):
                if n == 5:
                    gates_of(0)
                if n == 14:
                    choice_out(0)

            route(0, lambda n: None)
            route(1, first_choice)
            route(2, lambda n: gates_of(1) if n == 1 else None)
            gates_of(2)
            choice_out(1)
            choice_out(2)
            dve.wait_ge(idT_ready, TT)

            wide = iota[:, :].unsqueeze(1).to_broadcast([P, 8, P])

            def onehots(i):
                for h in range(4):
                    at_least(dve, gmm[h][1], i)

                    def col(j):
                        return idT[:, j, bass.ds(i * 32 + 8 * h, 8)].unsqueeze(2).to_broadcast([P, 8, P])
                    V.tensor_tensor(one1[:, h], wide, col(0), ALU.is_equal)
                    V.tensor_tensor(one2[:, h], wide, col(1), ALU.is_equal).then_inc(pairs_ready, 1)

            rounds(dve, T // 32, onehots)
            lo(M0 + ND)
            for c in range(2):
                dve.wait_ge(stage_out[c], 16 * (NCH // 2))

            def gated(t, gelu):
                dve.wait_ge(gate_in[t // EG % 2], 16 * (t // (2 * EG) + 1))
                if t >= 2:
                    dve.wait_ge(gw_ready, t - 1)
                V.tensor_tensor(prod[:, t % 2, :].rearrange("p (c t) -> p c t", t=TCH),
                                gelu.rearrange("p (c t) -> p c t", t=TCH), gates_in[:, t // EG % 2, :, t % EG, :],
                                ALU.mult).then_inc(prod_done, 1)

            def gated_low(t):
                dve.wait_ge(gwhi_ready, t + 1)
                V.tensor_tensor(gw_lo[:, t // EG % 2, t % EG, :], prod[:, t % 2, :],
                                gw_hi[:, t // EG % 2, t % EG, :].bitcast(F), ALU.subtract).then_inc(gw_ready, 1)

            def with_low(t):
                if t >= 2:
                    gated_low(t - 2)
                for b in range(2):
                    dve.wait_ge(bank_free[b], (ZP + 2 * EG + t + 2 - b) // 2)
                gated(t, gelq[:, t, :])

            t = 0
            for n, count in enumerate(GATED):
                lo(M0 + ND + n + 1)
                for _ in range(count):
                    with_low(t)
                    t += 1
            with_low(t)
            gated_low(t - 1)
            gated_low(t)
            dve.wait_ge(prod_done, 2 * EG)

            def expert_tiles(lo_of, tile, half, par, turn):
                dve.wait_ge(gate_in[par], turn)
                for k in range(EG):
                    lo_of(k)
                    dve.wait_ge(bank_free[k % 2], half + (ZP // 2 + k // 2 + 1))
                    V.tensor_tensor(prod[:, k % 2, :].rearrange("p (c t) -> p c t", t=TCH),
                                    gel[:, k % 2, :].rearrange("p (c t) -> p c t", t=TCH), gates_in[:, par, :, k, :],
                                    ALU.mult).then_inc(prod_done, 1)
                    dve.wait_ge(gwhi_ready, tile + (k + 1))
                    V.tensor_tensor(gw_lo[:, par, k, :], prod[:, k % 2, :], gw_hi[:, par, k, :].bitcast(F),
                                    ALU.subtract).then_inc(gw_ready, 1)

            def add_up(lo_of, unit, units, uses, also=lambda k: None, last=None):
                start = isinstance(uses, int) and uses == 0
                if not start:
                    for b in range(4):
                        dve.wait_ge(vbank_free[b], uses)
                for k in range(EG):
                    lo_of(k)
                    also(k)
                    dve.wait_ge(vhalf_done, units + (k + 1))
                    for h in range(2):
                        c = 2 * k + h
                        if h == 1:
                            dve.wait_ge(pe_unit, unit + (k + 1))
                        if start:
                            n = V.tensor_copy(acc[:, c, :], bank(2 + c % 4, T))
                        else:
                            n = V.tensor_tensor(acc[:, c, :], acc[:, c, :], bank(2 + c % 4, T), ALU.add)
                        n.then_inc(vbank_free[c % 4], 1)
                    if last:
                        last(2 * k)
                        last(2 * k + 1)

            def lo_after(u0, last=NU):
                return lambda k: lo(u0 + k + 1) if u0 + k + 1 < last else None

            def stored(g):
                def tile(k):
                    t = g * EG + k
                    dve.wait_ge(gelu_in[k % 2], 16 * ((t - 2 * EG) // 2 + 1))
                    gated(t, gel[:, k % 2, :])
                    gated_low(t)
                return tile

            add_up(lo_after(v_unit(0)), v_unit(0), 0, 0)
            add_up(lo_after(v_unit(1)), v_unit(1), EG, DC // 4, stored(2))
            add_up(lo_after(v_unit(2)), v_unit(2), 2 * EG, 2 * DC // 4, stored(3))
            with dve.Fori(0, (NG - 4) // 2) as i:
                for j in range(2):
                    g = 4 + j
                    expert_tiles(lambda k: lo_next(u_unit(g), i, 4 * EG, k), i * (2 * EG) + g * EG, i * EG + g * EG // 2,
                                 j, i * 16 + 48)
                    add_up(lambda k: lo_next(v_unit(g - 1), i, 4 * EG, k), i * (4 * EG) + v_unit(g - 1),
                           i * (2 * EG) + (g - 1) * EG, i * (DC // 2) + (g - 1) * DC // 4)
            g = NG - 1

            def finish(c):
                dve.wait_ge(vbank_free[c % 4], (NG - 1) * DC // 4 + c // 4 + 1)
                link(residual(c, acc[:, c, :], 5))
                add_square(c, prod[:, 0, :])

            dve.wait_ge(gw_ready, NG * EG)
            link(V.memset(rstd[:, 0, :], 0.0))
            add_up(lo_after(v_unit(g)), v_unit(g), g * EG, g * DC // 4, last=finish)
            V.tensor_copy(prod[:, 1, :], rstd[:, 0, :]).then_inc(sq_ready, 1)
            inv_std(5, rstd[:, 0, :])
            for c in range(DC):
                n = V.scalar_tensor_tensor(out=acc[:, c, :], in0=x[:, c, :], scalar=vec("final")[:, c:c + 1],
                                           in1=rstd[:, 0, :], op0=ALU.mult, op1=ALU.mult)
                if c % (DC // NQ) == DC // NQ - 1:
                    n.then_inc(out_ready, 1)

        @block.tensor
        def _(pe):
            mm = nc.tensor.matmul

            def hi_there(u):
                pe.wait_ge(hi_ready, u + 1)

            def lo_there(u, late=False, moved=0):
                if late:
                    pe.wait_ge(lo_ready, u + (1 - len(POOLED)))
                else:
                    wait_low(pe, lo_pool, lo_ready, u, moved)

            def project(u, slot, b, quarters=None, late=False, moved=0):
                s = slot % SPL
                hi_there(u + moved)
                for c in range(DC):
                    w = slice(c * P, (c + 1) * P)
                    if quarters is not None and c % (DC // NQ) == 0:
                        pe.wait_ge(alo_ready, quarters + c // (DC // NQ) + 1)
                    mm(bank(b, T), w_hi[:, s, w], act_hi[:, c, :], start=c == 0, stop=False)
                    n = mm(bank(b, T), w_hi[:, s, w], act_lo[:, c, :], start=False, stop=False)
                n.then_inc(pe_hi, 1)
                lo_there(u, late, moved)
                for c in range(DC):
                    w = slice(c * P, (c + 1) * P)
                    n = mm(bank(b, T), w_lo[:, s, w], act_hi[:, c, :], start=False, stop=c == DC - 1)
                n.then_inc(pe_unit, 1)

            def sums(n, src, chunks, b):
                pe.wait_ge(sq_ready, n)
                for c in range(chunks):
                    i = mm(bank(b, T), ones[:, :], src[:, c, :], start=c == 0, stop=c == chunks - 1)
                i.then_inc(stat_ready, 1)

            pe.wait_ge(consts, 5)
            pe.wait_ge(clo_ready, 1)
            def ada_unit(u, slot, m, k, base, first=False, last=False):
                hi_there(u)
                if first and m in (2, 3, 4):
                    before = 0 if m == 2 else m - 1
                    pe.wait_ge(row_ready, 4 * before + 4)
                    pe.wait_ge(mod_ready, before + 1)
                for w, there in ((w_hi, None), (w_lo, lo_there)):
                    if there:
                        there(u)
                    for b in range(4):
                        n = mm(bank(base + b), csplit[:, k * 2 * NC:k * 2 * NC + P], w[:, slot % SPL, b * 512:(b + 1) * 512],
                               start=first and not there, stop=last and there is not None)
                    if not there:
                        n.then_inc(pe_hi, 1)
                n.then_inc(pe_unit, 1)

            def turn_rows(m, base, bs):
                for b in bs:
                    pe.wait_ge(row_ready, 4 * m + b + 1)
                    for c in range(4):
                        n = nc.tensor.transpose(bank(base, 2 * NC, (4 * b + c) * 2 * NC),
                                                modrow[b % 2][:, c * P:(c + 1) * P], ident[0:2 * NC, 0:2 * NC])
                    n.then_inc(modT_done, 1)

            for u in range(2 * DC):
                m, k = u // DC, u % DC
                ada_unit(u, u, m, k, 4 * (1 - m), k == 0, k == DC - 1)
                if u == 10:
                    sums(1, rstd[:, 1:2, :], 1, 2)
                if u == DC:
                    turn_rows(0, 4, (0, 1))
                if u == DC + 1:
                    turn_rows(0, 4, (2, 3))
            turn_rows(1, 0, range(4))

            def projections(first, count, before):
                with pe.Fori(0, count // 4) as i:
                    for k in range(4):
                        pe.wait_ge(bank_free[k % 2], i * 2 + (before // 2 + k // 2))
                        project(first + k, k, k % 2, moved=i * 4)

            def pool_mm_of(c):
                g, j = c // 2, c % 2
                pe.wait_ge(in_poolw, 16)
                pe.wait_ge(d_ready, g + 1)
                if c >= 2:
                    pe.wait_ge(ypool_ready, c - 1)
                for h in range(2):
                    n = mm(bank(2 + c % 2, T), poolw[:, g, h, j * P:(j + 1) * P], dd[:, 2 * g + h, :], start=h == 0, stop=h == 1)
                n.then_inc(pool_mm, 1)

            def lru_mm_of(c):
                pe.wait_ge(in_lruw, 16)
                pe.wait_ge(ypool_ready, LC)
                pe.wait_ge(conv_ready, c + 1)
                if c >= 1:
                    pe.wait_ge(sig_ready, c)
                mm(bank(2, XL), lruw[:, 0, c, :], xc[:, c, :], start=True, stop=True)
                mm(bank(3, XL), lruw[:, 1, c, :], xc[:, c, :], start=True, stop=True).then_inc(lru_mm, 1)

            extra = {}
            extra[TAIL_AT + 7] = [lambda: sums(2, ysq, LC, 2)]
            extra[TAIL_AT + 8] = [lambda: sums(3, ysq[:, LC:, :], LC, 3)]
            for c in range(LC):
                extra[POOL_AT[c]] = extra.get(POOL_AT[c], []) + [lambda c=c: pool_mm_of(c)]
                extra[LRU_AT[c]] = extra.get(LRU_AT[c], []) + [lambda c=c: lru_mm_of(c)]
            for u in range(2 * DC, O0):
                kind = ORDER[u]
                if kind[0] == "ada":
                    ada_unit(u, u, kind[1], kind[2], 4, kind[2] == 0, kind[2] == DC - 1)
                else:
                    if kind[1] == 0:
                        pe.wait_ge(alo_ready, L1)
                    at_least(pe, bank_free[kind[1] % 2], kind[1] // 2)
                    project(u, u, kind[1] % 2)
                for back, bs in ((1, (0, 1)), (2, (2, 3))):
                    k = ORDER[u - back]
                    if k[0] == "ada" and k[2] == DC - 1 and u - back >= 2 * DC:
                        turn_rows(k[1], 4, bs)
                for f in extra.get(u, []):
                    f()
            turn_rows(4, 4, range(4))
            pe.wait_ge(alo_ready, L2)
            projections(O0, DC, NZ)
            for u in range(Q0, M0):
                kind, n = QORDER[u - Q0]
                if kind == "q":
                    pe.wait_ge(bank_free[n % 2], (NZ + DC + n) // 2)
                    project(u, u, n % 2, L2 if n == 0 else None)
                else:
                    ada_unit(u, u, 5, n, 4, n == 0, n == DC - 1)
                if u == Q0:
                    sums(4, work1[:, 1:2, :], 1, 2)
            turn_rows(5, 2, range(4))
            wait_evacuated(pe, ZP)
            pe.wait_ge(in_keys, 16)

            def scores(t):
                r = P if t < TT - 1 else T - (TT - 1) * P
                at_least(pe, score_copied, t)
                for j in range(DC):
                    n = mm(bank(4 + j // 4, P, j % 4 * P)[0:r, :], qT[:, j, t * P:t * P + r], keysT[:, j, :], start=True, stop=True)
                n.then_inc(score_mm, 1)

            def transposes(t):
                r = P if t < TT - 1 else T - (TT - 1) * P
                if t < TT - 1:
                    pe.wait_ge(sel_ready, t + 1)
                else:
                    pe.wait_ge(unpacked, 64)
                rows = sel if t < TT - 1 else loose
                at_least(pe, idT_ready, t - 1)
                if t == 0:
                    pe.wait_ge(mod_ready, 6)
                for j in range(3):
                    n = nc.tensor.transpose(bank(2 + t % 2, r, j * r), rows[0:r, j, :], ident[0:r, 0:r])
                n.then_inc(selT_done, 1)

            scores(0)
            def early_product(n):
                pe.wait_ge(bank_free[n % 2], (ZP + n) // 2)
                project(M0 + n, M0 + n, n % 2, late=n >= ND)

            for n in range(ND):
                early_product(n)
                for i in range(TT):
                    if n == SCORES_AT[i]:
                        scores(i)
                    if n == TURN_AT[i]:
                        transposes(i)

            def dense_gates(i):
                for h in range(4):
                    pe.wait_ge(onehots_ready, i * 4 + (h + 1))
                    for q in range(2):
                        b = 2 * h + q
                        at_least(pe, gcopied, i * 8 + (b - 3))
                        for t in range(4):
                            n = mm(bank(4 + b % 4, P, t * P), one1[:, h, 4 * q + t, :], one2[:, h, 4 * q + t, :],
                                   start=True, stop=True)
                        n.then_inc(gmm[h][q], 1)

            rounds(pe, T // 32, dense_gates)

            for n in range(ND, NE):
                early_product(n)

            def first_product(unit, half):
                for k in range(EG):
                    pe.wait_ge(bank_free[k % 2], half + (ZP // 2 + k // 2))
                    project(unit + k, k, k % 2, late=True)

            def second_product(unit, tiles, par, uses):
                pe.wait_ge(gw_ready, tiles + EG)
                for k in range(EG):
                    s = k % SPL
                    hi_there(unit + k)
                    for h in range(2):
                        b = (2 * k + h) % 4
                        at_least(pe, vbank_free[b], uses + (2 * k + h) // 4)
                        for e in range(EG):
                            w = slice(e * 2 * P + h * P, e * 2 * P + (h + 1) * P)
                            mm(bank(2 + b, T), w_hi[:, s, w], gw_hi[:, par, e, :], start=e == 0, stop=False)
                            n = mm(bank(2 + b, T), w_hi[:, s, w], gw_lo[:, par, e, :], start=False, stop=False)
                    n.then_inc(pe_hi, 1)
                    lo_there(unit + k, late=True)
                    for h in range(2):
                        b = (2 * k + h) % 4
                        for e in range(EG):
                            w = slice(e * 2 * P + h * P, e * 2 * P + (h + 1) * P)
                            n = mm(bank(2 + b, T), w_lo[:, s, w], gw_hi[:, par, e, :], start=False, stop=e == EG - 1)
                        n.then_inc(vhalf_done if h == 0 else pe_unit, 1)

            for g in range(3):
                second_product(v_unit(g), g * EG, g % 2, g * DC // 4)
            with pe.Fori(0, (NG - 4) // 2) as i:
                for j in range(2):
                    g = 4 + j
                    first_product(i * (4 * EG) + u_unit(g), i * EG + g * EG // 2)
                    second_product(i * (4 * EG) + v_unit(g - 1), i * (2 * EG) + (g - 1) * EG, (g - 1) % 2,
                                   i * (DC // 2) + (g - 1) * DC // 4)
            g = NG - 1
            second_product(v_unit(g), g * EG, g % 2, g * DC // 4)
            sums(5, prod[:, 1:2, :], 1, 6)


def kernel(**inputs):
    import concourse.bacc as _bacc
    from concourse.bass_utils import run_bass_kernel_spmd as _run

    a = {k: np.asarray(v) for k, v in inputs.items()}

    def cols(v):
        v = v.reshape(-1, v.shape[-1] // P, P)
        return v.transpose(2, 0, 1).reshape(P, -1)

    def proj(w, order):
        n = w.shape[1] // P
        return w.reshape(DC, P, n, P).transpose(2, 1, 0, 3).reshape(n, P, 2048)[order]

    u = a["peer_u"][0].reshape(P, P, DC, P).transpose(1, 3, 2, 0).reshape(NG, EG, P, 2048)
    v = a["peer_v"][0].reshape(P, NG, EG, EG, 2 * P).transpose(1, 3, 0, 2, 4).reshape(NG, EG, P, 2048)
    ada = a["w_ada"][0].reshape(DC, P, 6, 2048).transpose(2, 0, 1, 3)
    z = proj(a["w_in"][0], list(range(16, 24)) + list(range(16)))
    q = proj(a["peer_wq"][0], list(range(DC)))
    parts = [np.stack([ada[k[1], k[2]] if k[0] == "ada" else z[k[1]] for k in ORDER]),
             proj(a["w_out"][0], list(range(DC))), np.stack([q[n] if kind == "q" else ada[5, n] for kind, n in QORDER])]
    parts += [u[g] for g in EARLY] + [v[0], v[1], v[2]]
    for g in range(len(EARLY), NG):
        parts += [u[g], v[g - 1]]
    w_stream = np.concatenate(parts + [v[NG - 1]])

    tokens = np.concatenate([a["x_prompt"][0], a["x_sample"].reshape(NB * NS, D)])
    x_d = tokens.reshape(T, DC, P).transpose(2, 1, 0)
    c_d = np.concatenate([a["c_prompt"], a["c_sample"]]).reshape(NC, DC, P).transpose(2, 1, 0)
    hist_d = np.concatenate([a["state_conv"][0].reshape(NB, CW - 1, LC, P).transpose(3, 2, 0, 1).reshape(P, -1),
                             a["state_pool"][0].reshape(NB, HIST, LC, P).transpose(3, 2, 0, 1).reshape(P, -1)], axis=1)
    h0 = a["state_lru"][0].reshape(NB, LC, P).transpose(2, 1, 0).reshape(P, -1)
    cinv = np.array([[1.0 / min(t + 1, w) for t in range(HIST)] for w in WINDOWS], np.float32).reshape(1, -1)
    table = {"b_ada": cols(a["b_ada"]), "norm1": cols(a["norm1_g"]), "norm2": cols(a["norm2_g"]),
             "final": cols(a["final_g"]), "gn_lru": cols(a["gnorm_lru_g"]), "gn_pool": cols(a["gnorm_pool_g"]),
             "conv_w": cols(a["conv_w"][0]), "conv_b": cols(a["conv_b"]), "ba": cols(a["lru_ba"].reshape(1, -1)),
             "bx": cols(a["lru_bx"].reshape(1, -1)), "lam": cols(a["lru_lambda"]), "pool_b": cols(a["pool_b"].reshape(1, -1)),
             "pool_s": cols(a["pool_scale"]), "cinv": np.repeat(cinv, P, axis=0), "h0": h0}
    vecs_d = np.concatenate([table[n] for n, _ in VCOLS], axis=1)
    lruw_d = np.stack([a["lru_wa"][0], a["lru_wx"][0]]).transpose(2, 0, 1, 3)
    poolw_d = a["pool_w"][0].reshape(4, 2, P, 2 * P).transpose(2, 0, 1, 3)
    keys_d = a["peer_keys"][0].reshape(DC, P, P).transpose(2, 0, 1)

    nc = _bacc.Bacc("TRN2", target_bir_lowering=False, num_devices=1)
    arrays, args = {}, []
    for name, v_ in (("w_stream", w_stream), ("vecs", vecs_d), ("c", c_d), ("hist", hist_d), ("x", x_d),
                     ("lruw", lruw_d), ("poolw", poolw_d), ("keys", keys_d)):
        v_ = np.ascontiguousarray(v_)
        arrays[f"in_{name}_dram"] = v_
        args.append(nc.dram_tensor(f"in_{name}_dram", v_.shape, mybir.dt.from_np(v_.dtype), kind="ExternalInput").ap())
    for i, shape in enumerate([(P, DC, T), (P, LC, NC, CW - 1), (P, LC, NC), (P, LC, PL)]):
        args.append(nc.dram_tensor(f"out_{i}_dram", shape, F, kind="ExternalOutput").ap())
    hybrid_step(nc, *args)
    r = _run(nc, [arrays], core_ids=[0]).results[0]
    y, cv, hl, pc = (r[f"out_{i}_dram"] for i in range(4))
    y = y.transpose(2, 1, 0).reshape(T, D)
    cv = cv.transpose(2, 3, 1, 0).reshape(1, NC, CW - 1, LC * P)
    hl = hl.transpose(2, 1, 0).reshape(1, NC, LC * P)
    pc = pc.transpose(2, 1, 0).reshape(PL, LC * P)
    pool_s = np.stack([pc[PAT + PS * b + NS:PAT + PS * (b + 1)] for b in range(NB)])[None]
    return (y[:SEQ][None], y[SEQ:].reshape(NB, NS, D), cv[:, :1], hl[:, :1], pc[SEQ:PAT][None, None],
            cv[:, 1:], hl[:, 1:], pool_s)
```
